# Optimizing a Trainium2 kernel written in Bass

```python
import jax, jax.numpy as jnp
from jax import lax
import numpy as np

D_MODEL = 1024
BATCH = 1
SEQ = 512
DEPTH = 1

N_META = 16
ATT_HEADS = 8
ATT_HEAD_DIM = D_MODEL // 16
ATT_WIDTH = ATT_HEADS * ATT_HEAD_DIM
KV_LATENT = D_MODEL // 8
IDX_HEADS = 4
IDX_DIM = D_MODEL // 16
TOPK_MAX = 256
Q_BLOCK = 128
ML_HEADS = 4
ML_V_DIM = D_MODEL // 8
ML_QK_DIM = ML_V_DIM // 2
ML_WIDTH = ML_HEADS * ML_V_DIM
ML_CHUNK = 64
CONV_WIDTH = 4
GATE_SOFTCAP = 15.0
M_INIT = -1e30
D_FF = ((8 * D_MODEL // 3 + 255) // 256) * 256
LN_EPS = 1e-5
IN_SIZES = (ATT_WIDTH, KV_LATENT, IDX_HEADS * IDX_DIM, IDX_DIM, IDX_HEADS,
            2 * ML_HEADS * ML_QK_DIM, ML_WIDTH, ML_WIDTH, ML_HEADS, ML_HEADS)
D_IN = sum(IN_SIZES)

kernel_name = "hymba_dsa_mlstm_macaron_deepnorm"

def layer_norm(x, g, b):
    x32 = x.astype(jnp.float32)
    mu = jnp.mean(x32, axis=-1, keepdims=True)
    var = jnp.mean(jnp.square(x32 - mu), axis=-1, keepdims=True)
    return ((x32 - mu) * lax.rsqrt(var + LN_EPS) * g + b).astype(x.dtype)

def rms_norm(x, g):
    x32 = x.astype(jnp.float32)
    return (x32 * lax.rsqrt(jnp.mean(jnp.square(x32), axis=-1, keepdims=True) + LN_EPS) * g).astype(x.dtype)

def swiglu(x, w_gate, w_up, w_down):
    return (jax.nn.silu(x @ w_gate) * (x @ w_up)) @ w_down

def softcap(x):
    return GATE_SOFTCAP * jnp.tanh(x / GATE_SOFTCAP)

def causal_dwconv(x, w):
    t_len = x.shape[1]
    xp = jnp.pad(x, ((0, 0), (CONV_WIDTH - 1, 0), (0, 0)))
    return sum(xp[:, j:j + t_len] * w[j] for j in range(CONV_WIDTH))

def dsa_block(qpos, q_lat, q_idx, w_idx, c_kv, k_idx, topk):
    t_len = c_kv.shape[1]
    logits = jnp.einsum('bqhd,bsd->bqhs', q_idx, k_idx).astype(jnp.float32)
    score = jnp.einsum('bqhs,bqh->bqs', jax.nn.relu(logits), w_idx.astype(jnp.float32))
    causal = jnp.arange(t_len)[None, :] <= qpos[:, None]
    score = jnp.where(causal[None], score, -jnp.inf)
    _, sel = lax.top_k(score, topk)
    kv_sel = jax.vmap(lambda c, i: c[i])(c_kv, sel)
    s = jnp.einsum('bqhc,bqkc->bqhk', q_lat, kv_sel).astype(jnp.float32) * (ATT_HEAD_DIM ** -0.5)
    valid = sel <= qpos[None, :, None]
    s = jnp.where(valid[:, :, None, :], s, -jnp.inf)
    p = jax.nn.softmax(s, axis=-1).astype(c_kv.dtype)
    return jnp.einsum('bqhk,bqkc->bqhc', p, kv_sel)

def dsa_attention(q_lat, q_idx, w_idx, c_kv, k_idx):
    bsz, t_len = c_kv.shape[:2]
    s_len = t_len - N_META
    topk = min(TOPK_MAX, s_len // 4)
    out_meta = dsa_block(jnp.arange(N_META), q_lat[:, :N_META], q_idx[:, :N_META],
                         w_idx[:, :N_META], c_kv, k_idx, topk)
    nb = s_len // Q_BLOCK

    def blocks(a):
        a = a[:, N_META:]
        return jnp.moveaxis(a.reshape(bsz, nb, Q_BLOCK, *a.shape[2:]), 1, 0)

    pos = (N_META + jnp.arange(s_len)).reshape(nb, Q_BLOCK)
    out = lax.map(lambda xs: dsa_block(xs[0], xs[1], xs[2], xs[3], c_kv, k_idx, topk),
                  (pos, blocks(q_lat), blocks(q_idx), blocks(w_idx)))
    out = jnp.moveaxis(out, 0, 1).reshape(bsz, s_len, *q_lat.shape[2:])
    return jnp.concatenate([out_meta, out], axis=1)

def mlstm_chunk(state, inp):
    c_st, n_st, m_st = state
    q, k, v, ig, lf = inp
    chunk = q.shape[2]
    b = jnp.cumsum(lf, axis=-1)
    causal = jnp.tril(jnp.ones((chunk, chunk), dtype=bool))
    d = jnp.where(causal, b[..., :, None] - b[..., None, :] + ig[..., None, :], -jnp.inf)
    inter = b + m_st[..., None]
    m_t = jnp.maximum(jnp.max(d, axis=-1), inter)
    w_inter = jnp.exp(inter - m_t)
    s = jnp.einsum('bhld,bhsd->bhls', q, k) * jnp.exp(d - m_t[..., None])
    num = jnp.einsum('bhls,bhsv->bhlv', s, v) + w_inter[..., None] * jnp.einsum('bhvd,bhld->bhlv', c_st, q)
    den = jnp.sum(s, axis=-1) + w_inter * jnp.einsum('bhd,bhld->bhl', n_st, q)
    h = num / jnp.maximum(jnp.abs(den), jnp.exp(-m_t))[..., None]
    b_end = b[..., -1]
    g = b_end[..., None] - b + ig
    m_new = jnp.maximum(b_end + m_st, jnp.max(g, axis=-1))
    decay = jnp.exp(b_end + m_st - m_new)
    wg = jnp.exp(g - m_new[..., None])
    c_new = decay[..., None, None] * c_st + jnp.einsum('bhl,bhlv,bhld->bhvd', wg, v, k)
    n_new = decay[..., None] * n_st + jnp.einsum('bhl,bhld->bhd', wg, k)
    return (c_new, n_new, m_new), h

def mlstm_chunkwise(q, k, v, ig, lf):
    bsz, nh, t_len, dk = q.shape
    dv = v.shape[-1]
    s_len = t_len - N_META
    nc = s_len // ML_CHUNK
    state = (jnp.zeros((bsz, nh, dv, dk), jnp.float32), jnp.zeros((bsz, nh, dk), jnp.float32),
             jnp.full((bsz, nh), M_INIT, jnp.float32))
    state, h_meta = mlstm_chunk(state, (q[:, :, :N_META], k[:, :, :N_META], v[:, :, :N_META],
                                        ig[:, :, :N_META], lf[:, :, :N_META]))

    def chunks(a):
        a = a[:, :, N_META:]
        return jnp.moveaxis(a.reshape(bsz, nh, nc, ML_CHUNK, *a.shape[3:]), 2, 0)

    _, h_real = lax.scan(mlstm_chunk, state, (chunks(q), chunks(k), chunks(v), chunks(ig), chunks(lf)))
    h_real = jnp.moveaxis(h_real, 0, 2).reshape(bsz, nh, s_len, dv)
    return jnp.concatenate([h_meta, h_real], axis=2)

def hybrid_mixer(x, w_in, w_uk, w_uv, kv_norm_g, conv_w, b_igate, b_fgate, ml_norm_g, w_out):
    bsz, t_len, _ = x.shape
    split_points = np.cumsum(IN_SIZES)[:-1].tolist()
    q_a, c_kv, q_idx, k_idx, w_idx, qk_m, v_m, o_m, i_m, f_m = jnp.split(x @ w_in, split_points, axis=-1)

    q_a = q_a.reshape(bsz, t_len, ATT_HEADS, ATT_HEAD_DIM)
    c_kv = rms_norm(c_kv, kv_norm_g)
    q_lat = jnp.einsum('bthd,hdc->bthc', q_a, w_uk)
    q_idx = q_idx.reshape(bsz, t_len, IDX_HEADS, IDX_DIM)
    w_idx = w_idx * (IDX_HEADS ** -0.5 * IDX_DIM ** -0.5)
    o_lat = dsa_attention(q_lat, q_idx, w_idx, c_kv, k_idx)
    y_att = jnp.einsum('bthc,hcd->bthd', o_lat, w_uv).reshape(bsz, t_len, ATT_WIDTH)

    qk_m = jax.nn.silu(causal_dwconv(qk_m, conv_w))
    q_m, k_m = jnp.split(qk_m, 2, axis=-1)

    def to_heads(a, dim):
        return a.reshape(bsz, t_len, ML_HEADS, dim).transpose(0, 2, 1, 3).astype(jnp.float32)

    ig = softcap(i_m + b_igate).astype(jnp.float32).transpose(0, 2, 1)
    lf = jax.nn.log_sigmoid(softcap(f_m + b_fgate).astype(jnp.float32)).transpose(0, 2, 1)
    h = mlstm_chunkwise(to_heads(q_m, ML_QK_DIM), to_heads(k_m, ML_QK_DIM) * (ML_QK_DIM ** -0.5),
                        to_heads(v_m, ML_V_DIM), ig, lf)
    mu = jnp.mean(h, axis=-1, keepdims=True)
    var = jnp.mean(jnp.square(h - mu), axis=-1, keepdims=True)
    h = (h - mu) * lax.rsqrt(var + LN_EPS) * ml_norm_g.reshape(ML_HEADS, ML_V_DIM)[:, None, :]
    h = h.transpose(0, 2, 1, 3).reshape(bsz, t_len, ML_WIDTH).astype(x.dtype)
    y_ml = jax.nn.sigmoid(o_m) * h

    return jnp.concatenate([y_att, y_ml], axis=-1) @ w_out

def setup_inputs(seed: int = 0) -> dict:
    key = jax.random.key(seed)
    ks = jax.random.split(key, 24)
    beta = (8 * DEPTH) ** -0.25
    f32 = jnp.float32

    def nrm(k, shape, scale):
        return jax.random.normal(k, shape, f32) * scale

    return {
        "x": nrm(ks[0], (BATCH, SEQ, D_MODEL), 1.0),
        "meta_tokens": nrm(ks[1], (N_META, D_MODEL), 1.0),
        "ln1_g": 1.0 + nrm(ks[2], (DEPTH, D_MODEL), 0.02),
        "ln1_b": nrm(ks[3], (DEPTH, D_MODEL), 0.02),
        "ffn1_w_gate": nrm(ks[4], (DEPTH, D_MODEL, D_FF), D_MODEL ** -0.5),
        "ffn1_w_up": nrm(ks[5], (DEPTH, D_MODEL, D_FF), D_MODEL ** -0.5),
        "ffn1_w_down": nrm(ks[6], (DEPTH, D_FF, D_MODEL), D_FF ** -0.5 * beta),
        "w_in": nrm(ks[7], (DEPTH, D_MODEL, D_IN), D_MODEL ** -0.5),
        "w_uk": nrm(ks[8], (DEPTH, ATT_HEADS, ATT_HEAD_DIM, KV_LATENT), ATT_HEAD_DIM ** -0.5),
        "w_uv": nrm(ks[9], (DEPTH, ATT_HEADS, KV_LATENT, ATT_HEAD_DIM), KV_LATENT ** -0.5),
        "kv_norm_g": 1.0 + nrm(ks[10], (DEPTH, KV_LATENT), 0.02),
        "conv_w": nrm(ks[11], (DEPTH, CONV_WIDTH, 2 * ML_HEADS * ML_QK_DIM), CONV_WIDTH ** -0.5),
        "b_igate": nrm(ks[12], (DEPTH, ML_HEADS), 0.1),
        "b_fgate": jnp.linspace(3.0, 6.0, ML_HEADS, dtype=f32)[None, :] + nrm(ks[13], (DEPTH, ML_HEADS), 0.1),
        "ml_norm_g": 1.0 + nrm(ks[14], (DEPTH, ML_WIDTH), 0.02),
        "w_out": nrm(ks[15], (DEPTH, D_MODEL, D_MODEL), D_MODEL ** -0.5 * beta),
        "ln2_g": 1.0 + nrm(ks[16], (DEPTH, D_MODEL), 0.02),
        "ln2_b": nrm(ks[17], (DEPTH, D_MODEL), 0.02),
        "ffn2_w_gate": nrm(ks[18], (DEPTH, D_MODEL, D_FF), D_MODEL ** -0.5),
        "ffn2_w_up": nrm(ks[19], (DEPTH, D_MODEL, D_FF), D_MODEL ** -0.5),
        "ffn2_w_down": nrm(ks[20], (DEPTH, D_FF, D_MODEL), D_FF ** -0.5 * beta),
        "ln3_g": 1.0 + nrm(ks[21], (DEPTH, D_MODEL), 0.02),
        "ln3_b": nrm(ks[22], (DEPTH, D_MODEL), 0.02),
    }

def reference(x, meta_tokens, ln1_g, ln1_b, ffn1_w_gate, ffn1_w_up, ffn1_w_down, w_in, w_uk, w_uv,
              kv_norm_g, conv_w, b_igate, b_fgate, ml_norm_g, w_out, ln2_g, ln2_b,
              ffn2_w_gate, ffn2_w_up, ffn2_w_down, ln3_g, ln3_b):
    alpha = (2 * DEPTH) ** 0.25
    bsz = x.shape[0]
    meta = jnp.broadcast_to(meta_tokens.astype(x.dtype)[None], (bsz, N_META, x.shape[-1]))
    h = jnp.concatenate([meta, x], axis=1)
    for l in range(DEPTH):
        h = layer_norm(alpha * h + 0.5 * swiglu(h, ffn1_w_gate[l], ffn1_w_up[l], ffn1_w_down[l]),
                       ln1_g[l], ln1_b[l])
        h = layer_norm(alpha * h + hybrid_mixer(h, w_in[l], w_uk[l], w_uv[l], kv_norm_g[l], conv_w[l],
                                                b_igate[l], b_fgate[l], ml_norm_g[l], w_out[l]),
                       ln2_g[l], ln2_b[l])
        h = layer_norm(alpha * h + 0.5 * swiglu(h, ffn2_w_gate[l], ffn2_w_up[l], ffn2_w_down[l]),
                       ln3_g[l], ln3_b[l])
    return h[:, N_META:]


_drawn_inputs = setup_inputs


def setup_inputs(seed=0):
    import zlib

    import numpy as np

    out = dict(_drawn_inputs(seed))
    spreads = {}
    factors = {'kv_norm_g': 8.0,
     'b_igate': 64.0,
     'ml_norm_g': 44.838,
     'ln2_g': 2.832,
     'ln2_b': 2.835,
     'ln3_g': 7.568,
     'ln3_b': 7.78}
    for name, (base, spread) in spreads.items():
        noise = np.random.default_rng([zlib.crc32(name.encode()), seed]).standard_normal(out[name].shape)
        drawn = base * np.exp(spread * noise) if base else spread * noise
        out[name] = __import__('jax').numpy.asarray(drawn.astype(out[name].dtype))
    for name, factor in factors.items():
        out[name] = (out[name] * factor).astype(out[name].dtype)
    return out
```

```python
from contextlib import ExitStack

import numpy as np

import concourse.bass as bass
from concourse import mybir

F32 = mybir.dt.float32
F32R = mybir.dt.float32r
ALU = mybir.AluOpType
ACT = mybir.ActivationFunctionType
AX = mybir.AxisListType

P = 128
D = 1024
KT = D // P
N_META = 16
SEQ = 512
T = N_META + SEQ
HT = T // 2
D_FF = 2816
FT = D_FF // P
ATT_H, ATT_D, LAT = 8, 64, 128
IDX_H = 4
TOPK = min(256, SEQ // 4)
ML_H, ML_DV = 4, 128
CONV = 4
SOFTCAP = 15.0
EPS = 1e-5
ALPHA = 2.0 ** 0.25
IDX_SCALE = IDX_H ** -0.5 * 64 ** -0.5
ATT_SCALE = ATT_D ** -0.5
K_SCALE = 64 ** -0.5

START = [0] + [N_META + P * j for j in range(4)]
ROWS = [N_META] + [P] * 4
NT = len(START)
END = [s + r for s, r in zip(START, ROWS)]

C_QA, C_CKV, C_QI, C_KI, C_WI = 0, 512, 640, 896, 960
C_QK, C_V, C_O, C_IF = 964, 1476, 1988, 2500

UW = 2048
HALF_FT = FT // 2
DOWN_W = HALF_FT * P
FFN_UNITS = FT + 2 * KT
MIX_UNITS = 14
UNIT0 = {0: 0, 2: FFN_UNITS + MIX_UNITS}
MIX0 = FFN_UNITS
N_PROJ = 10
LATE_UNITS = {0: 12, 2: 13, 4: 14}
N_UNITS = 2 * FFN_UNITS + MIX_UNITS

V_G = [0, 16, 32]
V_B = [8, 24, 40]
V_MLG, V_CONV = 48, 52
NV = V_CONV + CONV * 4

MASKED, TAKEN, UNPICKED = -2.0e38, -3.0e38, -1.0e30


def build(nc, a, out):
    ctx = ExitStack()
    with ctx:
        def sb(name, shape, dt=F32, scope=ctx):
            return scope.enter_context(nc.sbuf_tensor(name, shape, dt))

        def sem(name):
            return ctx.enter_context(nc.semaphore(name))

        ps = ctx.enter_context(nc.psum_tensor("ps", [P, 8, 512], F32))

        ST_BANKS = [[(0, 0, 512, 0)],
                    [(0, 512, T, 0), (3, START[3], T, T - 512), (4, START[4], T, T - 512 + T - START[3])],
                    [(1, START[1], T, 0)], [(2, START[2], T, 0)]]

        def pair(b):
            return ps[:, b:b + 2, 0:HT]

        x = sb("x", [P, KT, T])
        xh = sb("xh", [P, KT, T], F32R)
        xl = sb("xl", [P, KT, T], F32R)
        wraw = sb("wraw", [P, 2, UW])
        whi = sb("whi", [P, 2, UW], F32R)
        wlo = sb("wlo", [P, 2, UW], F32R)
        sil = sb("sil", [P, 2, T])
        ht = sb("ht", [P, 2, T])
        ident = sb("ident", [P, P])
        mean_w = sb("mean_w", [P, P])
        vec = sb("vec", [P, NV])
        zsum, ssum = ht[:, 0, :], ht[:, 1, :]

        def halves(v):
            return v.rearrange("p (b n) -> p b n", b=2)

        with ExitStack() as s:
            xin = sb("xin", [P, NT, D], F32, s)
            vrows = sb("vrows", [NV, P], F32, s)
        with ExitStack() as s:
            hh = sb("hh", [P, FT, T], F32R, s)
            hl = sb("hl", [P, FT, T], F32R, s)
        with ExitStack() as s:
            qi = sb("qi", [P, 4, T], F32, s)
            qa = sb("qa", [P, 4, T], F32, s)
            ql = sb("ql", [P, ATT_H, T], F32, s)
            ct = sb("ct", [P, T], F32, s)
            cs = sb("cs", [P, NT * LAT + NT * 12], F32, s)
            wuk = sb("wuk", [P, 4, LAT], F32, s)
            wuv = sb("wuv", [P, ATT_H, ATT_D], F32, s)
            qk = sb("qk", [P, 4, T], F32, s)
            upad = sb("upad", [P, 4 * NT * (ML_DV + 1)], F32, s)
            v1 = sb("v1", [P, NT, ML_H, ML_DV + 1], F32, s)
            sg = sb("sg", [P, 4, T], F32, s)
            sc = sb("sc", [P, sum(END)], F32, s)
            rows = sb("rows", [P, 2, T], F32, s)
            kvg = sb("kvg", [P, LAT], F32, s)
            bg = sb("bg", [P, 8], F32, s)
            sraw = sb("sraw", [P, KT, 12], F32, s)
            shi = sb("shi", [P, KT, 12], F32R, s)
            slo = sb("slo", [P, KT, 12], F32R, s)
            wi = sb("wi", [P, NT, IDX_H], F32, s)
            gate = sb("gate", [P, NT, 8], F32, s)
            gate2 = sb("gate2", [P, NT, 4], F32, s)
            tok = sb("tok", [P, NT, 8], F32, s)
            top8 = sb("top8", [P, 2, 8], F32, s)
            crms = sb("crms", [P, 2, NT], F32, s)
            smax = sb("smax", [P, NT, ATT_H], F32, s)
            nmax = sb("nmax", [P, NT, ATT_H], F32, s)
            rsum = sb("rsum", [P, NT, ATT_H], F32, s)
            rinv = sb("rinv", [P, NT, ATT_H], F32, s)
            bst = sb("bst", [P, ML_H * NT, 6], F32, s)
            mv = sb("mv", [P, ML_H * NT, 2], F32, s)
            mls = sb("mls", [P, 3, ML_H * NT], F32, s)
        with ExitStack() as s:
            yout = sb("yout", [P, 4, D], F32, s)

        SC_OFF = [sum(END[:j]) for j in range(NT)]
        kit = qi[:, 2, :]
        wt_flat = ql[:, :, :].rearrange("p h t -> p (h t)")
        TP0 = [0]
        for G in range(2 * NT):
            TP0.append(TP0[-1] + G // 2 + 1)
        WT_OFF = [sum(T - START[k] for k in range(i)) for i in range(NT)]
        WT_W = sum(T - s_ for s_ in START)

        def wt(h, i, c0, c1):
            o = (h % 2) * WT_W + WT_OFF[i] - START[i]
            return wt_flat[0:ROWS[i], o + c0:o + c1]

        sel = wt_flat[:, 2 * WT_W:2 * WT_W + 4 * P]
        up = upad[:, 0:4 * (T + CONV - 1)].rearrange("p (c t) -> p c t", c=4)
        nums = upad[:, :].rearrange("p (h j v) -> p h j v", h=ML_H, j=NT)
        pbuf = [upad[:, 0:4 * T].rearrange("p (h t) -> p h t", h=4), qi[:, :, :]]
        pt_flat = v1[:, :, :, :].rearrange("p j h v -> p (j h v)")
        qk_flat = qk[:, :, :].rearrange("p c t -> p (c t)")
        olt = [qk_flat[:, g * 512:(g + 1) * 512] for g in range(2)]
        yatt = qk_flat[:, 1024:1536]
        ig_row, lf_row = ht[0:4, 0, :], ht[0:4, 1, :]
        b_row, m_row = rows[0:4, 0, :], rows[0:4, 1, :]
        cmat = cs[:, 0:NT * LAT].rearrange("p (j c) -> p j c", j=NT)
        small = cs[:, NT * LAT:].rearrange("p (j c) -> p j c", j=NT)

        x_split = sem("x_split")
        const_ready = sem("const_ready")
        rows_in = [sem(f"rows_in{j}") for j in range(NT)]
        vrows_in = sem("vrows_in")
        x_turned = sem("x_turned")
        vec_turned = sem("vec_turned")
        vec_ready = sem("vec_ready")
        x_copied = sem("x_copied")
        xin_hi = sem("xin_hi")
        raw_in = [sem("raw_in0"), sem("raw_in1")]
        w_hi = sem("w_hi")
        w_lo = sem("w_lo")
        w_used = sem("w_used")
        F = []
        for p in range(3):
            names = ["gate_done", "silu_done", "mul_done", "hh_done", "hl_done"] if p != 1 else []
            names += ["z_done", "sq_done", "sums_done", "zsum_done", "stats_done", "mu2_done",
                      "var_done", "varc_done", "sd_done", "rstd_done", "sub_done", "norm_done", "aff_done", "split_done"]
            F.append({n: sem(f"{n}{p}") for n in names})
        half_done = sem("half_done")
        proj_evac = sem("proj_evac")
        par_in = sem("par_in")
        small_in = sem("small_in")
        small_hi = sem("small_hi")
        small_lo = sem("small_lo")
        pad_ready = sem("pad_ready")
        idx_done = sem("idx_done")
        relu_done = sem("relu_done")
        acc_done = sem("acc_done")
        idx_masked = sem("idx_masked")
        bias_ready = sem("bias_ready")
        mask_ready = sem("mask_ready")
        dv = sem("dv")
        ac = sem("ac")
        pl = sem("pl")
        c_ms = sem("c_ms")
        c_sd = sem("c_sd")
        c_ready = sem("c_ready")
        ct_turned = sem("ct_turned")
        ct_ready = sem("ct_ready")
        gate_in = sem("gate_in")
        gate_act = sem("gate_act")
        row_turned = sem("row_turned")
        row_copied = sem("row_copied")
        row_ready = sem("row_ready")
        tok_turned = sem("tok_turned")
        tok_ready = sem("tok_ready")
        conv_done = sem("conv_done")
        qk_ready = sem("qk_ready")
        nm_spread = sem("nm_spread")
        nm_copied = sem("nm_copied")
        arg_done = sem("arg_done")
        exp_done = sem("exp_done")
        st_done = sem("st_done")
        st_used = sem("st_used")
        wt_masked = sem("wt_masked")
        num_done = sem("num_done")
        num_copied = sem("num_copied")
        ml_var = sem("ml_var")
        ml_sd = sem("ml_sd")
        hn_ready = sem("hn_ready")
        hn_turned = sem("hn_turned")
        yml_ready = sem("yml_ready")
        yml_hi = sem("yml_hi")
        yml_lo = sem("yml_lo")
        ql_done = sem("ql_done")
        ql_ready = sem("ql_ready")
        s_done = sem("s_done")
        s_masked = sem("s_masked")
        nmax_ready = sem("nmax_ready")
        p_ready = sem("p_ready")
        pt_turned = sem("pt_turned")
        pt_even = sem("pt_even")
        pt_odd = sem("pt_odd")
        pv_step = sem("pv_step")
        pv_done = sem("pv_done")
        ol_ready = sem("ol_ready")
        y_done = sem("y_done")
        y_ready = sem("y_ready")
        yt_turned = sem("yt_turned")
        ya_hi = sem("ya_hi")
        ya_lo = sem("ya_lo")
        o_turned = sem("o_turned")
        o_even = sem("o_even")
        o_odd = sem("o_odd")
        stored = sem("stored")

        block = ctx.enter_context(nc.Block())

        def landed(u, s, late):
            return 16 * u + (32 - 16 * s + (16 if late and s else 0))

        def filled(eng, use):
            if use % 2 == 0:
                eng.wait_ge(half_done, use // 2 + 1)
            else:
                eng.wait_ge(w_used, MIX0 + use // 2 + 1)

        def keys(r, n, b):
            return ps[0:r, b, 0:n] if n <= 512 else ps[0:r, b:b + 2, 0:n // 2]

        def like_keys(v, n):
            return v if n <= 512 else halves(v)

        def kview(w):
            return w[0].rearrange("(k p) n -> p k n", p=P)

        def slot3(t, s, n):
            return t[:, s, 0:(UW // n if n != P else UW // P) * n].rearrange("p (k n) -> p k n", n=n)

        @block.sync
        def _(sp):
            w_in = kview(a["w_in"])
            w_out = kview(a["w_out"])

            def load_inputs():
                meta = a["meta_tokens"]
                sp.dma_start(xin[0:N_META, 0, :], meta).then_inc(rows_in[0], 16)
                for j in range(1, NT):
                    sp.dma_start(xin[:, j, :], a["x"][0, (j - 1) * P:j * P, :]).then_inc(rows_in[j], 16)

            def slot_free(u, first):
                if not first:
                    sp.wait_ge(w_lo, u - 1)

            def load_gate_up(p, s, f, u, first=False):
                slot_free(u, first)
                g, v = kview(a[f"ffn{p // 2 + 1}_w_gate"]), kview(a[f"ffn{p // 2 + 1}_w_up"])
                dst = wraw[:, s, :].rearrange("p (m k n) -> p m k n", m=2, n=P)
                sp.dma_start(dst[:, 0], g[:, :, bass.ts(f, P)]).then_inc(raw_in[s], 16)
                sp.dma_start(dst[:, 1], v[:, :, bass.ts(f, P)]).then_inc(raw_in[s], 16)

            def load_down(p, half, m, u):
                slot_free(u, False)
                w = kview(a[f"ffn{p // 2 + 1}_w_down"])
                dst = wraw[:, half, 0:DOWN_W].rearrange("p (k n) -> p k n", n=P)
                for k0, k1 in ((0, 6), (6, HALF_FT)):
                    sp.dma_start(dst[:, k0:k1, :],
                                 w[:, half * HALF_FT + k0:half * HALF_FT + k1, bass.ts(m, P)]).then_inc(raw_in[half], 16)

            def ffn(p):
                u0 = UNIT0[p]
                for s in range(2):
                    load_gate_up(p, s, s, u0 + s, first=(p == 0))
                with sp.Fori(1, FT // 2) as i:
                    for s in range(2):
                        load_gate_up(p, s, 2 * i + s, 2 * i + (u0 + s))
                with sp.Fori(0, KT) as m:
                    for half in range(2):
                        load_down(p, half, m, 2 * m + (u0 + FT + half))

            def mixer():
                for n in range(MIX_UNITS):
                    u = MIX0 + n
                    s = u % 2
                    slot_free(u, False)
                    dst = slot3(wraw, s, 256)
                    if n == 1:
                        for c in range(2):
                            sp.dma_start(dst[:, :, 64 * c:64 * c + 64], w_in[:, :, C_KI:C_KI + 64]).then_inc(raw_in[s], 16)
                        sp.dma_start(dst[:, :, P:2 * P], w_in[:, :, C_CKV:C_CKV + LAT]).then_inc(raw_in[s], 16)
                        continue
                    if n < N_PROJ:
                        c0 = {0: C_QI, 2: C_QA, 3: C_QA + 256, 4: C_QK, 5: C_QK + 256, 6: C_V, 7: C_V + 256,
                              8: C_O, 9: C_O + 256}[n]
                        src = w_in[:, :, c0:c0 + 256]
                    else:
                        src = w_out[:, :, (n - N_PROJ) * 256:(n - N_PROJ + 1) * 256]
                    for k0 in (0, 4):
                        sp.dma_start(dst[:, k0:k0 + 4, :], src[:, k0:k0 + 4, :]).then_inc(raw_in[s], 16)

            def load_mixer_params():
                sp.wait_ge(w_used, FFN_UNITS)
                sp.dma_start(sraw[:, :, 0:4], w_in[:, :, C_WI:C_WI + 4]).then_inc(small_in, 16)
                sp.dma_start(sraw[:, :, 4:12], w_in[:, :, C_IF:C_IF + 8]).then_inc(small_in, 16)
                sp.dma_start(wuk[:, :, :], a["w_uk"][0].rearrange("(q two) d c -> (two d) q c", two=2)).then_inc(par_in, 16)
                sp.dma_start(wuv[:, :, :], a["w_uv"][0].rearrange("h c d -> c h d")).then_inc(par_in, 16)
                sp.dma_start(kvg[:, :], a["kv_norm_g"].broadcast_to([P, LAT])).then_inc(par_in, 16)
                sp.dma_start(bg[:, 0:4], a["b_igate"].broadcast_to([P, 4])).then_inc(par_in, 16)
                sp.dma_start(bg[:, 4:8], a["b_fgate"].broadcast_to([P, 4])).then_inc(par_in, 16)

            load_inputs()
            r = 0
            for name in ("ln1_g", "ln1_b", "ln2_g", "ln2_b", "ln3_g", "ln3_b"):
                sp.dma_start(vrows[r:r + KT, :], a[name].rearrange("o (k p) -> (o k) p", p=P)).then_inc(vrows_in, 16)
                r += KT
            sp.dma_start(vrows[V_MLG:V_CONV, :], a["ml_norm_g"].rearrange("o (k p) -> (o k) p", p=P)).then_inc(vrows_in, 16)
            sp.dma_start(vrows[V_CONV:NV, :], a["conv_w"].rearrange("o j (c p) -> (o j c) p", p=P)).then_inc(vrows_in, 16)
            ffn(0)
            load_mixer_params()
            mixer()
            ffn(2)
            for q in range(8):
                half, j = divmod(q, 4)
                sp.wait_ge(o_even if q % 2 == 0 else o_odd, q // 2 + 1)
                sp.dma_start(out[0, j * P:(j + 1) * P, half * 512:(half + 1) * 512],
                             yout[:, j, half * 512:(half + 1) * 512]).then_inc(stored, 16)
            sp.wait_ge(stored, 8 * 16)

        @block.gpsimd
        def _(pool):
            n_pl = [0]

            def link(ins):
                n_pl[0] += 1
                ins.then_inc(pl, 1)
                pool.wait_ge(pl, n_pl[0])

            def constants():
                link(pool.memset(ident[:, :], 0.0))
                pool.affine_select(out=ident[:, :], in_=ident[:, :], compare_op=ALU.not_equal, fill=1.0,
                                   base=0, pattern=[[-1, P]], channel_multiplier=1).then_inc(const_ready, 1)
                pool.memset(mean_w[:, :], 1.0 / D).then_inc(const_ready, 1)

            def x_lo(k, hi_sem, n, done):
                pool.wait_ge(hi_sem, n)
                pool.tensor_tensor(xl[:, k, :], x[:, k, :], xh[:, k, :].bitcast(F32), ALU.subtract)\
                    .then_inc(done, 1)

            def sums(p):
                s = F[p]
                if p != 1:
                    pool.wait_ge(s["hl_done"], FT)
                else:
                    pool.wait_ge(tok_turned, 1)
                    pool.wait_ge(nm_spread, ML_H)
                pool.memset(zsum, 0.0).then_inc(s["sums_done"], 1)
                pool.memset(ssum, 0.0).then_inc(s["sums_done"], 1)
                pool.wait_ge(s["sums_done"], 2)

                def add(m, sq_slot, n):
                    pool.wait_ge(s["z_done"], n)
                    pool.tensor_tensor(zsum, zsum, x[:, m, :], ALU.add).then_inc(s["zsum_done"], 1)
                    pool.wait_ge(s["sq_done"], n)
                    pool.tensor_tensor(ssum, ssum, sil[:, sq_slot, :], ALU.add).then_inc(s["sums_done"], 1)
                    pool.wait_ge(s["zsum_done"], n)
                    pool.wait_ge(s["sums_done"], n + 2)

                if p != 1:
                    with pool.Fori(0, KT // 2) as i:
                        for e in range(2):
                            add(2 * i + e, e, 2 * i + (e + 1))
                    return
                for m in range(KT):
                    add(m, m % 2, m + 1)
                    if m in LATE_UNITS:
                        mix_lo(LATE_UNITS[m])

            def norm_lo(p):
                for k in range(KT):
                    x_lo(k, F[p]["aff_done"], k + 1, F[p]["split_done"])

            def mix_lo(n):
                u = MIX0 + n
                pool.wait_ge(w_hi, u + 1)
                pool.tensor_tensor(wlo[:, u % 2, :], wraw[:, u % 2, :], whi[:, u % 2, :].bitcast(F32), ALU.subtract)\
                    .then_inc(w_lo, 1)

            def mixer():
                pool.wait_ge(w_used, FFN_UNITS)
                pool.memset(up[:, :, 0:CONV - 1], 0.0).then_inc(pad_ready, 1)
                link(pool.memset(sel, 0.0))
                pool.affine_select(out=sel.rearrange("p (h n) -> p h n", h=4), in_=sel.rearrange("p (h n) -> p h n", h=4),
                                   compare_op=ALU.not_equal, fill=1.0, base=0, pattern=[[-1, 4], [0, P]],
                                   channel_multiplier=1).then_inc(pad_ready, 1)
                pool.memset(v1[:, :, :, ML_DV:ML_DV + 1], 1.0).then_inc(pad_ready, 1)
                pool.wait_ge(small_hi, 1)
                pool.tensor_tensor(slo[:, :, :], sraw[:, :, :], shi[:, :, :].bitcast(F32), ALU.subtract)\
                    .then_inc(small_lo, 1)
                norm_lo(0)
                mix_lo(1)
                mix_lo(2)
                for j in range(1, NT):
                    pool.wait_ge(acc_done, 4 * j)
                    d = sc[:, SC_OFF[j] + START[j]:SC_OFF[j] + END[j]]
                    pool.affine_select(out=d, in_=d, compare_op=ALU.is_ge, fill=MASKED, base=0,
                                       pattern=[[-1, P]], channel_multiplier=1).then_inc(idx_masked, 1)
                m0 = sc[0:N_META, 0:N_META]
                link(pool.memset(m0, 0.0))
                pool.affine_select(out=m0, in_=m0, compare_op=ALU.is_ge, fill=UNPICKED, base=0,
                                   pattern=[[-1, N_META]], channel_multiplier=1).then_inc(mask_ready, 1)
                for n in range(3, N_PROJ + 1):
                    mix_lo(n)
                for j in range(1, NT):
                    pool.wait_ge(bias_ready, j)
                    d = sc[:, SC_OFF[j] + START[j]:SC_OFF[j] + END[j]]
                    pool.affine_select(out=d, in_=d, compare_op=ALU.is_ge, fill=UNPICKED, base=0,
                                       pattern=[[-1, P]], channel_multiplier=1).then_inc(mask_ready, 1)
                mix_lo(N_PROJ + 1)
                for h in range(ML_H):
                    for i in (0, 3, 4, 1, 2):
                        pool.wait_ge(st_used, 4 * h + {0: 1, 3: 2, 4: 2, 1: 3, 2: 4}[i])
                        d = wt(h, i, START[i], END[i])
                        pool.affine_select(out=d, in_=d, compare_op=ALU.is_ge, fill=0.0, base=0,
                                           pattern=[[1, ROWS[i]]], channel_multiplier=-1).then_inc(wt_masked, 1)
                for h in range(ML_H):
                    pool.wait_ge(yml_hi, h + 1)
                    pool.tensor_tensor(xl[:, 4 + h, :], sil[:, h % 2, :], xh[:, 4 + h, :].bitcast(F32), ALU.subtract)\
                        .then_inc(yml_lo, 1)

            constants()
            for k in range(KT):
                x_lo(k, xin_hi, k + 1, x_split)
            sums(0)
            mixer()
            sums(1)
            norm_lo(1)
            sums(2)

        @block.scalar
        def _(act):
            n_ac = [0]

            def link(ins):
                n_ac[0] += 1
                ins.then_inc(ac, 1)
                act.wait_ge(ac, n_ac[0])

            def hi(u, s, width, late, first=False):
                act.wait_ge(raw_in[s], landed(u, s, late))
                if not first:
                    act.wait_ge(w_used, u - 1)
                act.activation(whi[:, s, 0:width], wraw[:, s, 0:width], ACT.Copy).then_inc(w_hi, 1)

            def input_hi():
                for k in range(KT):
                    act.wait_ge(x_copied, k + 1)
                    act.activation(xh[:, k, :], x[:, k, :], ACT.Copy).then_inc(xin_hi, 1)

            def ffn(p):
                s, u0, late = F[p], UNIT0[p], p > 0

                def hidden(f, e, first):
                    act.wait_ge(s["gate_done"], f + 1)
                    if not first:
                        act.wait_ge(s["mul_done"], f - 1)
                    act.activation(halves(sil[:, e, :]), pair(4 * e), ACT.Silu).then_inc(s["silu_done"], 1)
                    act.wait_ge(s["mul_done"], f + 1)
                    act.activation(hh[:, f, :], ht[:, e, :], ACT.Copy).then_inc(s["hh_done"], 1)

                hi(u0 + 1, 1, UW, late, first=(p == 0))
                hidden(0, 0, True)
                hi(u0 + 2, 0, UW, late)
                hidden(1, 1, True)
                with act.Fori(1, FT // 2 - 1) as i:
                    for e in range(2):
                        hi(2 * i + (u0 + 1 + e), 1 - e, UW, late)
                        hidden(2 * i + e, e, False)
                hi(u0 + FT - 1, 1, UW, late)
                hidden(FT - 2, 0, False)
                hi(u0 + FT, 0, DOWN_W, late)
                hidden(FT - 1, 1, False)
                hi(u0 + FT + 1, 1, DOWN_W, late)
                hi(u0 + FT + 2, 0, DOWN_W, late)
                with act.Fori(0, KT // 2 - 1) as i:
                    for e in range(2):
                        m = 2 * i + e
                        square(p, m, e)
                        hi(2 * m + (u0 + FT + 3), 1, DOWN_W, late)
                        hi(2 * m + (u0 + FT + 4), 0, DOWN_W, late)
                square(p, KT - 2, 0)
                hi(u0 + FT + 15, 1, DOWN_W, late)
                if p == 0:
                    hi(MIX0, 0, UW, late)
                square(p, KT - 1, 1)

            def square(p, m, e):
                s = F[p]
                act.wait_ge(s["z_done"], m + 1)
                act.wait_ge(s["sums_done"], m + 1)
                act.activation(sil[:, e, :], x[:, m, :], ACT.Square).then_inc(s["sq_done"], 1)

            def norm(p):
                s = F[p]
                act.wait_ge(s["stats_done"], 1)
                act.activation(halves(sil[:, 0, :]), pair(4), ACT.Square).then_inc(s["mu2_done"], 1)
                act.wait_ge(s["varc_done"], 1)
                act.activation(sil[:, 1, :], sil[:, 0, :], ACT.Sqrt).then_inc(s["sd_done"], 1)
                for k in range(KT):
                    act.wait_ge(s["norm_done"], k + 1)
                    if k == 0:
                        act.wait_ge(vec_ready, 1)
                    g, b = vec[:, V_G[p] + k:V_G[p] + k + 1], vec[:, V_B[p] + k:V_B[p] + k + 1]
                    if p != 2:
                        act.activation(xh[:, k, :], ht[:, k % 2, :], ACT.Identity, bias=b, scale=g)
                    act.activation(x[:, k, :], ht[:, k % 2, :], ACT.Identity, bias=b, scale=g)\
                        .then_inc(s["aff_done"], 1)

            def proj_out(n, src, dst, func=ACT.Copy):
                filled(act, n)
                act.activation(dst, src, func).then_inc(proj_evac, 1)

            def mixer():
                act.wait_ge(small_in, 32)
                act.activation(shi[:, :, :], sraw[:, :, :], ACT.Copy).then_inc(small_hi, 1)
                hi(MIX0 + 1, 1, UW, True)
                for c in range(2):
                    proj_out(c, pair(2 * c), halves(qi[:, c, :]))
                hi(MIX0 + 2, 0, UW, False)
                proj_out(2, pair(0), halves(kit))
                proj_out(3, ps[:, 2:4, :].rearrange("p b n -> p (b n)")[:, 0:NT * (LAT + 12)], cs[:, :])
                for k in range(4 * (NT - 1)):
                    j = 1 + k // 4
                    act.wait_ge(idx_done, k + 1)
                    if k >= 2:
                        act.wait_ge(acc_done, k - 1)
                    src = keys(ROWS[j], END[j], 4 + 2 * (k % 2))
                    dst = like_keys(sil[0:ROWS[j], k % 2, 0:END[j]], END[j])
                    act.activation(dst, src, ACT.Relu).then_inc(relu_done, 1)
                act.wait_ge(c_ms, 1)
                act.activation(crms[:, 1, :], crms[:, 0, :], ACT.Sqrt).then_inc(c_sd, 1)
                hi(MIX0 + 3, 1, UW, True)
                act.wait_ge(gate_in, 1)
                link(act.activation(gate[:, :, :], gate[:, :, :], ACT.Tanh, scale=1.0 / SOFTCAP))
                link(act.activation(gate2[:, :, :], gate[:, :, 4:8], ACT.Exp, scale=-SOFTCAP))
                act.activation(gate2[:, :, :], gate2[:, :, :], ACT.Ln, bias=1.0).then_inc(gate_act, 1)
                for c in range(2):
                    proj_out(4 + c, pair(2 * c), halves(qa[:, c, :]))
                act.wait_ge(ct_turned, 1)
                act.activation(ct[:, 0:END[3]], ps[:, 4, 0:END[3]], ACT.Copy)
                act.activation(ct[:, END[3]:T], ps[:, 5, 0:P], ACT.Copy).then_inc(ct_ready, 1)
                hi(MIX0 + 4, 0, UW, False)
                for c in range(2):
                    proj_out(6 + c, pair(2 * c), halves(qa[:, 2 + c, :]))
                hi(MIX0 + 5, 1, UW, True)
                act.wait_ge(pad_ready, 1)
                for n in (4, 5):
                    for c in range(2):
                        proj_out(2 * n + c, pair(2 * c), halves(up[:, 2 * (n - 4) + c, CONV - 1:CONV - 1 + T]))
                    hi(MIX0 + n + 2, n % 2, UW, True)
                act.wait_ge(tok_turned, 1)
                tt = ps[:, 6, 0:NT * 8].rearrange("p (j e) -> p j e", e=8)
                act.activation(tok[:, :, 0:4], tt[:, :, 0:4], ACT.Copy)
                act.activation(tok[:, :, 4:8], tt[:, :, 4:8], ACT.Exp).then_inc(tok_ready, 1)
                for n in (6, 7):
                    h0 = 2 * (n - 6)
                    proj_out(2 * n, ps[:, 0:2, :].rearrange("p b (j h v) -> p (b j) h v", j=2, h=2),
                             v1[:, 0:4, h0:h0 + 2, 0:ML_DV])
                    proj_out(2 * n + 1, ps[:, 2, 0:256].rearrange("p (h v) -> p h v", h=2),
                             v1[:, 4, h0:h0 + 2, 0:ML_DV])
                    hi(MIX0 + n + 2, n % 2, UW, True)
                for n in (8, 9):
                    for c in range(2):
                        proj_out(2 * n + c, pair(2 * c), halves(sg[:, 2 * (n - 8) + c, :]), ACT.Sigmoid)
                    hi(MIX0 + n + 2, n % 2, UW, True)
                for c in range(4):
                    act.wait_ge(conv_done, c + 1)
                    act.activation(qk[:, c, :], qk[:, c, :], ACT.Silu).then_inc(qk_ready, 1)

                def spread_m(h):
                    act.wait_ge(nm_spread, h + 1)
                    if h >= 2:
                        act.wait_ge(arg_done, 5 * (h - 1))
                    act.activation(halves(sil[:, h % 2, :]), pair(5), ACT.Copy).then_inc(nm_copied, 1)

                def exps(h):
                    for e, i in enumerate((0, 3, 4, 1, 2)):
                        act.wait_ge(arg_done, 5 * h + e + 1)
                        w = wt(h, i, START[i], T)
                        act.activation(w, w, ACT.Exp).then_inc(exp_done, 1)

                def copy_num(h):
                    act.wait_ge(num_done, 2 * h + 1)
                    act.activation(nums[:, h, 0:3, :], ps[:, 4, 0:3 * (ML_DV + 1)].rearrange("p (j v) -> p j v", j=3),
                                   ACT.Copy).then_inc(num_copied, 1)
                    act.wait_ge(num_done, 2 * h + 2)
                    act.activation(nums[:, h, 3:5, :], ps[:, 7, 0:2 * (ML_DV + 1)].rearrange("p (j v) -> p j v", j=2),
                                   ACT.Copy).then_inc(num_copied, 1)

                for h in range(ML_H):
                    spread_m(h)
                    exps(h)
                    if h >= 1:
                        copy_num(h - 1)
                copy_num(ML_H - 1)
                for h in range(ATT_H):
                    act.wait_ge(ql_done, h + 1)
                    act.activation(halves(ql[:, h, :]), pair(4 + 2 * (h % 2)), ACT.Copy).then_inc(ql_ready, 1)
                act.wait_ge(ml_var, 1)
                act.activation(mls[:, 0, :], mls[:, 0, :], ACT.Sqrt).then_inc(ml_sd, 1)
                for h in range(ML_H):
                    act.wait_ge(yml_ready, h + 1)
                    act.activation(xh[:, 4 + h, :], sil[:, h % 2, :], ACT.Copy).then_inc(yml_hi, 1)
                attention()
                for m in range(KT):
                    square(1, m, m % 2)
                    if m in LATE_UNITS:
                        hi(MIX0 + LATE_UNITS[m], LATE_UNITS[m] % 2, UW, True)

            def attention():
                late = None
                for G in range(11):
                    if G < 10:
                        j, g = divmod(G, 2)
                        R, n = ROWS[j], END[j]
                        for q in range(4):
                            k = 4 * G + q
                            h = 4 * g + q
                            act.wait_ge(nmax_ready, k + 1)
                            if q == 0 and G >= 2:
                                act.wait_ge(pt_turned, TP0[G - 1])
                            if G == 0 and q == 0:
                                act.wait_ge(hn_turned, ML_H)
                            act.activation(pbuf[G % 2][0:R, q, 0:n], sil[0:R, k % 2, 0:n], ACT.Exp,
                                           bias=nmax[0:R, j, h:h + 1], scale=ATT_SCALE,
                                           accum_out=rsum[0:R, j, h:h + 1]).then_inc(p_ready, 1)
                    if G >= 1:
                        j, g = divmod(G - 1, 2)
                        R = ROWS[j]
                        for i in range(j + 1):
                            t = TP0[G - 1] + i
                            if t % 2 == 1:
                                act.wait_ge(pt_turned, t + 1)
                                if t >= 2:
                                    act.wait_ge(pv_step, t - 1)
                                act.activation(pt_flat[0:ROWS[i], 512:512 + 4 * R], ps[0:ROWS[i], 1, 0:4 * R],
                                               ACT.Copy).then_inc(pt_odd, 1)
                        act.wait_ge(pv_step, TP0[G])
                        if G - 1 >= 2:
                            act.wait_ge(y_done, j)
                        act.activation(olt[g][:, 0:4 * R], ps[:, 3, 0:4 * R], ACT.Copy).then_inc(ol_ready, 1)
                        if late is not None:
                            att_hi(late)
                            late = None
                        if g == 1:
                            late = j
                att_hi(NT - 1)

            def att_hi(j):
                act.wait_ge(yt_turned, j + 1)
                act.activation(xh[:, 0:4, START[j]:END[j]], ps[:, 2, 0:4 * ROWS[j]].rearrange("p (c r) -> p c r", c=4),
                               ACT.Copy).then_inc(ya_hi, 1)

            hi(0, 0, UW, False, first=True)
            input_hi()
            ffn(0)
            norm(0)
            mixer()
            norm(1)
            ffn(2)
            norm(2)
            for q in range(1, 8, 2):
                half, j = divmod(q, 4)
                act.wait_ge(o_turned, q + 1)
                act.activation(yout[:, j, half * 512:(half + 1) * 512], ps[:, j, :], ACT.Copy).then_inc(o_odd, 1)

        @block.tensor
        def _(pe):
            def split_product(s, col, k, b, first, last, kin=None):
                w_h, w_l = whi[:, s, col:col + P], wlo[:, s, col:col + P]
                a_h, a_l = kin
                for n, (w, v) in enumerate(((w_h, a_h), (w_h, a_l), (w_l, a_h))):
                    for e in range(2):
                        mm = pe.matmul(ps[:, b + e, 0:HT], w, v[:, k, e * HT:(e + 1) * HT],
                                       start=(first and n == 0), stop=(last and n == 2))
                return mm

            X = (xh, xl)

            def turn_inputs():
                pe.wait_ge(const_ready, 2)
                pe.wait_ge(vrows_in, 16 * 8)
                pe.transpose(ps[:, 7, 0:NV], vrows[:, :], ident[0:NV, 0:NV]).then_inc(vec_turned, 1)
                for k in range(KT):
                    b = 2 * (k % 3)
                    if k >= 3:
                        pe.wait_ge(x_copied, k - 2)
                    for j in range(NT):
                        if k == 0:
                            pe.wait_ge(rows_in[j], 16)
                        dst = ps[:, b, START[j]:END[j]] if j < 4 else ps[:, b + 1, 0:P]
                        tp = pe.transpose(dst, xin[0:ROWS[j], j, k * P:(k + 1) * P], ident[0:ROWS[j], 0:ROWS[j]])
                    tp.then_inc(x_turned, 1)

            def ffn(p):
                s, u0 = F[p], UNIT0[p]
                x_ready = x_split if p == 0 else F[1]["split_done"]

                def gate_up(f, u, e, start=False, early=False):
                    pe.wait_ge(w_lo, u + 1)
                    if not early:
                        pe.wait_ge(s["mul_done"], f - 1)
                    for m in range(2):
                        for k in range(KT):
                            if start and m == 0:
                                pe.wait_ge(x_ready, k + 1)
                            mm = split_product(e, m * KT * P + k * P, k, 4 * e + 2 * m, k == 0, k == KT - 1, X)
                        mm.then_inc(w_used if m else s["gate_done"], 1)

                if p == 0:
                    pe.wait_ge(x_copied, KT)
                    pe.wait_ge(vec_ready, 1)
                for e in range(2):
                    gate_up(e, u0 + e, e, start=(e == 0), early=True)
                with pe.Fori(1, FT // 2) as i:
                    for e in range(2):
                        gate_up(2 * i + e, 2 * i + (u0 + e), e)

                def down(m, b, u):
                    for half in range(2):
                        pe.wait_ge(w_lo, u + (half + 1))
                        for k in range(HALF_FT):
                            kk = half * HALF_FT + k
                            if isinstance(m, int) and m == 0 and kk == FT - 1:
                                pe.wait_ge(s["hl_done"], FT)
                            mm = split_product(half, k * P, kk, b, kk == 0, kk == FT - 1, (hh, hl))
                        mm.then_inc(w_used, 1)

                pe.wait_ge(s["mul_done"], FT - 1)
                pe.wait_ge(s["hl_done"], FT - 1)
                for m in range(2):
                    down(m, 2 * m, u0 + FT + 2 * m)
                with pe.Fori(1, KT // 2) as i:
                    for e in range(2):
                        pe.wait_ge(s["z_done"], 2 * i + (e - 1))
                        down(2 * i + e, 2 * e, 4 * i + (u0 + FT + 2 * e))

            def stats(p):
                s = F[p]
                pe.wait_ge(s["sums_done"], KT + 2)
                for b, v in ((4, zsum), (6, ssum)):
                    for e in range(2):
                        mm = pe.matmul(ps[:, b + e, 0:HT], mean_w[:, :], v[:, e * HT:(e + 1) * HT], start=True, stop=True)
                mm.then_inc(s["stats_done"], 1)

            def by_feature(n, use, mc, start=False, order=range(KT)):
                u = MIX0 + n
                for q, k in enumerate(order):
                    if start:
                        pe.wait_ge(F[0]["split_done"], k + 1)
                    mm = split_product(u % 2, k * 256 + mc * P, k, 2 * (use % 2), q == 0, q == KT - 1, X)
                mm.then_inc(w_used if use % 2 else half_done, 1)

            def by_token(dst, j, w_h, w_l):
                for k in range(KT):
                    t0 = START[j]
                    v_h, v_l = xh[:, k, t0:t0 + P], xl[:, k, t0:t0 + P]
                    for n, (v, w) in enumerate(((v_h, w_h(k)), (v_l, w_h(k)), (v_h, w_l(k)))):
                        mm = pe.matmul(dst, v, w, start=(k == 0 and n == 0), stop=(k == KT - 1 and n == 2))
                return mm

            def bank_pair_free(use):
                if use >= 2:
                    pe.wait_ge(proj_evac, use - 1)

            def unit(n):
                u = MIX0 + n
                pe.wait_ge(w_lo, u + 1)
                for c in range(2):
                    bank_pair_free(2 * n + c)
                    by_feature(n, 2 * n + c, c, start=(n == 0 and c == 0))

            def unit_v(n):
                u = MIX0 + n
                s = u % 2
                pe.wait_ge(w_lo, u + 1)
                for j in range(NT):
                    if j in (0, 4):
                        bank_pair_free(2 * n + j // 4)
                    mm = by_token(ps[:, j // 2, (j % 2) * 256:(j % 2) * 256 + 256], j,
                                  lambda k: whi[:, s, k * 256:(k + 1) * 256], lambda k: wlo[:, s, k * 256:(k + 1) * 256])
                    if j >= 3:
                        mm.then_inc(half_done if j == 3 else w_used, 1)

            def mixer():
                unit(0)
                u = MIX0 + 1
                s = u % 2
                pe.wait_ge(w_lo, u + 1)
                bank_pair_free(2)
                by_feature(1, 2, 0)
                bank_pair_free(3)
                pe.wait_ge(small_lo, 1)
                for j in range(NT):
                    by_token(ps[:, 2 + j // 4, (j % 4) * P:(j % 4 + 1) * P], j,
                             lambda k: whi[:, s, k * 256 + P:(k + 1) * 256], lambda k: wlo[:, s, k * 256 + P:(k + 1) * 256])
                for j in range(NT):
                    mm = by_token(ps[:, 3, P + 12 * j:P + 12 * (j + 1)], j, lambda k: shi[:, k, :], lambda k: slo[:, k, :])
                mm.then_inc(w_used, 1)

                pe.wait_ge(proj_evac, 3)
                for k in range(4 * (NT - 1)):
                    j, h = 1 + k // 4, k % 4
                    r0, n = 64 * (h % 2), END[j]
                    if k >= 2:
                        pe.wait_ge(relu_done, k - 1)
                    cols = 1 if n <= 512 else 2
                    for e in range(cols):
                        w = n // cols
                        mm = pe.matmul(ps[0:ROWS[j], 4 + 2 * (k % 2) + e, 0:w], qi[r0:r0 + 64, h // 2, START[j]:END[j]],
                                       qi[r0:r0 + 64, 2, e * w:(e + 1) * w], start=True, stop=True)
                    mm.then_inc(idx_done, 1)
                unit(2)
                pe.wait_ge(relu_done, 4 * (NT - 1))
                pe.wait_ge(c_ready, 1)
                for j in range(NT):
                    dst = ps[:, 4, START[j]:END[j]] if j < 4 else ps[:, 5, 0:P]
                    mm = pe.transpose(dst, cmat[0:ROWS[j], j, :], ident[0:ROWS[j], 0:ROWS[j]])
                mm.then_inc(ct_turned, 1)
                pe.wait_ge(gate_act, 1)

                def turn_rows(src, b):
                    for j in range(NT):
                        dst = ps[0:4, b, START[j]:END[j]] if j < 4 else ps[0:4, b + 1, 0:P]
                        mm = pe.transpose(dst, src[0:ROWS[j], j, 0:4], ident[0:ROWS[j], 0:ROWS[j]])
                    mm.then_inc(row_turned, 1)

                turn_rows(gate, 6)
                pe.wait_ge(ct_ready, 1)
                turn_rows(gate2, 4)
                unit(3)
                unit(4)
                unit(5)
                pe.wait_ge(row_ready, 1)
                for j in range(NT):
                    for c, src in ((0, ig_row), (4, b_row)):
                        mm = pe.transpose(ps[:, 6, 8 * j + c:8 * j + c + 4], src[:, START[j]:START[j] + P], ident[0:4, 0:4])
                mm.then_inc(tok_turned, 1)
                unit_v(6)
                unit_v(7)
                unit(8)
                unit(9)
                mlstm()
                attention()
                pe.wait_ge(ya_lo, NT)
                pe.wait_ge(yml_lo, ML_H)
                for n in range(N_PROJ, MIX_UNITS):
                    pe.wait_ge(w_lo, MIX0 + n + 1)
                    for c in range(2):
                        m = 2 * (n - N_PROJ) + c
                        if m >= 2:
                            pe.wait_ge(F[1]["z_done"], m - 1)
                        by_feature(n, m, c, order=(4, 5, 6, 7, 0, 1, 2, 3))

            def mlstm():
                def spread(h):
                    if h >= 1:
                        pe.wait_ge(nm_copied, h)
                    else:
                        pe.wait_ge(tok_ready, 1)
                    for e in range(2):
                        mm = pe.matmul(ps[:, 5 + e, 0:HT], sel[0:4, h * P:(h + 1) * P], lf_row[:, e * HT:(e + 1) * HT],
                                       start=True, stop=True)
                    mm.then_inc(nm_spread, 1)

                def scores(h):
                    r0 = 64 * (h % 2)

                    def part(i, c0, c1, b, o):
                        return pe.matmul(ps[0:ROWS[i], b, o:o + c1 - c0], qk[r0:r0 + 64, 2 + h // 2, START[i]:END[i]],
                                         qk[r0:r0 + 64, h // 2, c0:c1], start=True, stop=True)

                    for b, parts in enumerate(ST_BANKS):
                        if h >= 1:
                            pe.wait_ge(st_used, 4 * (h - 1) + b + 1)
                        for i, c0, c1, o in parts:
                            mm = part(i, c0, c1, b, o)
                        mm.then_inc(st_done, 1)

                def numerators(h):
                    pe.wait_ge(wt_masked, 5 * (h + 1))
                    for b, js in ((4, (0, 1, 2)), (7, (3, 4))):
                        if h >= 1:
                            pe.wait_ge(num_copied, 2 * h - (b == 4))
                        for q, j in enumerate(js):
                            for i in range(j + 1):
                                mm = pe.matmul(ps[:, b, q * (ML_DV + 1):(q + 1) * (ML_DV + 1)],
                                               wt(h, i, START[j], START[j] + P), v1[0:ROWS[i], i, h, :],
                                               start=(i == 0), stop=(i == j))
                        mm.then_inc(num_done, 1)

                pe.wait_ge(pad_ready, 3)
                spread(0)
                pe.wait_ge(proj_evac, 2 * N_PROJ)
                pe.wait_ge(qk_ready, 4)
                for h in range(ML_H):
                    scores(h)
                    if h + 1 < ML_H:
                        spread(h + 1)
                    if h >= 1:
                        numerators(h - 1)
                numerators(ML_H - 1)
                pe.wait_ge(num_copied, 2 * ML_H)
                pe.wait_ge(nm_copied, ML_H)
                pe.wait_ge(par_in, 16 * 5)
                for h in range(ATT_H):
                    r0 = 64 * (h % 2)
                    if h >= 2:
                        pe.wait_ge(ql_ready, h - 1)
                    for e in range(2):
                        mm = pe.matmul(ps[:, 4 + 2 * (h % 2) + e, 0:HT], wuk[r0:r0 + 64, h // 2, :],
                                       qa[r0:r0 + 64, h // 2, e * HT:(e + 1) * HT], start=True, stop=True)
                    mm.then_inc(ql_done, 1)
                pe.wait_ge(st_used, 4 * ML_H)
                for h in range(ML_H):
                    pe.wait_ge(hn_ready, NT * (h + 1))
                    if h >= 2:
                        pe.wait_ge(yml_ready, h - 1)
                    b = 2 * (h % 2)
                    for j in range(NT):
                        dst = ps[:, b, START[j]:END[j]] if j < 4 else ps[:, b + 1, 0:P]
                        mm = pe.transpose(dst, nums[0:ROWS[j], h, j, 0:ML_DV], ident[0:ROWS[j], 0:ROWS[j]])
                    mm.then_inc(hn_turned, 1)

            def attention():
                def scores(k):
                    j, h = divmod(k, ATT_H)
                    R, n = ROWS[j], END[j]
                    if k >= 2:
                        pe.wait_ge(s_masked, k - 1)
                    cols = 1 if n <= 512 else 2
                    w = n // cols
                    for e in range(cols):
                        mm = pe.matmul(ps[0:R, 4 + 2 * (k % 2) + e, 0:w], ql[:, h, START[j]:END[j]],
                                       ct[:, e * w:(e + 1) * w], start=True, stop=True)
                    mm.then_inc(s_done, 1)

                def turn(G, i):
                    j = G // 2
                    R, t = ROWS[j], TP0[G] + i
                    if i == 0:
                        pe.wait_ge(p_ready, 4 * G + 4)
                    if t >= 2:
                        pe.wait_ge(pt_even if t % 2 == 0 else pt_odd, t // 2)
                    for q in range(4):
                        mm = pe.transpose(ps[0:ROWS[i], t % 2, q * R:(q + 1) * R], pbuf[G % 2][0:R, q, START[i]:END[i]],
                                          ident[0:R, 0:R])
                    mm.then_inc(pt_turned, 1)

                def weigh(G, i):
                    j = G // 2
                    R, t = ROWS[j], TP0[G] + i
                    pe.wait_ge(pt_even if t % 2 == 0 else pt_odd, t // 2 + 1)
                    if i == 0 and G >= 1:
                        pe.wait_ge(ol_ready, G)
                    pe.matmul(ps[:, 3, 0:4 * R], cmat[0:ROWS[i], i, :], pt_flat[0:ROWS[i], (t % 2) * 512:(t % 2) * 512 + 4 * R],
                              start=(i == 0), stop=(i == j)).then_inc(pv_step, 1)

                def project(j):
                    R = ROWS[j]
                    pe.wait_ge(ol_ready, 2 * j + 2)
                    if j >= 1:
                        pe.wait_ge(ya_lo, j)
                    for h in range(ATT_H):
                        mm = pe.matmul(ps[0:R, 2, h * ATT_D:(h + 1) * ATT_D], olt[h // 4][:, (h % 4) * R:(h % 4 + 1) * R],
                                       wuv[:, h, :], start=True, stop=True)
                    mm.then_inc(y_done, 1)

                def turn_y(j):
                    R = ROWS[j]
                    pe.wait_ge(y_ready, j + 1)
                    for c in range(4):
                        mm = pe.transpose(ps[:, 2, c * R:(c + 1) * R], yatt[0:R, c * P:(c + 1) * P], ident[0:R, 0:R])
                    mm.then_inc(yt_turned, 1)

                pe.wait_ge(ql_ready, ATT_H)
                late = None
                for G in range(2 * NT + 1):
                    if G < 2 * NT:
                        for q in range(4):
                            scores(4 * G + q)
                    if G == 0:
                        pe.wait_ge(yml_ready, ML_H)
                    if late is not None:
                        project(late)
                    if G >= 1:
                        j = (G - 1) // 2
                        turn(G - 1, 0)
                        for i in range(j + 1):
                            if i + 1 <= j:
                                turn(G - 1, i + 1)
                            weigh(G - 1, i)
                        if late is not None:
                            turn_y(late)
                        late = j if (G - 1) % 2 else None
                project(late)
                turn_y(late)

            turn_inputs()
            ffn(0)
            stats(0)
            mixer()
            stats(1)
            ffn(2)
            stats(2)
            for q in range(8):
                half, j = divmod(q, 4)
                if q >= 4:
                    pe.wait_ge(o_even if q % 2 == 0 else o_odd, (q - 4) // 2 + 1)
                pe.wait_ge(F[2]["aff_done"], 4 * half + 4)
                for c in range(4):
                    k = 4 * half + c
                    mm = pe.transpose(ps[:, j, c * P:(c + 1) * P], x[:, k, START[j + 1]:END[j + 1]], ident[:, :])
                mm.then_inc(o_turned, 1)

        @block.vector
        def _(dve):
            n_dv = [0]

            def link(ins):
                n_dv[0] += 1
                ins.then_inc(dv, 1)
                dve.wait_ge(dv, n_dv[0])

            def lo(u, s, width):
                dve.wait_ge(w_hi, u + 1)
                dve.tensor_tensor(wlo[:, s, 0:width], wraw[:, s, 0:width], whi[:, s, 0:width].bitcast(F32), ALU.subtract)\
                    .then_inc(w_lo, 1)

            def inputs():
                dve.wait_ge(vec_turned, 1)
                dve.tensor_copy(vec[:, :], ps[:, 7, 0:NV]).then_inc(vec_ready, 1)
                for k in range(KT):
                    b = 2 * (k % 3)
                    dve.wait_ge(x_turned, k + 1)
                    dve.tensor_copy(x[:, k, 0:END[3]], ps[:, b, 0:END[3]])
                    dve.tensor_copy(x[:, k, END[3]:T], ps[:, b + 1, 0:P]).then_inc(x_copied, 1)

            def residual(p, m, b, c):
                if p == 1:
                    filled(dve, 2 * N_PROJ + m)
                else:
                    dve.wait_ge(w_used, 2 * m + (UNIT0[p] + FT + 2))
                dve.scalar_tensor_tensor(halves(x[:, m, :]), pair(b), c, halves(x[:, m, :]), ALU.mult, ALU.add)\
                    .then_inc(F[p]["z_done"], 1)

            def ffn(p):
                s, u0 = F[p], UNIT0[p]

                def hidden(f, e):
                    dve.wait_ge(w_used, f + (u0 + 1))
                    dve.wait_ge(s["silu_done"], f + 1)
                    dve.tensor_tensor(halves(ht[:, e, :]), pair(4 * e + 2), halves(sil[:, e, :]), ALU.mult)\
                        .then_inc(s["mul_done"], 1)
                    dve.wait_ge(s["hh_done"], f + 1)
                    dve.tensor_tensor(hl[:, f, :], ht[:, e, :], hh[:, f, :].bitcast(F32), ALU.subtract)\
                        .then_inc(s["hl_done"], 1)

                lo(u0 + 1, 1, UW)
                hidden(0, 0)
                lo(u0 + 2, 0, UW)
                hidden(1, 1)
                with dve.Fori(1, FT // 2 - 1) as i:
                    for e in range(2):
                        lo(2 * i + (u0 + 1 + e), 1 - e, UW)
                        hidden(2 * i + e, e)
                lo(u0 + FT - 1, 1, UW)
                hidden(FT - 2, 0)
                lo(u0 + FT, 0, DOWN_W)
                hidden(FT - 1, 1)
                lo(u0 + FT + 1, 1, DOWN_W)
                lo(u0 + FT + 2, 0, DOWN_W)
                with dve.Fori(0, KT // 2 - 1) as i:
                    for e in range(2):
                        m = 2 * i + e
                        residual(p, m, 2 * e, 0.5 / ALPHA)
                        lo(2 * m + (u0 + FT + 3), 1, DOWN_W)
                        lo(2 * m + (u0 + FT + 4), 0, DOWN_W)
                residual(p, KT - 2, 0, 0.5 / ALPHA)
                lo(u0 + FT + 15, 1, DOWN_W)
                if p == 0:
                    lo(MIX0, 0, UW)
                residual(p, KT - 1, 2, 0.5 / ALPHA)

            def norm(p):
                s = F[p]
                eps = EPS / ALPHA ** 2
                dve.wait_ge(s["mu2_done"], 1)
                dve.tensor_tensor(halves(sil[:, 0, :]), pair(6), halves(sil[:, 0, :]), ALU.subtract).then_inc(s["var_done"], 1)
                dve.wait_ge(s["var_done"], 1)
                dve.tensor_scalar(sil[:, 0, :], sil[:, 0, :], eps, eps, ALU.add, ALU.max).then_inc(s["varc_done"], 1)
                dve.wait_ge(s["sd_done"], 1)
                dve.reciprocal(sil[:, 0, :], sil[:, 1, :]).then_inc(s["rstd_done"], 1)

                def centre(k):
                    if k >= 2:
                        dve.wait_ge(s["aff_done"], k - 1)
                    dve.tensor_tensor(halves(ht[:, k % 2, :]), halves(x[:, k, :]), pair(4), ALU.subtract)\
                        .then_inc(s["sub_done"], 1)

                centre(0)
                dve.wait_ge(s["rstd_done"], 1)
                for k in range(KT):
                    if k + 1 < KT:
                        centre(k + 1)
                    dve.wait_ge(s["sub_done"], k + 1)
                    dve.tensor_tensor(ht[:, k % 2, :], ht[:, k % 2, :], sil[:, 0, :], ALU.mult).then_inc(s["norm_done"], 1)

            def index_scores():
                dve.wait_ge(proj_evac, 4)
                link(dve.tensor_scalar(wi[:, :, :], small[:, :, 0:4], IDX_SCALE, None, ALU.mult))
                dve.wait_ge(par_in, 16 * 5)
                dve.tensor_tensor(gate[:, :, :], small[:, :, 4:12], bg[:, :].unsqueeze(1).broadcast_to([P, NT, 8]), ALU.add)\
                    .then_inc(gate_in, 1)
                sq = qk_flat[:, 0:NT * LAT]
                link(dve.tensor_tensor(sq, cs[:, 0:NT * LAT], cs[:, 0:NT * LAT], ALU.mult))
                link(dve.tensor_reduce(crms[:, 0, :], sq.rearrange("p (j c) -> p j c", j=NT), AX.X, ALU.add))
                dve.tensor_scalar(crms[:, 0, :], crms[:, 0, :], 1.0 / LAT, EPS, ALU.mult, ALU.add).then_inc(c_ms, 1)
                for k in range(4 * (NT - 1)):
                    j, h = 1 + k // 4, k % 4
                    dst = sc[:, SC_OFF[j]:SC_OFF[j] + END[j]]
                    dve.wait_ge(relu_done, k + 1)
                    src = sil[:, k % 2, 0:END[j]]
                    if h == 0:
                        dve.tensor_scalar(dst, src, wi[:, j, 0:1], None, ALU.mult).then_inc(acc_done, 1)
                    else:
                        dve.wait_ge(acc_done, k)
                        dve.scalar_tensor_tensor(dst, src, wi[:, j, h:h + 1], dst, ALU.mult, ALU.add).then_inc(acc_done, 1)
                dve.wait_ge(c_sd, 1)
                link(dve.reciprocal(crms[:, 0, :], crms[:, 1, :]))
                link(dve.tensor_tensor(cmat, cmat, crms[:, 0, :].unsqueeze(2).broadcast_to([P, NT, LAT]), ALU.mult))
                dve.tensor_tensor(cmat, cmat, kvg[:, :].unsqueeze(1).broadcast_to([P, NT, LAT]), ALU.mult).then_inc(c_ready, 1)

            def select(j):
                w = sc[:, SC_OFF[j]:SC_OFF[j] + END[j]]
                dve.wait_ge(idx_masked, j)
                for r in range(TOPK // 8):
                    link(dve.max(top8[:, r % 2, :], w))
                    link(dve.match_replace(w, top8[:, r % 2, :], w, TAKEN))
                dve.tensor_scalar(w, w, (MASKED + TAKEN) / 2, UNPICKED, ALU.is_gt, ALU.mult).then_inc(bias_ready, 1)

            def gate_rows():
                link(dve.memset(m_row, 0.0))

                def fetch(row, b, c):
                    dve.tensor_scalar(row[:, 0:END[3]], ps[0:4, b, 0:END[3]], c, None, ALU.mult)
                    return dve.tensor_scalar(row[:, END[3]:T], ps[0:4, b + 1, 0:P], c, None, ALU.mult)

                dve.wait_ge(row_turned, 1)
                link(fetch(ig_row, 6, SOFTCAP))
                dve.wait_ge(row_turned, 2)
                link(fetch(lf_row, 4, -1.0))
                link(dve.tensor_tensor_scan(b_row, lf_row, m_row, 0.0, ALU.add, ALU.add))
                link(dve.tensor_tensor(ig_row, ig_row, b_row, ALU.subtract))
                link(dve.tensor_tensor_scan(m_row, ig_row, ig_row, -1.0e30, ALU.max, ALU.max))
                link(dve.tensor_scalar(lf_row, m_row, -1.0, None, ALU.mult))
                dve.scalar_tensor_tensor(b_row, b_row, -1.0, m_row, ALU.mult, ALU.subtract).then_inc(row_ready, 1)

            def convolve():
                for c in range(4):
                    dve.wait_ge(proj_evac, 8 + c + 1)
                    for t in range(CONV):
                        tap = vec[:, V_CONV + 4 * t + c:V_CONV + 4 * t + c + 1]
                        src = up[:, c, t:t + T]
                        if t == 0:
                            ins = dve.tensor_scalar(qk[:, c, :], src, tap, None, ALU.mult)
                        else:
                            ins = dve.scalar_tensor_tensor(qk[:, c, :], src, tap, qk[:, c, :], ALU.mult, ALU.add)
                        if t < CONV - 1:
                            link(ins)
                    ins.then_inc(conv_done, 1)

            def mlstm():
                def arguments(h):
                    dve.wait_ge(nm_copied, h + 1)
                    if h >= 2:
                        dve.wait_ge(num_done, 2 * (h - 1))
                    for i in (0, 3, 4, 1, 2):
                        R = ROWS[i]
                        dve.tensor_scalar(wt(h, i, START[i], T), sil[0:R, h % 2, START[i]:T], tok[0:R, i, h:h + 1], 0.0,
                                          ALU.add, ALU.min).then_inc(arg_done, 1)

                def weights(h):
                    for b, parts in enumerate(ST_BANKS):
                        dve.wait_ge(st_done, 4 * h + b + 1)
                        dve.wait_ge(exp_done, 5 * h + (1, 3, 4, 5)[b])
                        for i, c0, c1, o in parts:
                            w = wt(h, i, c0, c1)
                            ins = dve.scalar_tensor_tensor(w, ps[0:ROWS[i], b, o:o + c1 - c0], K_SCALE, w, ALU.mult, ALU.mult)
                        ins.then_inc(st_used, 1)

                dve.wait_ge(tok_ready, 1)
                arguments(0)
                arguments(1)
                weights(0)
                weights(1)
                for h in (2, 3):
                    arguments(h)
                    weights(h)
                for h in range(ML_H):
                    for j in range(NT):
                        if j in (0, 3):
                            dve.wait_ge(num_copied, 2 * h + 1 + j // 3)
                        dve.bn_stats(bst[:, h * NT + j, :], nums[:, h, j, 0:ML_DV]).then_inc(dv, 1)
                        n_dv[0] += 1
                dve.wait_ge(dv, n_dv[0])
                for q in range(ML_H * NT):
                    dve.bn_aggr(mv[:, q, :], bst[:, q, :]).then_inc(dv, 1)
                    n_dv[0] += 1
                dve.wait_ge(dv, n_dv[0])
                hj = lambda v: v.rearrange("p (h j) -> p h j", h=ML_H)
                em = tok[:, :, :].rearrange("p j e -> p e j")[:, 4:8, :]
                den = nums[:, :, :, ML_DV]
                link(dve.scalar_tensor_tensor(hj(mls[:, 0, :]), den, -1.0, den, ALU.mult, ALU.max))
                link(dve.tensor_tensor(hj(mls[:, 0, :]), hj(mls[:, 0, :]), em, ALU.max))
                link(dve.reciprocal(mls[:, 1, :], mls[:, 0, :]))
                link(dve.tensor_tensor(mls[:, 0, :], mls[:, 1, :], mls[:, 1, :], ALU.mult))
                link(dve.tensor_tensor(mls[:, 0, :], mls[:, 0, :], mv[:, :, 1], ALU.mult))
                dve.tensor_scalar(mls[:, 0, :], mls[:, 0, :], EPS, None, ALU.add).then_inc(ml_var, 1)
                dve.wait_ge(ml_sd, 1)
                link(dve.reciprocal(mls[:, 2, :], mls[:, 0, :]))
                link(dve.tensor_tensor(mls[:, 2, :], mls[:, 2, :], mls[:, 1, :], ALU.mult))
                for h in range(ML_H):
                    for j in range(NT):
                        q = h * NT + j
                        v = nums[:, h, j, 0:ML_DV]
                        dve.tensor_scalar(v, v, mv[:, q, 0:1], mls[:, 2, q:q + 1], ALU.subtract, ALU.mult).then_inc(hn_ready, 1)
                for h in range(ML_H):
                    dve.wait_ge(hn_turned, h + 1)
                    if h >= 2:
                        dve.wait_ge(yml_lo, h - 1)
                    g = vec[:, V_MLG + h:V_MLG + h + 1]
                    b = 2 * (h % 2)
                    y = sil[:, h % 2, :]
                    dve.scalar_tensor_tensor(y[:, 0:END[3]], ps[:, b, 0:END[3]], g, sg[:, h, 0:END[3]], ALU.mult, ALU.mult)
                    dve.scalar_tensor_tensor(y[:, END[3]:T], ps[:, b + 1, 0:P], g, sg[:, h, END[3]:T], ALU.mult, ALU.mult)\
                        .then_inc(yml_ready, 1)

            def attention():
                def masked(k):
                    j, h = divmod(k, ATT_H)
                    R, n = ROWS[j], END[j]
                    dve.wait_ge(s_done, k + 1)
                    if k == 0:
                        dve.wait_ge(yml_lo, ML_H)
                    if k >= 2:
                        dve.wait_ge(p_ready, k - 1)
                    if h == 0:
                        dve.wait_ge(mask_ready, j + 1)
                    dst, msk = (like_keys(v, n) for v in (sil[0:R, k % 2, 0:n], sc[0:R, SC_OFF[j]:SC_OFF[j] + n]))
                    dve.tensor_tensor_reduce(dst, keys(R, n, 4 + 2 * (k % 2)), msk, 1.0, -3.0e38, ALU.add, ALU.max,
                                             smax[0:R, j, h:h + 1]).then_inc(s_masked, 1)
                    dve.wait_ge(s_masked, k + 1)
                    dve.tensor_scalar(nmax[0:R, j, h:h + 1], smax[0:R, j, h:h + 1], -ATT_SCALE, None, ALU.mult)\
                        .then_inc(nmax_ready, 1)

                def normalise(j):
                    R = ROWS[j]
                    dve.wait_ge(p_ready, ATT_H * (j + 1))
                    link(dve.reciprocal(rinv[0:R, j, :], rsum[0:R, j, :]))
                    dve.wait_ge(y_done, j + 1)
                    if j >= 1:
                        dve.wait_ge(yt_turned, j)
                    dve.tensor_tensor(yatt[0:R, :].rearrange("p (h d) -> p h d", h=ATT_H),
                                      ps[0:R, 2, :].rearrange("p (h d) -> p h d", h=ATT_H),
                                      rinv[0:R, j, :].unsqueeze(2).broadcast_to([R, ATT_H, ATT_D]), ALU.mult).then_inc(y_ready, 1)

                def att_lo(j):
                    dve.wait_ge(ya_hi, j + 1)
                    dve.tensor_tensor(xl[:, 0:4, START[j]:END[j]], ps[:, 2, 0:4 * ROWS[j]].rearrange("p (c r) -> p c r", c=4),
                                      xh[:, 0:4, START[j]:END[j]].bitcast(F32), ALU.subtract).then_inc(ya_lo, 1)

                late = None
                for G in range(2 * NT + 1):
                    if G < 2 * NT:
                        for q in range(4):
                            masked(4 * G + q)
                    if late is not None:
                        normalise(late)
                    if G >= 1:
                        j = (G - 1) // 2
                        for i in range(j + 1):
                            t = TP0[G - 1] + i
                            if t % 2 == 0:
                                dve.wait_ge(pt_turned, t + 1)
                                if t >= 2:
                                    dve.wait_ge(pv_step, t - 1)
                                dve.tensor_copy(pt_flat[0:ROWS[i], 0:4 * ROWS[j]], ps[0:ROWS[i], 0, 0:4 * ROWS[j]])\
                                    .then_inc(pt_even, 1)
                        if late is not None:
                            att_lo(late)
                        late = j if (G - 1) % 2 else None
                normalise(late)
                att_lo(late)

            dve.wait_ge(w_hi, 1)
            dve.tensor_tensor(wlo[:, 0, :], wraw[:, 0, :], whi[:, 0, :].bitcast(F32), ALU.subtract).then_inc(w_lo, 1)
            inputs()
            ffn(0)
            norm(0)
            index_scores()
            select(1)
            select(2)
            gate_rows()
            select(3)
            select(4)
            convolve()
            mlstm()
            attention()
            for m in range(KT):
                residual(1, m, 2 * (m % 2), 1.0 / ALPHA)
            norm(1)
            ffn(2)
            norm(2)
            for q in range(0, 8, 2):
                half, j = divmod(q, 4)
                dve.wait_ge(o_turned, q + 1)
                dve.tensor_copy(yout[:, j, half * 512:(half + 1) * 512], ps[:, j, :]).then_inc(o_even, 1)


_INS = ["x", "meta_tokens", "ln1_g", "ln1_b", "ffn1_w_gate", "ffn1_w_up", "ffn1_w_down", "w_in", "w_uk", "w_uv",
        "kv_norm_g", "conv_w", "b_igate", "b_fgate", "ml_norm_g", "w_out", "ln2_g", "ln2_b",
        "ffn2_w_gate", "ffn2_w_up", "ffn2_w_down", "ln3_g", "ln3_b"]


def kernel(**inputs):
    import concourse.bacc as _bacc
    from concourse.bass_utils import run_bass_kernel_spmd as _run

    nc = _bacc.Bacc("TRN2", target_bir_lowering=False, num_devices=1)
    arrays, aps = {}, {}
    for name in _INS:
        v = np.ascontiguousarray(inputs[name])
        arrays[f"in_{name}"] = v
        aps[name] = nc.dram_tensor(f"in_{name}", v.shape, mybir.dt.from_np(v.dtype), kind="ExternalInput").ap()
    out = nc.dram_tensor("out_0", (1, SEQ, D), F32, kind="ExternalOutput").ap()
    build(nc, aps, out)
    r = _run(nc, [arrays], core_ids=[0])
    return r.results[0]["out_0"]
```

```python
from contextlib import ExitStack

import numpy as np

import concourse.bass as bass
from concourse import mybir

F32 = mybir.dt.float32
F32R = mybir.dt.float32r
ALU = mybir.AluOpType
ACT = mybir.ActivationFunctionType
AX = mybir.AxisListType

P = 128
D = 1024
KT = D // P
N_META = 16
SEQ = 512
T = N_META + SEQ
HT = T // 2
D_FF = 2816
FT = D_FF // P
ATT_H, ATT_D, LAT = 8, 64, 128
IDX_H = 4
TOPK = min(256, SEQ // 4)
ML_H, ML_DV = 4, 128
CONV = 4
SOFTCAP = 15.0
EPS = 1e-5
ALPHA = 2.0 ** 0.25
IDX_SCALE = IDX_H ** -0.5 * 64 ** -0.5
ATT_SCALE = ATT_D ** -0.5
K_SCALE = 64 ** -0.5

START = [0] + [N_META + P * j for j in range(4)]
ROWS = [N_META] + [P] * 4
NT = len(START)
END = [s + r for s, r in zip(START, ROWS)]

C_QA, C_CKV, C_QI, C_KI, C_WI = 0, 512, 640, 896, 960
C_QK, C_V, C_O, C_IF = 964, 1476, 1988, 2500
S_KI, S_WI, S_IF = 128, 192, 248

UW = 2048
HALF_W = UW // 2
HALF_FT = FT // 2
DOWN_W = HALF_FT * P
FFN_UNITS = FT + 2 * KT
MIX_UNITS = 14
UNIT0 = {0: 0, 2: FFN_UNITS + MIX_UNITS}
MIX0 = FFN_UNITS
N_PROJ = 10
LATE_UNITS = {1: 12, 3: 13, 5: 14}
GROUPS = 2 * (NT - 1)

V_G = [0, 16, 32]
V_B = [8, 24, 40]
V_MLG, V_CONV = 48, 52
NV = V_CONV + CONV * 4

MASKED, TAKEN, UNPICKED = -2.0e38, -3.0e38, -1.0e30


def build(nc, a, out):
    ctx = ExitStack()
    with ctx:
        def sb(name, shape, dt=F32, scope=ctx):
            return scope.enter_context(nc.sbuf_tensor(name, shape, dt))

        def sem(name):
            return ctx.enter_context(nc.semaphore(name))

        ps = ctx.enter_context(nc.psum_tensor("ps", [P, 8, 512], F32))

        ST_BANKS = [[(0, 0)], [(1, 0)], [(2, 0)], [(3, 0), (4, T - START[3])]]

        def pair(b):
            return ps[:, b:b + 2, 0:HT]

        x = sb("x", [P, KT, T])
        xh = sb("xh", [P, KT, T], F32R)
        xl = sb("xl", [P, KT, T], F32R)
        wraw = sb("wraw", [P, 2, UW])
        whi = sb("whi", [P, 2, UW], F32R)
        wlo = sb("wlo", [P, 2, UW], F32R)
        sil = sb("sil", [P, 2, T])
        ht = sb("ht", [P, 2, T])
        ident = sb("ident", [P, P])
        mean_w = sb("mean_w", [P, P])
        vec = sb("vec", [P, NV])
        vrows = sb("vrows", [NV, P])
        zsum, ssum = ht[:, 0, :], ht[:, 1, :]

        def cols(v, p):
            return halves(v) if p == 0 else v[:, N_META:T]

        def flat(v, p):
            return v if p == 0 else v[:, N_META:T]

        def bank(b, p):
            return pair(b) if p == 0 else ps[:, b, :]

        def moving(v, p):
            if p == 0:
                return [(e, HT, v[:, e * HT:(e + 1) * HT]) for e in range(2)]
            return [(0, SEQ, v[:, N_META:T])]

        def halves(v):
            return v.rearrange("p (b n) -> p b n", b=2)

        with ExitStack() as s:
            xin = sb("xin", [P, NT, D], F32, s)
        with ExitStack() as s:
            hh = sb("hh", [P, FT, T], F32R, s)
            hl = sb("hl", [P, FT, T], F32R, s)
        with ExitStack() as s:
            qi = sb("qi", [P, 4, T], F32, s)
            qa = sb("qa", [P, 4, T], F32, s)
            ql = sb("ql", [P, ATT_H, T], F32, s)
            ct = sb("ct", [P, T], F32, s)
            cs = sb("cs", [P, NT, 256], F32, s)
            wuk = sb("wuk", [P, 4, LAT], F32, s)
            wuv = sb("wuv", [P, ATT_H, ATT_D], F32, s)
            qk = sb("qk", [P, 4, T], F32, s)
            upad = sb("upad", [P, 4 * (T + CONV - 1)], F32, s)
            v1 = sb("v1", [P, NT, ML_H, ML_DV + 1], F32, s)
            sg = sb("sg", [P, 4, T], F32, s)
            sc = sb("sc", [P, sum(END[1:])], F32, s)
            rows = sb("rows", [P, 2, T], F32, s)
            kvg = sb("kvg", [P, LAT], F32, s)
            bg = sb("bg", [P, 8], F32, s)
            wi = sb("wi", [P, NT, IDX_H], F32, s)
            gate = sb("gate", [P, NT, 8], F32, s)
            gate2 = sb("gate2", [P, NT, 4], F32, s)
            tok = sb("tok", [P, NT, 8], F32, s)
            top8 = sb("top8", [P, 2, 8], F32, s)
            crms = sb("crms", [P, 2, NT], F32, s)
            smax = sb("smax", [P, NT, ATT_H], F32, s)
            nmax = sb("nmax", [P, NT, ATT_H], F32, s)
            rsum = sb("rsum", [P, NT, ATT_H], F32, s)
            rinv = sb("rinv", [P, NT, ATT_H], F32, s)
            bst = sb("bst", [P, ML_H * 4, 6], F32, s)
            mv = sb("mv", [P, ML_H * 4, 2], F32, s)
            mls = sb("mls", [P, 3, ML_H * 4], F32, s)
        with ExitStack() as s:
            yout = sb("yout", [P, 4, D], F32, s)

        SC_OFF = [None] + [sum(END[1:j]) for j in range(1, NT)]
        kit = qi[:, 2, :]
        wt_flat = ql[:, :, :].rearrange("p h t -> p (h t)")
        TP0 = [0]
        for G in range(GROUPS):
            TP0.append(TP0[-1] + G // 2 + 2)
        QS = [max(s_, N_META) for s_ in START]
        WT_OFF = [sum(T - QS[k] for k in range(i)) for i in range(NT)]
        WT_W = sum(T - s_ for s_ in QS)

        def wt(h, i, c0, c1):
            o = (0, WT_W, 0, 0)[h] + WT_OFF[i] - QS[i]
            return (qi_flat if h == 2 else wt_flat)[0:ROWS[i], o + c0:o + c1]

        sel = wt_flat[:, 2 * WT_W:2 * WT_W + 4 * P]
        up = upad[:, :].rearrange("p (c t) -> p c t", c=4)
        nums = upad[:, 0:ML_H * 4 * (ML_DV + 1)].rearrange("p (h j v) -> p h j v", h=ML_H, j=4)
        pbuf = [upad[:, 0:4 * T].rearrange("p (h t) -> p h t", h=4), qi[:, :, :]]
        qi_flat = qi[:, :, :].rearrange("p c t -> p (c t)")
        yml = qi_flat[:, 0:ML_H * SEQ].rearrange("p (h n) -> p h n", h=ML_H)
        pt_flat = v1[:, :, :, :].rearrange("p j h v -> p (j h v)")
        qk_flat = qk[:, :, :].rearrange("p c t -> p (c t)")
        olt = [qk_flat[:, g * 512:(g + 1) * 512] for g in range(2)]
        yatt = qk_flat[:, 1024:1536]
        ig_row, lf_row = ht[0:4, 0, :], ht[0:4, 1, :]
        b_row, m_row = rows[0:4, 0, :], rows[0:4, 1, :]
        cmat = cs[:, :, 0:LAT]

        x_split = sem("x_split")
        const_ready = sem("const_ready")
        rows_in = [sem("rows_in0"), sem("rows_in1")]
        vrows_in = sem("vrows_in")
        x_turned = sem("x_turned")
        vec_turned = sem("vec_turned")
        vec_ready = sem("vec_ready")
        x_copied = sem("x_copied")
        xin_hi = sem("xin_hi")
        raw_in = [sem("raw_in0"), sem("raw_in1")]
        gate0_in = sem("gate0_in")
        gate0_hi = sem("gate0_hi")
        gate0_lo = sem("gate0_lo")
        w_hi = sem("w_hi")
        w_lo = sem("w_lo")
        w_used = sem("w_used")
        F = []
        for p in range(3):
            names = ["gate_done", "silu_done", "mul_done", "hh_done", "hl_done"] if p != 1 else []
            names += ["z_done", "sq_done", "sums_done", "zsum_done", "stats_done", "mu2_done",
                      "var_done", "varc_done", "sd_done", "rstd_done", "sub_done", "norm_done", "hi_done", "aff_done", "split_done"]
            F.append({n: sem(f"{n}{p}") for n in names})
        half_done = sem("half_done")
        proj_evac = sem("proj_evac")
        par_in = sem("par_in")
        pad_ready = sem("pad_ready")
        idx_done = sem("idx_done")
        relu_done = sem("relu_done")
        acc_done = sem("acc_done")
        idx_masked = sem("idx_masked")
        bias_ready = sem("bias_ready")
        mask_ready = sem("mask_ready")
        dv = sem("dv")
        ac = sem("ac")
        pl = sem("pl")
        c_ms = sem("c_ms")
        c_sd = sem("c_sd")
        c_ready = sem("c_ready")
        ct_turned = sem("ct_turned")
        ct_ready = sem("ct_ready")
        ki_turned = sem("ki_turned")
        ki_ready = sem("ki_ready")
        gate_in = sem("gate_in")
        gate_act = sem("gate_act")
        row_turned = sem("row_turned")
        row_copied = sem("row_copied")
        row_ready = sem("row_ready")
        tok_turned = sem("tok_turned")
        tok_ready = sem("tok_ready")
        conv_done = sem("conv_done")
        qk_ready = sem("qk_ready")
        nm_spread = sem("nm_spread")
        arg_done = sem("arg_done")
        exp_done = sem("exp_done")
        st_done = sem("st_done")
        st_used = sem("st_used")
        wt_masked = sem("wt_masked")
        num_done = sem("num_done")
        num_copied = sem("num_copied")
        ml_var = sem("ml_var")
        ml_sd = sem("ml_sd")
        hn_ready = sem("hn_ready")
        hn_turned = sem("hn_turned")
        yml_ready = sem("yml_ready")
        yml_hi = sem("yml_hi")
        yml_lo = sem("yml_lo")
        ql_done = sem("ql_done")
        ql_ready = sem("ql_ready")
        s_done = sem("s_done")
        s_masked = sem("s_masked")
        nmax_ready = sem("nmax_ready")
        p_ready = sem("p_ready")
        pt_turned = sem("pt_turned")
        pt_even = sem("pt_even")
        pt_odd = sem("pt_odd")
        pv_step = sem("pv_step")
        ol_ready = sem("ol_ready")
        y_done = sem("y_done")
        y_ready = sem("y_ready")
        yt_turned = sem("yt_turned")
        ya_hi = sem("ya_hi")
        ya_lo = sem("ya_lo")
        o_turned = sem("o_turned")
        o_even = sem("o_even")
        o_odd = sem("o_odd")
        stored = sem("stored")

        block = ctx.enter_context(nc.Block())

        def landed(u, s, late):
            return 16 * u + (32 - 16 * s + (16 if late and s else 0))

        def filled(eng, use):
            if use % 2 == 0:
                eng.wait_ge(half_done, use // 2 + 1)
            else:
                eng.wait_ge(w_used, MIX0 + use // 2 + 1)

        def keys(r, n, b):
            return ps[0:r, b, 0:n] if n <= 512 else ps[0:r, b:b + 2, 0:n // 2]

        def like_keys(v, n):
            return v if n <= 512 else halves(v)

        def kview(w):
            return w[0].rearrange("(k p) n -> p k n", p=P)

        def slot3(t, s, n):
            return t[:, s, 0:(UW // n if n != P else UW // P) * n].rearrange("p (k n) -> p k n", n=n)

        @block.sync
        def _(sp):
            w_in = kview(a["w_in"])
            w_out = kview(a["w_out"])

            def load_inputs(c):
                w = slice(c * (D // 2), (c + 1) * (D // 2))
                sp.dma_start(xin[0:N_META, 0, w], a["meta_tokens"][:, w]).then_inc(rows_in[c], 16)
                for j in range(1, NT):
                    sp.dma_start(xin[:, j, w], a["x"][0, (j - 1) * P:j * P, w]).then_inc(rows_in[c], 16)

            def slot_free(u, first):
                if not first:
                    sp.wait_ge(w_lo, u - 1)

            def load_gate_up(p, s, f, u, first=False):
                slot_free(u, first)
                g, v = kview(a[f"ffn{p // 2 + 1}_w_gate"]), kview(a[f"ffn{p // 2 + 1}_w_up"])
                dst = wraw[:, s, :].rearrange("p (m k n) -> p m k n", m=2, n=P)
                if first and s == 0:
                    sp.dma_start(dst[:, 0], g[:, :, bass.ts(f, P)]).then_inc(gate0_in, 16)
                    load_inputs(0)
                    for k0 in (0, 4):
                        sp.dma_start(dst[:, 1, k0:k0 + 4], v[:, k0:k0 + 4, bass.ts(f, P)]).then_inc(raw_in[s], 16)
                    return
                sp.dma_start(dst[:, 0], g[:, :, bass.ts(f, P)]).then_inc(raw_in[s], 16)
                sp.dma_start(dst[:, 1], v[:, :, bass.ts(f, P)]).then_inc(raw_in[s], 16)

            def load_down(p, half, m, u):
                slot_free(u, False)
                w = kview(a[f"ffn{p // 2 + 1}_w_down"])
                dst = wraw[:, half, 0:DOWN_W].rearrange("p (k n) -> p k n", n=P)
                for k0, k1 in ((0, 6), (6, HALF_FT)):
                    sp.dma_start(dst[:, k0:k1, :],
                                 w[:, half * HALF_FT + k0:half * HALF_FT + k1, bass.ts(m, P)]).then_inc(raw_in[half], 16)

            def ffn(p):
                u0 = UNIT0[p]
                for s in range(2):
                    load_gate_up(p, s, s, u0 + s, first=(p == 0))
                    if p == 0 and s == 0:
                        load_inputs(1)
                if p == 0:
                    load_vectors()
                with sp.Fori(1, FT // 2) as i:
                    for s in range(2):
                        load_gate_up(p, s, 2 * i + s, 2 * i + (u0 + s))
                with sp.Fori(0, KT) as m:
                    for half in range(2):
                        load_down(p, half, m, 2 * m + (u0 + FT + half))

            def mixer():
                for n in range(MIX_UNITS):
                    u = MIX0 + n
                    s = u % 2
                    slot_free(u, False)
                    dst = slot3(wraw, s, 256)
                    if n == 1:
                        sp.dma_start(dst[:, :, 0:LAT], w_in[:, :, C_CKV:C_CKV + LAT]).then_inc(raw_in[s], 16)
                        sp.dma_start(dst[:, :, LAT:S_IF], w_in[:, :, C_KI:C_KI + S_IF - LAT]).then_inc(raw_in[s], 16)
                        sp.dma_start(dst[:, :, S_IF:256], w_in[:, :, C_IF:C_IF + 8]).then_inc(raw_in[s], 16)
                        continue
                    if n == 3:
                        load_mixer_params()
                    if n < N_PROJ:
                        c0 = {0: C_QI, 2: C_QA, 3: C_QA + 256, 4: C_QK, 5: C_QK + 256, 6: C_V, 7: C_V + 256,
                              8: C_O, 9: C_O + 256}[n]
                        src = w_in[:, :, c0:c0 + 256]
                    else:
                        src = w_out[:, :, (n - N_PROJ) * 256:(n - N_PROJ + 1) * 256]
                    for k0 in (0, 4):
                        sp.dma_start(dst[:, k0:k0 + 4, :], src[:, k0:k0 + 4, :]).then_inc(raw_in[s], 16)

            def load_mixer_params():
                sp.wait_ge(w_used, FFN_UNITS)
                sp.dma_start(wuk[:, :, :], a["w_uk"][0].rearrange("(q two) d c -> (two d) q c", two=2)).then_inc(par_in, 16)
                sp.dma_start(wuv[:, :, :], a["w_uv"][0].rearrange("h c d -> c h d")).then_inc(par_in, 16)
                sp.dma_start(kvg[:, :], a["kv_norm_g"].broadcast_to([P, LAT])).then_inc(par_in, 16)
                sp.dma_start(bg[:, 0:4], a["b_igate"].broadcast_to([P, 4])).then_inc(par_in, 16)
                sp.dma_start(bg[:, 4:8], a["b_fgate"].broadcast_to([P, 4])).then_inc(par_in, 16)

            def load_vectors():
                r = 0
                for name in ("ln1_g", "ln1_b", "ln2_g", "ln2_b", "ln3_g", "ln3_b"):
                    sp.dma_start(vrows[r:r + KT, :], a[name].rearrange("o (k p) -> (o k) p", p=P)).then_inc(vrows_in, 16)
                    r += KT
                sp.dma_start(vrows[V_MLG:V_CONV, :], a["ml_norm_g"].rearrange("o (k p) -> (o k) p", p=P)).then_inc(vrows_in, 16)
                sp.dma_start(vrows[V_CONV:NV, :], a["conv_w"].rearrange("o j (c p) -> (o j c) p", p=P)).then_inc(vrows_in, 16)

            ffn(0)
            mixer()
            ffn(2)
            for q in range(8):
                half, j = divmod(q, 4)
                sp.wait_ge(o_even if q % 2 == 0 else o_odd, q // 2 + 1)
                sp.dma_start(out[0, j * P:(j + 1) * P, half * 512:(half + 1) * 512],
                             yout[:, j, half * 512:(half + 1) * 512]).then_inc(stored, 16)
            sp.wait_ge(stored, 8 * 16)

        @block.gpsimd
        def _(pool):
            n_pl = [0]

            def link(ins):
                n_pl[0] += 1
                ins.then_inc(pl, 1)
                pool.wait_ge(pl, n_pl[0])

            def constants():
                link(pool.memset(ident[:, :], 0.0))
                pool.affine_select(out=ident[:, :], in_=ident[:, :], compare_op=ALU.not_equal, fill=1.0,
                                   base=0, pattern=[[-1, P]], channel_multiplier=1).then_inc(const_ready, 1)
                pool.memset(mean_w[:, :], 1.0 / D).then_inc(const_ready, 1)

            def x_lo(k, hi_sem, n, done, p):
                pool.wait_ge(hi_sem, n)
                pool.tensor_tensor(flat(xl[:, k, :], p), flat(x[:, k, :], p), flat(xh[:, k, :], p).bitcast(F32), ALU.subtract)\
                    .then_inc(done, 1)

            def sums(p):
                s = F[p]
                if p != 1:
                    pool.wait_ge(s["hl_done"], FT)
                else:
                    pool.wait_ge(nm_spread, ML_H)
                    pool.wait_ge(tok_turned, 1)
                pool.memset(zsum, 0.0).then_inc(s["sums_done"], 1)
                pool.memset(ssum, 0.0).then_inc(s["sums_done"], 1)
                pool.wait_ge(s["sums_done"], 2)
                zs, ss = flat(zsum, p), flat(ssum, p)

                def add(m, sq_slot, n):
                    pool.wait_ge(s["z_done"], n)
                    pool.tensor_tensor(zs, zs, flat(x[:, m, :], p), ALU.add).then_inc(s["zsum_done"], 1)
                    pool.wait_ge(s["sq_done"], n)
                    pool.tensor_tensor(ss, ss, flat(sil[:, sq_slot, :], p), ALU.add).then_inc(s["sums_done"], 1)
                    pool.wait_ge(s["zsum_done"], n)
                    pool.wait_ge(s["sums_done"], n + 2)

                if p != 1:
                    with pool.Fori(0, KT // 2 - 1) as i:
                        for e in range(2):
                            add(2 * i + e, e, 2 * i + (e + 1))
                    add(KT - 2, 0, KT - 1)
                    return
                for m in range(KT - 1):
                    add(m, m % 2, m + 1)

            def norm_lo(p):
                for k in range(KT):
                    x_lo(k, F[p]["aff_done"], k + 1, F[p]["split_done"], p)

            def mix_lo(n):
                u = MIX0 + n
                pool.wait_ge(w_hi, u + 1)
                pool.tensor_tensor(wlo[:, u % 2, :], wraw[:, u % 2, :], whi[:, u % 2, :].bitcast(F32), ALU.subtract)\
                    .then_inc(w_lo, 1)

            def mixer():
                pool.wait_ge(w_used, FFN_UNITS)
                pool.memset(up[:, :, 0:CONV - 1], 0.0).then_inc(pad_ready, 1)
                link(pool.memset(sel, 0.0))
                pool.affine_select(out=sel.rearrange("p (h n) -> p h n", h=4), in_=sel.rearrange("p (h n) -> p h n", h=4),
                                   compare_op=ALU.not_equal, fill=1.0, base=0, pattern=[[-1, 4], [0, P]],
                                   channel_multiplier=1).then_inc(pad_ready, 1)
                pool.memset(v1[:, :, :, ML_DV:ML_DV + 1], 1.0).then_inc(pad_ready, 1)
                mix_lo(1)
                norm_lo(0)
                mix_lo(2)
                mix_lo(3)
                for j in range(1, NT):
                    pool.wait_ge(acc_done, 4 * j)
                    d = sc[:, SC_OFF[j] + START[j]:SC_OFF[j] + END[j]]
                    pool.affine_select(out=d, in_=d, compare_op=ALU.is_ge, fill=MASKED, base=0,
                                       pattern=[[-1, P]], channel_multiplier=1).then_inc(idx_masked, 1)
                for n in range(4, N_PROJ + 1):
                    mix_lo(n)
                for j in range(1, NT):
                    pool.wait_ge(bias_ready, j)
                    d = sc[:, SC_OFF[j] + START[j]:SC_OFF[j] + END[j]]
                    pool.affine_select(out=d, in_=d, compare_op=ALU.is_ge, fill=UNPICKED, base=0,
                                       pattern=[[-1, P]], channel_multiplier=1).then_inc(mask_ready, 1)
                mix_lo(N_PROJ + 1)
                for h in range(ML_H):
                    for i in range(1, NT):
                        pool.wait_ge(st_used, 4 * h + min(i, 3) + 1)
                        d = wt(h, i, START[i], END[i])
                        pool.affine_select(out=d, in_=d, compare_op=ALU.is_ge, fill=0.0, base=0,
                                           pattern=[[1, ROWS[i]]], channel_multiplier=-1).then_inc(wt_masked, 1)
                for h in range(ML_H):
                    pool.wait_ge(yml_hi, h + 1)
                    pool.tensor_tensor(xl[:, 4 + h, N_META:T], yml[:, h, :], xh[:, 4 + h, N_META:T].bitcast(F32),
                                       ALU.subtract)\
                        .then_inc(yml_lo, 1)

            constants()
            for k in range(KT):
                x_lo(k, xin_hi, k + 1, x_split, 0)
            sums(0)
            mixer()
            sums(1)
            norm_lo(1)
            sums(2)

        @block.scalar
        def _(act):
            n_ac = [0]

            def link(ins):
                n_ac[0] += 1
                ins.then_inc(ac, 1)
                act.wait_ge(ac, n_ac[0])

            def hi(u, s, width, late, first=False):
                act.wait_ge(raw_in[s], landed(u, s, late))
                if not first:
                    act.wait_ge(w_used, u - 1)
                act.activation(whi[:, s, 0:width], wraw[:, s, 0:width], ACT.Copy).then_inc(w_hi, 1)

            def input_hi():
                for k in range(KT):
                    if k == 0:
                        act.wait_ge(gate0_in, 16)
                        act.activation(whi[:, 0, 0:HALF_W], wraw[:, 0, 0:HALF_W], ACT.Copy).then_inc(gate0_hi, 1)
                    if k == KT // 2:
                        act.wait_ge(raw_in[0], 32)
                        act.activation(whi[:, 0, HALF_W:UW], wraw[:, 0, HALF_W:UW], ACT.Copy).then_inc(w_hi, 1)
                    act.wait_ge(x_copied, k + 1)
                    act.activation(xh[:, k, :], x[:, k, :], ACT.Copy).then_inc(xin_hi, 1)

            def ffn(p):
                s, u0, late = F[p], UNIT0[p], p > 0

                def hidden(f, e, first):
                    act.wait_ge(s["gate_done"], f + 1)
                    if not first:
                        act.wait_ge(s["mul_done"], f - 1)
                    act.activation(cols(sil[:, e, :], p), bank(4 * e, p), ACT.Silu).then_inc(s["silu_done"], 1)
                    act.wait_ge(s["mul_done"], f + 1)
                    act.activation(flat(hh[:, f, :], p), flat(ht[:, e, :], p), ACT.Copy).then_inc(s["hh_done"], 1)

                hi(u0 + 1, 1, UW, late, first=(p == 0))
                hidden(0, 0, True)
                hi(u0 + 2, 0, UW, late)
                hidden(1, 1, True)
                with act.Fori(1, FT // 2 - 1) as i:
                    for e in range(2):
                        hi(2 * i + (u0 + 1 + e), 1 - e, UW, late)
                        hidden(2 * i + e, e, False)
                hi(u0 + FT - 1, 1, UW, late)
                hidden(FT - 2, 0, False)
                hi(u0 + FT, 0, DOWN_W, late)
                hidden(FT - 1, 1, False)
                hi(u0 + FT + 1, 1, DOWN_W, late)
                hi(u0 + FT + 2, 0, DOWN_W, late)
                with act.Fori(0, KT // 2 - 1) as i:
                    for e in range(2):
                        m = 2 * i + e
                        square(p, m, e)
                        hi(2 * m + (u0 + FT + 3), 1, DOWN_W, late)
                        hi(2 * m + (u0 + FT + 4), 0, DOWN_W, late)
                square(p, KT - 2, 0)
                hi(u0 + FT + 15, 1, DOWN_W, late)
                if p == 0:
                    hi(MIX0, 0, UW, late)
                square(p, KT - 1, 1)
                if p == 0:
                    hi(MIX0 + 1, 1, UW, True)

            def square(p, m, e):
                s = F[p]
                act.wait_ge(s["z_done"], m + 1)
                act.wait_ge(s["sums_done"], m + 1)
                act.activation(flat(sil[:, e, :], p), flat(x[:, m, :], p), ACT.Square).then_inc(s["sq_done"], 1)

            def norm(p):
                s = F[p]
                act.wait_ge(s["stats_done"], 1)
                act.activation(cols(sil[:, 0, :], p), bank(4, p), ACT.Square).then_inc(s["mu2_done"], 1)
                act.wait_ge(s["varc_done"], 1)
                act.activation(flat(sil[:, 1, :], p), flat(sil[:, 0, :], p), ACT.Sqrt).then_inc(s["sd_done"], 1)
                for k in range(KT):
                    act.wait_ge(s["norm_done"], k + 1)
                    if k == 0:
                        act.wait_ge(vec_ready, 1)
                    g, b = vec[:, V_G[p] + k:V_G[p] + k + 1], vec[:, V_B[p] + k:V_B[p] + k + 1]
                    xk = flat(x[:, k, :], p)
                    if p != 2:
                        act.activation(flat(xh[:, k, :], p), xk, ACT.Identity, bias=b, scale=g).then_inc(s["hi_done"], 1)
                    act.activation(xk, xk, ACT.Identity, bias=b, scale=g).then_inc(s["aff_done"], 1)

            def proj_out(n, src, dst, func=ACT.Copy):
                filled(act, n)
                act.activation(dst, src, func).then_inc(proj_evac, 1)

            def mixer():
                for c in range(2):
                    proj_out(c, pair(2 * c), halves(qi[:, c, :]))
                hi(MIX0 + 2, 0, UW, False)
                for n, (j0, j1) in ((2, (0, 4)), (3, (4, 5))):
                    filled(act, n)
                    src = ps[:, 0:2, :] if n == 2 else ps[:, 2, 0:256]
                    dst = cs[:, j0:j1, :].rearrange("p j n -> p (j n)")
                    act.activation(halves(dst) if n == 2 else dst, src, ACT.Copy).then_inc(proj_evac, 1)
                hi(MIX0 + 3, 1, UW, True)
                proj_out(4, pair(0), halves(qa[:, 0, :]))
                for c in range(2):
                    act.wait_ge(ki_turned, c + 1)
                    r = slice(64 * c, 64 * c + 64)
                    act.activation(kit[r, 0:END[3]], ps[r, 4 + 2 * c, 0:END[3]], ACT.Copy)
                    act.activation(kit[r, END[3]:T], ps[r, 5 + 2 * c, 0:P], ACT.Copy).then_inc(ki_ready, 1)
                for k in range(4 * (NT - 1)):
                    j = 1 + k // 4
                    act.wait_ge(idx_done, k + 1)
                    if k >= 2:
                        act.wait_ge(acc_done, k - 1)
                    src = keys(ROWS[j], END[j], 4 + 2 * (k % 2))
                    dst = like_keys(sil[0:ROWS[j], k % 2, 0:END[j]], END[j])
                    act.activation(dst, src, ACT.Relu).then_inc(relu_done, 1)
                act.wait_ge(c_ms, 1)
                act.activation(crms[:, 1, :], crms[:, 0, :], ACT.Sqrt).then_inc(c_sd, 1)
                act.wait_ge(gate_in, 1)
                link(act.activation(gate[:, :, :], gate[:, :, :], ACT.Tanh, scale=1.0 / SOFTCAP))
                link(act.activation(gate2[:, :, :], gate[:, :, 4:8], ACT.Exp, scale=-SOFTCAP))
                act.activation(gate2[:, :, :], gate2[:, :, :], ACT.Ln, bias=1.0).then_inc(gate_act, 1)
                proj_out(5, pair(2), halves(qa[:, 1, :]))
                act.wait_ge(ct_turned, 1)
                act.activation(ct[:, 0:END[3]], ps[:, 4, 0:END[3]], ACT.Copy)
                act.activation(ct[:, END[3]:T], ps[:, 5, 0:P], ACT.Copy).then_inc(ct_ready, 1)
                hi(MIX0 + 4, 0, UW, False)
                for c in range(2):
                    proj_out(6 + c, pair(2 * c), halves(qa[:, 2 + c, :]))
                hi(MIX0 + 5, 1, UW, True)
                act.wait_ge(pad_ready, 1)
                for n in (4, 5):
                    for c in range(2):
                        proj_out(2 * n + c, pair(2 * c), halves(up[:, 2 * (n - 4) + c, CONV - 1:CONV - 1 + T]))
                    hi(MIX0 + n + 2, n % 2, UW, True)
                act.wait_ge(tok_turned, 1)
                tt = ps[:, 6, 0:NT * 8].rearrange("p (j e) -> p j e", e=8)
                act.activation(tok[:, :, 0:4], tt[:, :, 0:4], ACT.Copy)
                act.activation(tok[:, :, 4:8], tt[:, :, 4:8], ACT.Exp).then_inc(tok_ready, 1)
                for n in (6, 7):
                    h0 = 2 * (n - 6)
                    proj_out(2 * n, ps[:, 0:2, :].rearrange("p b (j h v) -> p (b j) h v", j=2, h=2),
                             v1[:, 0:4, h0:h0 + 2, 0:ML_DV])
                    proj_out(2 * n + 1, ps[:, 2, 0:256].rearrange("p (h v) -> p h v", h=2),
                             v1[:, 4, h0:h0 + 2, 0:ML_DV])
                    hi(MIX0 + n + 2, n % 2, UW, True)
                for c in range(4):
                    act.wait_ge(conv_done, c + 1)
                    act.activation(qk[:, c, :], qk[:, c, :], ACT.Silu).then_inc(qk_ready, 1)
                def exps(h):
                    for i in range(NT):
                        act.wait_ge(arg_done, 5 * h + i + 1)
                        w = wt(h, i, QS[i], T)
                        act.activation(w, w, ACT.Exp).then_inc(exp_done, 1)

                for n in (8, 9):
                    for c in range(2):
                        proj_out(2 * n + c, pair(2 * c), halves(sg[:, 2 * (n - 8) + c, :]), ACT.Sigmoid)
                    hi(MIX0 + n + 2, n % 2, UW, True)
                    if n == 8:
                        exps(0)
                        exps(1)
                exps(2)
                def copy_num(h):
                    for c, b in ((0, 4), (1, 7)):
                        act.wait_ge(num_done, 2 * h + c + 1)
                        act.activation(nums[:, h, 2 * c:2 * c + 2, :],
                                       ps[:, b, 0:2 * (ML_DV + 1)].rearrange("p (j v) -> p j v", j=2),
                                       ACT.Copy).then_inc(num_copied, 1)

                copy_num(0)
                exps(3)
                for h in range(1, ML_H):
                    copy_num(h)
                for h in range(ATT_H):
                    if h == 2:
                        act.wait_ge(ml_var, 1)
                        act.activation(mls[:, 0, :], mls[:, 0, :], ACT.Sqrt).then_inc(ml_sd, 1)
                    act.wait_ge(ql_done, h + 1)
                    act.activation(ql[:, h, N_META:T], ps[:, 4 + h % 4, :], ACT.Copy).then_inc(ql_ready, 1)
                attention()
                for m in range(KT):
                    square(1, m, m % 2)
                    if m in LATE_UNITS:
                        hi(MIX0 + LATE_UNITS[m], LATE_UNITS[m] % 2, UW, True)

            def mlstm_hi(h):
                act.wait_ge(yml_ready, h + 1)
                act.activation(xh[:, 4 + h, N_META:T], yml[:, h, :], ACT.Copy).then_inc(yml_hi, 1)

            def attention():
                def exps(G, qs):
                    j, g = 1 + G // 2, G % 2
                    n = END[j]
                    for q in qs:
                        k = 4 * G + q
                        h = 4 * g + q
                        act.wait_ge(nmax_ready, k + 1)
                        if q == 0 and G >= 2:
                            act.wait_ge(pt_turned, TP0[G - 1])
                        if q == 0 and G == 0:
                            act.wait_ge(hn_turned, ML_H)
                        if q == 0 and G == 1:
                            act.wait_ge(yml_lo, ML_H)
                        act.activation(pbuf[G % 2][:, q, 0:n], sil[:, k % 2, 0:n], ACT.Exp,
                                       bias=nmax[:, j, h:h + 1], scale=ATT_SCALE,
                                       accum_out=rsum[:, j, h:h + 1]).then_inc(p_ready, 1)

                def copy_odd(G, tiles):
                    for i in tiles:
                        t = TP0[G] + i
                        if t % 2 == 1:
                            act.wait_ge(pt_turned, t + 1)
                            if t >= 2:
                                act.wait_ge(pv_step, t - 1)
                            act.activation(pt_flat[0:ROWS[i], 512:1024], ps[0:ROWS[i], 1, :], ACT.Copy)\
                                .then_inc(pt_odd, 1)

                late = None
                for G in range(GROUPS + 1):
                    for half in range(2):
                        if G < GROUPS:
                            exps(G, (2 * half, 2 * half + 1))
                        if half == 0:
                            if G == 0:
                                for h in range(ML_H):
                                    mlstm_hi(h)
                            if G >= 1:
                                copy_odd(G - 1, (0, 1))
                    if G >= 1:
                        j, g = 1 + (G - 1) // 2, (G - 1) % 2
                        copy_odd(G - 1, range(2, j + 1))
                        act.wait_ge(pv_step, TP0[G])
                        if G - 1 >= 2:
                            act.wait_ge(y_done, j - 1)
                        act.activation(olt[g], ps[:, 3, :], ACT.Copy).then_inc(ol_ready, 1)
                        if late is not None:
                            att_hi(late)
                            late = None
                        if g == 1:
                            late = j
                att_hi(NT - 1)

            def att_hi(j):
                act.wait_ge(yt_turned, j)
                act.activation(xh[:, 0:4, START[j]:END[j]], ps[:, 2, :].rearrange("p (c r) -> p c r", c=4),
                               ACT.Copy).then_inc(ya_hi, 1)

            input_hi()
            ffn(0)
            norm(0)
            mixer()
            norm(1)
            ffn(2)
            norm(2)
            for q in range(1, 8, 2):
                half, j = divmod(q, 4)
                act.wait_ge(o_turned, q + 1)
                act.activation(yout[:, j, half * 512:(half + 1) * 512], ps[:, j, :], ACT.Copy).then_inc(o_odd, 1)

        @block.tensor
        def _(pe):
            def split_product(s, col, k, b, first, last, data, p=0, passes=(0, 1, 2)):
                w_h, w_l = whi[:, s, col:col + P], wlo[:, s, col:col + P]
                a_h, a_l = data
                for n, (w, v) in enumerate(((w_h, a_h), (w_l, a_h), (w_h, a_l))):
                    if n in passes:
                        for e, width, mov in moving(v[:, k, :], p):
                            mm = pe.matmul(ps[:, b + e, 0:width], w, mov, start=(first and n == 0), stop=(last and n == 2))
                return mm

            X = (xh, xl)

            def turn(k):
                b = 4 + 2 * (k % 2)
                if k >= 2:
                    pe.wait_ge(x_copied, k - 1)
                if k % 4 == 0:
                    pe.wait_ge(rows_in[k // 4], 16 * NT)
                for j in range(NT):
                    dst = ps[:, b, START[j]:END[j]] if j < 4 else ps[:, b + 1, 0:P]
                    tp = pe.transpose(dst, xin[0:ROWS[j], j, k * P:(k + 1) * P], ident[0:ROWS[j], 0:ROWS[j]])
                tp.then_inc(x_turned, 1)

            def ffn(p):
                s, u0 = F[p], UNIT0[p]
                x_hi, x_ready = (xin_hi, x_split) if p == 0 else (F[1]["hi_done"], F[1]["split_done"])

                def first_unit(ks, ms):
                    for k in ks:
                        for passes, done in (((0, 1), x_hi), ((2,), x_ready)):
                            pe.wait_ge(done, k + 1)
                            for m in ms:
                                mm = split_product(0, m * KT * P + k * P, k, 2 * m, k == 0, k == KT - 1, X, p, passes)
                                if k == KT - 1 and passes == (2,):
                                    mm.then_inc(w_used if m else s["gate_done"], 1)

                if p == 0:
                    pe.wait_ge(const_ready, 2)
                    for k in range(4):
                        turn(k)
                    pe.wait_ge(gate0_lo, 1)
                    first_unit(range(4), (0,))
                    pe.wait_ge(w_lo, 1)
                    first_unit(range(4), (1,))
                    for k in range(4, KT):
                        turn(k)
                        if k >= 6:
                            first_unit((k - 2,), (0, 1))
                    first_unit((KT - 2, KT - 1), (0, 1))
                    pe.wait_ge(x_copied, KT)
                else:
                    pe.wait_ge(w_lo, u0 + 1)
                    first_unit(range(KT), (0, 1))

                def gate_up(f, u, e):
                    pe.wait_ge(w_lo, u + 1)
                    if not isinstance(f, int):
                        pe.wait_ge(s["mul_done"], f - 1)
                    for m in range(2):
                        for k in range(KT):
                            mm = split_product(e, m * KT * P + k * P, k, 4 * e + 2 * m, k == 0, k == KT - 1, X, p)
                        mm.then_inc(w_used if m else s["gate_done"], 1)

                gate_up(1, u0 + 1, 1)
                with pe.Fori(1, FT // 2) as i:
                    for e in range(2):
                        gate_up(2 * i + e, 2 * i + (u0 + e), e)

                def down(m, b, u):
                    for half in range(2):
                        pe.wait_ge(w_lo, u + (half + 1))
                        for k in range(HALF_FT):
                            kk = half * HALF_FT + k
                            if isinstance(m, int) and m == 0 and kk == FT - 1:
                                pe.wait_ge(s["hl_done"], FT)
                            mm = split_product(half, k * P, kk, b, kk == 0, kk == FT - 1, (hh, hl), p)
                        mm.then_inc(w_used, 1)

                pe.wait_ge(s["mul_done"], FT - 1)
                pe.wait_ge(s["hl_done"], FT - 1)
                for m in range(2):
                    down(m, 2 * m, u0 + FT + 2 * m)
                if p == 0:
                    pe.wait_ge(vrows_in, 16 * 8)
                    pe.transpose(ps[:, 7, 0:NV], vrows[:, :], ident[0:NV, 0:NV]).then_inc(vec_turned, 1)
                with pe.Fori(1, KT // 2) as i:
                    for e in range(2):
                        pe.wait_ge(s["z_done"], 2 * i + (e - 1))
                        down(2 * i + e, 2 * e, 4 * i + (u0 + FT + 2 * e))

            def stats(p):
                s = F[p]
                pe.wait_ge(s["sums_done"], KT + 1)
                if p == 0:
                    pe.wait_ge(vec_ready, 1)
                for b, v in ((4, zsum), (6, ssum)):
                    for e, width, mov in moving(v, p):
                        pe.matmul(ps[:, b + e, 0:width], mean_w[:, :], mov, start=True, stop=False)
                for b, v, done in ((4, x[:, KT - 1, :], "z_done"), (6, sil[:, (KT - 1) % 2, :], "sq_done")):
                    pe.wait_ge(s[done], KT)
                    for e, width, mov in moving(v, p):
                        mm = pe.matmul(ps[:, b + e, 0:width], mean_w[:, :], mov, start=False, stop=True)
                    mm.then_inc(s["stats_done"], 1)

            def by_feature(n, use, mc):
                u = MIX0 + n
                for k in range(KT):
                    mm = split_product(u % 2, k * 256 + mc * P, k, 2 * (use % 2), k == 0, k == KT - 1, X)
                mm.then_inc(w_used if use % 2 else half_done, 1)

            def by_token(dst, j, w_h, w_l):
                for k in range(KT):
                    t0 = START[j]
                    v_h, v_l = xh[:, k, t0:t0 + P], xl[:, k, t0:t0 + P]
                    for n, (v, w) in enumerate(((v_h, w_h(k)), (v_l, w_h(k)), (v_h, w_l(k)))):
                        mm = pe.matmul(dst, v, w, start=(k == 0 and n == 0), stop=(k == KT - 1 and n == 2))
                return mm

            def bank_pair_free(use):
                if use >= 2:
                    pe.wait_ge(proj_evac, use - 1)

            def unit(n):
                pe.wait_ge(w_lo, MIX0 + n + 1)
                for c in range(2):
                    bank_pair_free(2 * n + c)
                    by_feature(n, 2 * n + c, c)

            def unit_v(n):
                u = MIX0 + n
                s = u % 2
                pe.wait_ge(w_lo, u + 1)
                for j in range(NT):
                    if j in (0, 4):
                        bank_pair_free(2 * n + j // 4)
                    mm = by_token(ps[:, j // 2, (j % 2) * 256:(j % 2) * 256 + 256], j,
                                  lambda k: whi[:, s, k * 256:(k + 1) * 256], lambda k: wlo[:, s, k * 256:(k + 1) * 256])
                    if j >= 3:
                        mm.then_inc(half_done if j == 3 else w_used, 1)

            def mixer():
                s = MIX0 % 2
                pe.wait_ge(w_lo, MIX0 + 1)
                for k in range(KT):
                    for passes, done in (((0, 1), "hi_done"), ((2,), "split_done")):
                        pe.wait_ge(F[0][done], k + 1)
                        for c in range(2):
                            mm = split_product(s, k * 256 + c * P, k, 2 * c, k == 0, k == KT - 1, X, 0, passes)
                            if k == KT - 1 and passes == (2,):
                                mm.then_inc(w_used if c else half_done, 1)
                unit_v(1)
                pe.wait_ge(w_lo, MIX0 + 3)
                bank_pair_free(4)
                by_feature(2, 4, 0)
                pe.wait_ge(proj_evac, 4)
                for c in range(2):
                    for j in range(NT):
                        b, o = (4 + 2 * c, START[j]) if j < 4 else (5 + 2 * c, 0)
                        c0 = S_KI - 64 * c
                        mm = pe.transpose(ps[:, b, o:o + ROWS[j]], cs[0:ROWS[j], j, c0:c0 + P], ident[0:ROWS[j], 0:ROWS[j]])
                    mm.then_inc(ki_turned, 1)
                pe.wait_ge(ki_ready, 2)
                for k in range(4 * (NT - 1)):
                    j, h = 1 + k // 4, k % 4
                    r0, n = 64 * (h % 2), END[j]
                    if k >= 2:
                        pe.wait_ge(relu_done, k - 1)
                    cols = 1 if n <= 512 else 2
                    for e in range(cols):
                        w = n // cols
                        mm = pe.matmul(ps[0:ROWS[j], 4 + 2 * (k % 2) + e, 0:w], qi[r0:r0 + 64, h // 2, START[j]:END[j]],
                                       qi[r0:r0 + 64, 2, e * w:(e + 1) * w], start=True, stop=True)
                    mm.then_inc(idx_done, 1)
                bank_pair_free(5)
                by_feature(2, 5, 1)
                pe.wait_ge(relu_done, 4 * (NT - 1))
                pe.wait_ge(c_ready, 1)
                for j in range(NT):
                    dst = ps[:, 4, START[j]:END[j]] if j < 4 else ps[:, 5, 0:P]
                    mm = pe.transpose(dst, cmat[0:ROWS[j], j, :], ident[0:ROWS[j], 0:ROWS[j]])
                mm.then_inc(ct_turned, 1)
                pe.wait_ge(gate_act, 1)

                def turn_rows(src, b):
                    for j in range(NT):
                        dst = ps[0:4, b, START[j]:END[j]] if j < 4 else ps[0:4, b + 1, 0:P]
                        mm = pe.transpose(dst, src[0:ROWS[j], j, 0:4], ident[0:ROWS[j], 0:ROWS[j]])
                    mm.then_inc(row_turned, 1)

                turn_rows(gate, 6)
                pe.wait_ge(ct_ready, 1)
                turn_rows(gate2, 4)
                unit(3)
                unit(4)
                unit(5)
                pe.wait_ge(row_ready, 1)
                for j in range(NT):
                    for c, src in ((0, ig_row), (4, b_row)):
                        mm = pe.transpose(ps[:, 6, 8 * j + c:8 * j + c + 4], src[:, START[j]:START[j] + P], ident[0:4, 0:4])
                mm.then_inc(tok_turned, 1)
                unit_v(6)
                unit_v(7)
                pe.wait_ge(pad_ready, 3)
                pe.wait_ge(tok_ready, 1)
                spread(0)
                spread(1)
                unit(8)
                spread(2)
                unit(9)
                mlstm()
                attention()
                for n in range(N_PROJ, MIX_UNITS):
                    for c in range(2):
                        if n > N_PROJ:
                            out_product(n, c, MLSTM_K, True)
                        else:
                            pe.wait_ge(ya_lo, NT - 1)
                        out_product(n, c, ATT_K, False)

            MLSTM_K, ATT_K = (4, 5, 6, 7), (0, 1, 2, 3)

            def out_product(n, c, ks, first):
                m = 2 * (n - N_PROJ) + c
                s = (MIX0 + n) % 2
                if first:
                    pe.wait_ge(w_lo, MIX0 + n + 1)
                    if m >= 2:
                        pe.wait_ge(F[1]["z_done"], m - 1)
                for k in ks:
                    mm = split_product(s, k * 256 + c * P, k, 4 + c, first and k == ks[0], not first and k == ks[-1], X, 1)
                if not first:
                    mm.then_inc(w_used if c else half_done, 1)

            def spread(h):
                if h >= 2:
                    pe.wait_ge(arg_done, 5 * (h - 1))
                pe.matmul(ps[:, 5 + h % 2, :], sel[0:4, h * P:(h + 1) * P], lf_row[:, N_META:T], start=True, stop=True)\
                    .then_inc(nm_spread, 1)

            def mlstm():
                def scores(h):
                    r0 = 64 * (h % 2)
                    for b, parts in enumerate(ST_BANKS):
                        if h >= 1:
                            pe.wait_ge(st_used, 4 * (h - 1) + b + 1)
                        for i, o in parts:
                            mm = pe.matmul(ps[0:ROWS[i], b, o:o + T - QS[i]], qk[r0:r0 + 64, 2 + h // 2, START[i]:END[i]],
                                           qk[r0:r0 + 64, h // 2, QS[i]:T], start=True, stop=True)
                        mm.then_inc(st_done, 1)

                def numerators(h):
                    pe.wait_ge(wt_masked, 4 * (h + 1))
                    for c, b in ((0, 4), (1, 7)):
                        if h >= 1:
                            pe.wait_ge(num_copied, 2 * h - 1 + c)
                        for q in range(2):
                            j = 1 + 2 * c + q
                            for i in range(j + 1):
                                mm = pe.matmul(ps[:, b, q * (ML_DV + 1):(q + 1) * (ML_DV + 1)],
                                               wt(h, i, START[j], END[j]), v1[0:ROWS[i], i, h, :],
                                               start=(i == 0), stop=(i == j))
                        mm.then_inc(num_done, 1)

                spread(3)
                pe.wait_ge(proj_evac, 2 * N_PROJ)
                pe.wait_ge(qk_ready, 4)
                for h in range(ML_H):
                    scores(h)
                    if h >= 1:
                        numerators(h - 1)
                numerators(ML_H - 1)
                pe.wait_ge(num_copied, 2 * ML_H)
                pe.wait_ge(arg_done, 5 * ML_H)
                pe.wait_ge(par_in, 16 * 5)
                for h in range(ATT_H):
                    r0 = 64 * (h % 2)
                    if h >= 4:
                        pe.wait_ge(ql_ready, h - 3)
                    pe.matmul(ps[:, 4 + h % 4, :], wuk[r0:r0 + 64, h // 2, :], qa[r0:r0 + 64, h // 2, N_META:T],
                              start=True, stop=True).then_inc(ql_done, 1)

            def turn_mlstm():
                pe.wait_ge(st_used, 4 * ML_H)
                for h in range(ML_H):
                    pe.wait_ge(hn_ready, 4 * (h + 1))
                    for j in range(4):
                        mm = pe.transpose(ps[:, h, j * P:(j + 1) * P], nums[:, h, j, 0:ML_DV], ident[:, :])
                    mm.then_inc(hn_turned, 1)

            def attention():
                def scores(k):
                    j, h = 1 + k // ATT_H, k % ATT_H
                    n = END[j]
                    if k >= 2:
                        pe.wait_ge(s_masked, k - 1)
                    parts = 1 if n <= 512 else 2
                    w = n // parts
                    for e in range(parts):
                        mm = pe.matmul(ps[:, 4 + 2 * (k % 2) + e, 0:w], ql[:, h, START[j]:END[j]],
                                       ct[:, e * w:(e + 1) * w], start=True, stop=True)
                    mm.then_inc(s_done, 1)

                def turn(G, i):
                    t = TP0[G] + i
                    if i == 0:
                        pe.wait_ge(p_ready, 4 * G + 4)
                    if t >= 2:
                        pe.wait_ge(pt_even if t % 2 == 0 else pt_odd, t // 2)
                    for q in range(4):
                        mm = pe.transpose(ps[0:ROWS[i], t % 2, q * P:(q + 1) * P], pbuf[G % 2][:, q, START[i]:END[i]],
                                          ident[:, :])
                    mm.then_inc(pt_turned, 1)

                def weigh(G, i):
                    t = TP0[G] + i
                    pe.wait_ge(pt_even if t % 2 == 0 else pt_odd, t // 2 + 1)
                    if i == 0 and G >= 1:
                        pe.wait_ge(ol_ready, G)
                    pe.matmul(ps[:, 3, :], cmat[0:ROWS[i], i, :], pt_flat[0:ROWS[i], (t % 2) * 512:(t % 2 + 1) * 512],
                              start=(i == 0), stop=(i == 1 + G // 2)).then_inc(pv_step, 1)

                def project(j):
                    pe.wait_ge(ol_ready, 2 * j)
                    if j >= 2:
                        pe.wait_ge(ya_lo, j - 1)
                    for h in range(ATT_H):
                        mm = pe.matmul(ps[:, 2, h * ATT_D:(h + 1) * ATT_D], olt[h // 4][:, (h % 4) * P:(h % 4 + 1) * P],
                                       wuv[:, h, :], start=True, stop=True)
                    mm.then_inc(y_done, 1)

                def turn_y(j):
                    pe.wait_ge(y_ready, j)
                    for c in range(4):
                        mm = pe.transpose(ps[:, 2, c * P:(c + 1) * P], yatt[:, c * P:(c + 1) * P], ident[:, :])
                    mm.then_inc(yt_turned, 1)

                pe.wait_ge(ql_ready, ATT_H)
                late = None
                for G in range(GROUPS + 1):
                    last_tile = 1 + (G - 1) // 2
                    for half in range(2):
                        if G < GROUPS:
                            for q in (2 * half, 2 * half + 1):
                                scores(4 * G + q)
                        if half == 0:
                            if G == 0:
                                turn_mlstm()
                                pe.wait_ge(yml_ready, ML_H)
                            if late is not None:
                                project(late)
                            if G >= 1:
                                turn(G - 1, 0)
                                turn(G - 1, 1)
                    if G >= 1:
                        for i in range(last_tile + 1):
                            if 2 <= i + 1 <= last_tile:
                                turn(G - 1, i + 1)
                            weigh(G - 1, i)
                        if late is not None:
                            turn_y(late)
                        late = last_tile if (G - 1) % 2 else None
                pe.wait_ge(yml_lo, ML_H)
                pe.wait_ge(s_masked, ATT_H * (NT - 1))
                out_product(N_PROJ, 0, MLSTM_K, True)
                project(late)
                out_product(N_PROJ, 1, MLSTM_K, True)
                turn_y(late)

            ffn(0)
            stats(0)
            mixer()
            stats(1)
            ffn(2)
            stats(2)
            for q in range(8):
                half, j = divmod(q, 4)
                if q >= 4:
                    pe.wait_ge(o_even if q % 2 == 0 else o_odd, (q - 4) // 2 + 1)
                pe.wait_ge(F[2]["aff_done"], 4 * half + 4)
                for c in range(4):
                    k = 4 * half + c
                    mm = pe.transpose(ps[:, j, c * P:(c + 1) * P], x[:, k, START[j + 1]:END[j + 1]], ident[:, :])
                mm.then_inc(o_turned, 1)

        @block.vector
        def _(dve):
            n_dv = [0]

            def link(ins):
                n_dv[0] += 1
                ins.then_inc(dv, 1)
                dve.wait_ge(dv, n_dv[0])

            def lo(u, s, width):
                dve.wait_ge(w_hi, u + 1)
                dve.tensor_tensor(wlo[:, s, 0:width], wraw[:, s, 0:width], whi[:, s, 0:width].bitcast(F32), ALU.subtract)\
                    .then_inc(w_lo, 1)

            def inputs():
                for k in range(KT):
                    b = 4 + 2 * (k % 2)
                    if k % 4 == 0:
                        w = slice(0, HALF_W) if k == 0 else slice(HALF_W, UW)
                        dve.wait_ge(w_hi if k else gate0_hi, 1)
                        dve.tensor_tensor(wlo[:, 0, w], wraw[:, 0, w], whi[:, 0, w].bitcast(F32), ALU.subtract)\
                            .then_inc(w_lo if k else gate0_lo, 1)
                    dve.wait_ge(x_turned, k + 1)
                    dve.tensor_copy(x[:, k, 0:END[3]], ps[:, b, 0:END[3]])
                    dve.tensor_copy(x[:, k, END[3]:T], ps[:, b + 1, 0:P]).then_inc(x_copied, 1)
            def residual(p, m, b, c):
                if p == 1:
                    filled(dve, 2 * N_PROJ + m)
                else:
                    dve.wait_ge(w_used, 2 * m + (UNIT0[p] + FT + 2))
                z = cols(x[:, m, :], p)
                dve.scalar_tensor_tensor(z, bank(b, p), c, z, ALU.mult, ALU.add)\
                    .then_inc(F[p]["z_done"], 1)

            def ffn(p):
                s, u0 = F[p], UNIT0[p]

                def hidden(f, e):
                    dve.wait_ge(w_used, f + (u0 + 1))
                    dve.wait_ge(s["silu_done"], f + 1)
                    dve.tensor_tensor(cols(ht[:, e, :], p), bank(4 * e + 2, p), cols(sil[:, e, :], p), ALU.mult)\
                        .then_inc(s["mul_done"], 1)
                    dve.wait_ge(s["hh_done"], f + 1)
                    dve.tensor_tensor(flat(hl[:, f, :], p), flat(ht[:, e, :], p), flat(hh[:, f, :], p).bitcast(F32), ALU.subtract)\
                        .then_inc(s["hl_done"], 1)

                lo(u0 + 1, 1, UW)
                hidden(0, 0)
                lo(u0 + 2, 0, UW)
                hidden(1, 1)
                with dve.Fori(1, FT // 2 - 1) as i:
                    for e in range(2):
                        lo(2 * i + (u0 + 1 + e), 1 - e, UW)
                        hidden(2 * i + e, e)
                lo(u0 + FT - 1, 1, UW)
                hidden(FT - 2, 0)
                lo(u0 + FT, 0, DOWN_W)
                hidden(FT - 1, 1)
                lo(u0 + FT + 1, 1, DOWN_W)
                lo(u0 + FT + 2, 0, DOWN_W)
                if p == 0:
                    for m in range(2):
                        residual(p, m, 2 * m, 0.5 / ALPHA)
                        lo(2 * m + (u0 + FT + 3), 1, DOWN_W)
                        lo(2 * m + (u0 + FT + 4), 0, DOWN_W)
                    dve.wait_ge(vec_turned, 1)
                    dve.tensor_copy(vec[:, :], ps[:, 7, 0:NV]).then_inc(vec_ready, 1)
                with dve.Fori(1 if p == 0 else 0, KT // 2 - 1) as i:
                    for e in range(2):
                        m = 2 * i + e
                        residual(p, m, 2 * e, 0.5 / ALPHA)
                        lo(2 * m + (u0 + FT + 3), 1, DOWN_W)
                        lo(2 * m + (u0 + FT + 4), 0, DOWN_W)
                residual(p, KT - 2, 0, 0.5 / ALPHA)
                lo(u0 + FT + 15, 1, DOWN_W)
                if p == 0:
                    lo(MIX0, 0, UW)
                residual(p, KT - 1, 2, 0.5 / ALPHA)

            def norm(p):
                s = F[p]
                eps = EPS / ALPHA ** 2

                def centre(k):
                    z = cols(x[:, k, :], p)
                    dve.tensor_tensor(z, z, bank(4, p), ALU.subtract).then_inc(s["sub_done"], 1)

                var = flat(sil[:, 0, :], p)
                dve.wait_ge(s["stats_done"], 2)
                dve.wait_ge(s["mu2_done"], 1)
                dve.tensor_tensor(cols(sil[:, 0, :], p), bank(6, p), cols(sil[:, 0, :], p), ALU.subtract).then_inc(s["var_done"], 1)
                dve.wait_ge(s["var_done"], 1)
                dve.tensor_scalar(var, var, eps, eps, ALU.add, ALU.max).then_inc(s["varc_done"], 1)
                centre(0)
                centre(1)
                dve.wait_ge(s["sd_done"], 1)
                dve.reciprocal(var, flat(sil[:, 1, :], p)).then_inc(s["rstd_done"], 1)
                dve.wait_ge(s["rstd_done"], 1)
                for k in range(KT):
                    if 2 <= k + 1 < KT:
                        centre(k + 1)
                    dve.wait_ge(s["sub_done"], k + 1)
                    dve.tensor_tensor(flat(x[:, k, :], p), flat(x[:, k, :], p), var, ALU.mult).then_inc(s["norm_done"], 1)

            def index_scores():
                dve.wait_ge(proj_evac, 4)
                link(dve.tensor_scalar(wi[:, :, :], cs[:, :, S_WI:S_WI + 4], IDX_SCALE, None, ALU.mult))
                dve.wait_ge(par_in, 16 * 5)
                dve.tensor_tensor(gate[:, :, :], cs[:, :, S_IF:S_IF + 8], bg[:, :].unsqueeze(1).broadcast_to([P, NT, 8]), ALU.add)\
                    .then_inc(gate_in, 1)
                sq = qk_flat[:, 0:NT * LAT].rearrange("p (j c) -> p j c", j=NT)
                link(dve.tensor_tensor(sq, cmat, cmat, ALU.mult))
                link(dve.tensor_reduce(crms[:, 0, :], sq, AX.X, ALU.add))
                dve.tensor_scalar(crms[:, 0, :], crms[:, 0, :], 1.0 / LAT, EPS, ALU.mult, ALU.add).then_inc(c_ms, 1)
                for k in range(4 * (NT - 1)):
                    j, h = 1 + k // 4, k % 4
                    dst = sc[:, SC_OFF[j]:SC_OFF[j] + END[j]]
                    dve.wait_ge(relu_done, k + 1)
                    src = sil[:, k % 2, 0:END[j]]
                    if h == 0:
                        dve.tensor_scalar(dst, src, wi[:, j, 0:1], None, ALU.mult).then_inc(acc_done, 1)
                    else:
                        dve.wait_ge(acc_done, k)
                        dve.scalar_tensor_tensor(dst, src, wi[:, j, h:h + 1], dst, ALU.mult, ALU.add).then_inc(acc_done, 1)
                dve.wait_ge(c_sd, 1)
                link(dve.reciprocal(crms[:, 0, :], crms[:, 1, :]))
                link(dve.tensor_tensor(cmat, cmat, crms[:, 0, :].unsqueeze(2).broadcast_to([P, NT, LAT]), ALU.mult))
                dve.tensor_tensor(cmat, cmat, kvg[:, :].unsqueeze(1).broadcast_to([P, NT, LAT]), ALU.mult).then_inc(c_ready, 1)

            def select(j, r0=0, r1=TOPK // 8):
                w = sc[:, SC_OFF[j]:SC_OFF[j] + END[j]]
                dve.wait_ge(idx_masked, j)
                for r in range(r0, r1):
                    link(dve.max(top8[:, r % 2, :], w))
                    link(dve.match_replace(w, top8[:, r % 2, :], w, TAKEN))
                if r1 == TOPK // 8:
                    dve.tensor_scalar(w, w, (MASKED + TAKEN) / 2, UNPICKED, ALU.is_gt, ALU.mult).then_inc(bias_ready, 1)

            def gate_rows():
                link(dve.memset(m_row, 0.0))

                def fetch(row, b, c):
                    dve.tensor_scalar(row[:, 0:END[3]], ps[0:4, b, 0:END[3]], c, None, ALU.mult)
                    return dve.tensor_scalar(row[:, END[3]:T], ps[0:4, b + 1, 0:P], c, None, ALU.mult)

                dve.wait_ge(row_turned, 1)
                link(fetch(ig_row, 6, SOFTCAP))
                dve.wait_ge(row_turned, 2)
                link(fetch(lf_row, 4, -1.0))
                link(dve.tensor_tensor_scan(b_row, lf_row, m_row, 0.0, ALU.add, ALU.add))
                link(dve.tensor_tensor(ig_row, ig_row, b_row, ALU.subtract))
                link(dve.tensor_tensor_scan(m_row, ig_row, ig_row, -1.0e30, ALU.max, ALU.max))
                link(dve.tensor_scalar(lf_row, m_row, -1.0, None, ALU.mult))
                dve.scalar_tensor_tensor(b_row, b_row, -1.0, m_row, ALU.mult, ALU.subtract).then_inc(row_ready, 1)

            def convolve():
                for c in range(4):
                    dve.wait_ge(proj_evac, 8 + c + 1)
                    for t in range(CONV):
                        tap = vec[:, V_CONV + 4 * t + c:V_CONV + 4 * t + c + 1]
                        src = up[:, c, t:t + T]
                        if t == 0:
                            ins = dve.tensor_scalar(qk[:, c, :], src, tap, None, ALU.mult)
                        else:
                            ins = dve.scalar_tensor_tensor(qk[:, c, :], src, tap, qk[:, c, :], ALU.mult, ALU.add)
                        if t < CONV - 1:
                            link(ins)
                    ins.then_inc(conv_done, 1)

            def arguments(h):
                dve.wait_ge(nm_spread, h + 1)
                if h == 3:
                    dve.wait_ge(num_done, 2)
                for i in range(NT):
                    R = ROWS[i]
                    dve.tensor_scalar(wt(h, i, QS[i], T), ps[0:R, 5 + h % 2, QS[i] - N_META:SEQ], tok[0:R, i, h:h + 1],
                                      0.0, ALU.add, ALU.min).then_inc(arg_done, 1)

            def mlstm():
                def weights(h):
                    for b, parts in enumerate(ST_BANKS):
                        dve.wait_ge(st_done, 4 * h + b + 1)
                        dve.wait_ge(exp_done, 5 * h + (1, 2, 3, 5)[b])
                        for i, o in parts:
                            w = wt(h, i, QS[i], T)
                            ins = dve.scalar_tensor_tensor(w, ps[0:ROWS[i], b, o:o + T - QS[i]], K_SCALE, w, ALU.mult, ALU.mult)
                        ins.then_inc(st_used, 1)

                def head_stats(h):
                    for j in range(4):
                        if j in (0, 2):
                            dve.wait_ge(num_copied, 2 * h + 1 + j // 2)
                        dve.bn_stats(bst[:, h * 4 + j, :], nums[:, h, j, 0:ML_DV]).then_inc(dv, 1)
                        n_dv[0] += 1
                    dve.wait_ge(dv, n_dv[0])
                    for q in range(4 * h, 4 * h + 4):
                        dve.bn_aggr(mv[:, q, :], bst[:, q, :]).then_inc(dv, 1)
                        n_dv[0] += 1

                weights(0)
                weights(1)
                weights(2)
                arguments(3)
                head_stats(0)
                head_stats(1)
                weights(3)
                head_stats(2)
                head_stats(3)
                head_stats(2)
                head_stats(3)
                dve.wait_ge(dv, n_dv[0])
                hj = lambda v: v.rearrange("p (h j) -> p h j", h=ML_H)
                em = tok[:, :, :].rearrange("p j e -> p e j")[:, 4:8, 1:NT]
                den = nums[:, :, :, ML_DV]
                link(dve.scalar_tensor_tensor(hj(mls[:, 0, :]), den, -1.0, den, ALU.mult, ALU.max))
                link(dve.tensor_tensor(hj(mls[:, 0, :]), hj(mls[:, 0, :]), em, ALU.max))
                link(dve.reciprocal(mls[:, 1, :], mls[:, 0, :]))
                link(dve.tensor_tensor(mls[:, 0, :], mls[:, 1, :], mls[:, 1, :], ALU.mult))
                link(dve.tensor_tensor(mls[:, 0, :], mls[:, 0, :], mv[:, :, 1], ALU.mult))
                dve.tensor_scalar(mls[:, 0, :], mls[:, 0, :], EPS, None, ALU.add).then_inc(ml_var, 1)
                dve.wait_ge(ml_sd, 1)
                link(dve.reciprocal(mls[:, 2, :], mls[:, 0, :]))
                link(dve.tensor_tensor(mls[:, 2, :], mls[:, 2, :], mls[:, 1, :], ALU.mult))
                for h in range(ML_H):
                    for j in range(4):
                        q = h * 4 + j
                        v = nums[:, h, j, 0:ML_DV]
                        dve.tensor_scalar(v, v, mv[:, q, 0:1], mls[:, 2, q:q + 1], ALU.subtract, ALU.mult).then_inc(hn_ready, 1)

            def gated_mlstm():
                for h in range(ML_H):
                    dve.wait_ge(hn_turned, h + 1)
                    g = vec[:, V_MLG + h:V_MLG + h + 1]
                    dve.scalar_tensor_tensor(yml[:, h, :], ps[:, h, :], g, sg[:, h, N_META:T], ALU.mult, ALU.mult)\
                        .then_inc(yml_ready, 1)

            def attention():
                def masked(k):
                    j, h = 1 + k // ATT_H, k % ATT_H
                    n = END[j]
                    dve.wait_ge(s_done, k + 1)
                    if k >= 2:
                        dve.wait_ge(p_ready, k - 1)
                    if h == 0:
                        dve.wait_ge(mask_ready, j)
                    dst, msk = (like_keys(v, n) for v in (sil[:, k % 2, 0:n], sc[:, SC_OFF[j]:SC_OFF[j] + n]))
                    dve.tensor_tensor_reduce(dst, keys(P, n, 4 + 2 * (k % 2)), msk, 1.0, -3.0e38, ALU.add, ALU.max,
                                             smax[:, j, h:h + 1]).then_inc(s_masked, 1)
                    dve.wait_ge(s_masked, k + 1)
                    dve.tensor_scalar(nmax[:, j, h:h + 1], smax[:, j, h:h + 1], -ATT_SCALE, None, ALU.mult)\
                        .then_inc(nmax_ready, 1)

                def normalise(j):
                    dve.wait_ge(p_ready, ATT_H * j)
                    link(dve.reciprocal(rinv[:, j, :], rsum[:, j, :]))
                    dve.wait_ge(y_done, j)
                    if j >= 2:
                        dve.wait_ge(yt_turned, j - 1)
                    dve.tensor_tensor(yatt.rearrange("p (h d) -> p h d", h=ATT_H),
                                      ps[:, 2, :].rearrange("p (h d) -> p h d", h=ATT_H),
                                      rinv[:, j, :].unsqueeze(2).broadcast_to([P, ATT_H, ATT_D]), ALU.mult).then_inc(y_ready, 1)

                def att_lo(j):
                    dve.wait_ge(ya_hi, j)
                    dve.tensor_tensor(xl[:, 0:4, START[j]:END[j]], ps[:, 2, :].rearrange("p (c r) -> p c r", c=4),
                                      xh[:, 0:4, START[j]:END[j]].bitcast(F32), ALU.subtract).then_inc(ya_lo, 1)

                late = None
                def copy_even(G, tiles):
                    for i in tiles:
                        t = TP0[G] + i
                        if t % 2 == 0:
                            dve.wait_ge(pt_turned, t + 1)
                            if t >= 2:
                                dve.wait_ge(pv_step, t - 1)
                            dve.tensor_copy(pt_flat[0:ROWS[i], 0:512], ps[0:ROWS[i], 0, :]).then_inc(pt_even, 1)

                for G in range(GROUPS + 1):
                    last_tile = 1 + (G - 1) // 2
                    for half in range(2):
                        if G < GROUPS:
                            for q in (2 * half, 2 * half + 1):
                                masked(4 * G + q)
                        if half == 0:
                            if G == 0:
                                gated_mlstm()
                            if late is not None:
                                normalise(late)
                            if G >= 1:
                                copy_even(G - 1, (0, 1))
                    if G >= 1:
                        copy_even(G - 1, range(2, last_tile + 1))
                        if late is not None:
                            att_lo(late)
                        late = last_tile if (G - 1) % 2 else None
                normalise(late)
                att_lo(late)

            inputs()
            ffn(0)
            norm(0)
            index_scores()
            select(1)
            select(2)
            gate_rows()
            select(3)
            convolve()
            select(4, 0, TOPK // 16)
            dve.wait_ge(tok_ready, 1)
            arguments(0)
            arguments(1)
            select(4, TOPK // 16, TOPK // 8)
            arguments(2)
            mlstm()
            attention()
            for m in range(KT):
                residual(1, m, 4 + m % 2, 1.0 / ALPHA)
                if m in LATE_UNITS:
                    lo(MIX0 + LATE_UNITS[m], LATE_UNITS[m] % 2, UW)
            norm(1)
            ffn(2)
            norm(2)
            for q in range(0, 8, 2):
                half, j = divmod(q, 4)
                dve.wait_ge(o_turned, q + 1)
                dve.tensor_copy(yout[:, j, half * 512:(half + 1) * 512], ps[:, j, :]).then_inc(o_even, 1)


_INS = ["x", "meta_tokens", "ln1_g", "ln1_b", "ffn1_w_gate", "ffn1_w_up", "ffn1_w_down", "w_in", "w_uk", "w_uv",
        "kv_norm_g", "conv_w", "b_igate", "b_fgate", "ml_norm_g", "w_out", "ln2_g", "ln2_b",
        "ffn2_w_gate", "ffn2_w_up", "ffn2_w_down", "ln3_g", "ln3_b"]


def kernel(**inputs):
    import concourse.bacc as _bacc
    from concourse.bass_utils import run_bass_kernel_spmd as _run

    nc = _bacc.Bacc("TRN2", target_bir_lowering=False, num_devices=1)
    arrays, aps = {}, {}
    for name in _INS:
        v = np.ascontiguousarray(inputs[name])
        arrays[f"in_{name}"] = v
        aps[name] = nc.dram_tensor(f"in_{name}", v.shape, mybir.dt.from_np(v.dtype), kind="ExternalInput").ap()
    out = nc.dram_tensor("out_0", (1, SEQ, D), F32, kind="ExternalOutput").ap()
    build(nc, aps, out)
    r = _run(nc, [arrays], core_ids=[0])
    return r.results[0]["out_0"]
```

```python
from contextlib import ExitStack

import numpy as np

import concourse.bass as bass
from concourse import mybir

F32 = mybir.dt.float32
F32R = mybir.dt.float32r
ALU = mybir.AluOpType
ACT = mybir.ActivationFunctionType
AX = mybir.AxisListType

P = 128
D = 1024
KT = D // P
N_META = 16
SEQ = 512
T = N_META + SEQ
HT = T // 2
D_FF = 2816
FT = D_FF // P
ATT_H, ATT_D, LAT = 8, 64, 128
IDX_H = 4
TOPK = min(256, SEQ // 4)
ML_H, ML_DV = 4, 128
CONV = 4
SOFTCAP = 15.0
EPS = 1e-5
ALPHA = 2.0 ** 0.25
IDX_SCALE = IDX_H ** -0.5 * 64 ** -0.5
ATT_SCALE = ATT_D ** -0.5
K_SCALE = 64 ** -0.5

START = [0] + [N_META + P * j for j in range(4)]
ROWS = [N_META] + [P] * 4
NT = len(START)
END = [s + r for s, r in zip(START, ROWS)]

C_QA, C_CKV, C_QI, C_KI, C_WI = 0, 512, 640, 896, 960
C_QK, C_V, C_O, C_IF = 964, 1476, 1988, 2500
S_KI, S_WI, S_IF = 128, 192, 248

UW = 2048
HALF_W = UW // 2
HALF_FT = FT // 2
DOWN_W = HALF_FT * P
FFN_UNITS = FT + 2 * KT
MIX_UNITS = 14
UNIT0 = {0: 0, 2: FFN_UNITS + MIX_UNITS}
MIX0 = FFN_UNITS
N_PROJ = 10
LATE_UNITS = {1: 12, 3: 13, 5: 14}
GROUPS = 2 * (NT - 1)

V_G = [0, 16]
V_B = [8, 24]
V_MLG, V_CONV = 32, 36
NV = V_CONV + CONV * 4

WARM_START, WARM_NORM = 10, 32

MASKED, TAKEN, UNPICKED = -2.0e38, -3.0e38, -1.0e30


def build(nc, a, out):
    ctx = ExitStack()
    with ctx:
        def sb(name, shape, dt=F32, scope=ctx):
            return scope.enter_context(nc.sbuf_tensor(name, shape, dt))

        def sem(name):
            return ctx.enter_context(nc.semaphore(name))

        ps = ctx.enter_context(nc.psum_tensor("ps", [P, 8, 512], F32))

        ST_BANKS = [[(0, 0)], [(1, 0)], [(2, 0)], [(3, 0), (4, T - START[3])]]

        def pair(b):
            return ps[:, b:b + 2, 0:HT]

        x = sb("x", [P, KT, T])
        wraw = sb("wraw", [P, 2, UW])
        whi = sb("whi", [P, 2, UW], F32R)
        wlo = sb("wlo", [P, 2, UW], F32R)
        sil = sb("sil", [P, 2, T])
        ht = sb("ht", [P, 2, T])
        ident = sb("ident", [P, P])
        mean_w = sb("mean_w", [P, P])
        vec = sb("vec", [P, NV])
        vrows = sb("vrows", [NV, P])
        zsum, ssum = ht[:, 0, :], ht[:, 1, :]

        def cols(v, p):
            return halves(v) if p == 0 else v[:, N_META:T]

        def flat(v, p):
            return v if p == 0 else v[:, N_META:T]

        def bank(b, p):
            return pair(b) if p == 0 else ps[:, b, :]

        def moving(v, p):
            if p == 0:
                return [(e, HT, v[:, e * HT:(e + 1) * HT]) for e in range(2)]
            return [(0, SEQ, v[:, N_META:T])]

        def halves(v):
            return v.rearrange("p (b n) -> p b n", b=2)

        split_scope = ExitStack()
        xh = sb("xh", [P, KT, T], F32R, split_scope)
        xl = sb("xl", [P, KT, T], F32R, split_scope)
        with ExitStack() as s:
            xin = sb("xin", [P, NT, D], F32, s)
        with ExitStack() as s:
            hh = sb("hh", [P, FT, T], F32R, s)
            hl = sb("hl", [P, FT, T], F32R, s)
        with ExitStack() as s:
            qi = sb("qi", [P, 4, T], F32, s)
            qa = sb("qa", [P, 4, T], F32, s)
            ql = sb("ql", [P, ATT_H, T], F32, s)
            ct = sb("ct", [P, T], F32, s)
            cs = sb("cs", [P, NT, 256], F32, s)
            wuk = sb("wuk", [P, 4, LAT], F32, s)
            wuv = sb("wuv", [P, ATT_H, ATT_D], F32, s)
            qk = sb("qk", [P, 4, T], F32, s)
            upad = sb("upad", [P, 4 * (T + CONV - 1)], F32, s)
            v1 = sb("v1", [P, NT, ML_H, ML_DV + 1], F32, s)
            sg = sb("sg", [P, 4, T], F32, s)
            sc = sb("sc", [P, sum(END[1:])], F32, s)
            rows = sb("rows", [P, 2, T], F32, s)
            kvg = sb("kvg", [P, LAT], F32, s)
            bg = sb("bg", [P, 8], F32, s)
            wi = sb("wi", [P, NT, IDX_H], F32, s)
            gate = sb("gate", [P, NT, 8], F32, s)
            gate2 = sb("gate2", [P, NT, 4], F32, s)
            tok = sb("tok", [P, NT, 8], F32, s)
            top8 = sb("top8", [P, 2, 8], F32, s)
            crms = sb("crms", [P, 2, NT], F32, s)
            smax = sb("smax", [P, NT, ATT_H], F32, s)
            nmax = sb("nmax", [P, NT, ATT_H], F32, s)
            rsum = sb("rsum", [P, NT, ATT_H], F32, s)
            rinv = sb("rinv", [P, NT, ATT_H], F32, s)
            bst = sb("bst", [P, ML_H * 4, 6], F32, s)
            mv = sb("mv", [P, ML_H * 4, 2], F32, s)
            mls = sb("mls", [P, 3, ML_H * 4], F32, s)
        split_scope.close()
        with ExitStack() as s:
            zrow = sb("zrow", [P, 4, D], F32, s)
            gb = sb("gb", [P, 2, D], F32, s)
        bst3 = sil[:, 0, 0:4 * KT * 6].rearrange("p (j n) -> p j n", j=4)
        mv3 = sil[:, 0, 192:200].rearrange("p (j n) -> p j n", j=4)
        sd3, rstd3 = sil[:, 0, 200:204], sil[:, 0, 204:208]

        SC_OFF = [None] + [sum(END[1:j]) for j in range(1, NT)]
        kit = qi[:, 2, :]
        wt_flat = ql[:, :, :].rearrange("p h t -> p (h t)")
        TP0 = [0]
        for G in range(GROUPS):
            TP0.append(TP0[-1] + G // 2 + 2)
        QS = [max(s_, N_META) for s_ in START]
        WT_OFF = [sum(T - QS[k] for k in range(i)) for i in range(NT)]
        WT_W = sum(T - s_ for s_ in QS)

        def wt(h, i, c0, c1):
            o = (0, WT_W, 0, 0)[h] + WT_OFF[i] - QS[i]
            return (qi_flat if h == 2 else wt_flat)[0:ROWS[i], o + c0:o + c1]

        sel = wt_flat[:, 2 * WT_W:2 * WT_W + 4 * P]
        up = upad[:, :].rearrange("p (c t) -> p c t", c=4)
        nums = upad[:, 0:ML_H * 4 * (ML_DV + 1)].rearrange("p (h j v) -> p h j v", h=ML_H, j=4)
        pbuf = [qi[:, :, :], upad[:, 0:4 * T].rearrange("p (h t) -> p h t", h=4)]
        qi_flat = qi[:, :, :].rearrange("p c t -> p (c t)")
        pt_flat = v1[:, :, :, :].rearrange("p j h v -> p (j h v)")
        qk_flat = qk[:, :, :].rearrange("p c t -> p (c t)")
        olt = [qk_flat[:, g * 512:(g + 1) * 512] for g in range(2)]
        yatt = qk_flat[:, 1024:1536]
        ig_row, lf_row = ht[0:4, 0, :], ht[0:4, 1, :]

        def yml(h):
            return (ht if h < 2 else rows)[:, h % 2, N_META:T]

        b_row, m_row = rows[0:4, 0, :], rows[0:4, 1, :]
        cmat = cs[:, :, 0:LAT]

        x_split = sem("x_split")
        const_ready = sem("const_ready")
        rows_in = [sem(f"rows_in{c}") for c in range(2)]
        vrows_in = sem("vrows_in")
        x_turned = sem("x_turned")
        vec_turned = sem("vec_turned")
        vec_ready = sem("vec_ready")
        x_copied = sem("x_copied")
        xin_hi = sem("xin_hi")
        raw_in = [sem("raw_in0"), sem("raw_in1")]
        gate0_in = sem("gate0_in")
        gate0_hi = sem("gate0_hi")
        gate0_lo = sem("gate0_lo")
        w_hi = sem("w_hi")
        w_lo = sem("w_lo")
        w_used = sem("w_used")
        F = []
        for p in range(3):
            names = ["gate_done", "silu_done", "mul_done", "hh_done", "hl_done"] if p != 1 else []
            names += ["z_done"]
            if p != 2:
                names += ["sq_done", "sums_done", "zsum_done", "stats_done", "mu2_done", "var_done", "varc_done",
                          "sd_done", "rstd_done", "sub_done", "norm_done", "hi_done", "aff_done", "split_done"]
            F.append({n: sem(f"{n}{p}") for n in names})
        half_done = sem("half_done")
        proj_evac = sem("proj_evac")
        par_in = sem("par_in")
        pad_ready = sem("pad_ready")
        idx_done = sem("idx_done")
        relu_done = sem("relu_done")
        acc_done = sem("acc_done")
        idx_masked = sem("idx_masked")
        bias_ready = sem("bias_ready")
        mask_ready = sem("mask_ready")
        dv = sem("dv")
        ac = sem("ac")
        pl = sem("pl")
        c_ms = sem("c_ms")
        c_sd = sem("c_sd")
        c_ready = sem("c_ready")
        ct_turned = sem("ct_turned")
        ct_ready = sem("ct_ready")
        ki_turned = sem("ki_turned")
        ki_ready = sem("ki_ready")
        gate_in = sem("gate_in")
        gate_act = sem("gate_act")
        row_turned = sem("row_turned")
        row_copied = sem("row_copied")
        row_ready = sem("row_ready")
        tok_turned = sem("tok_turned")
        tok_ready = sem("tok_ready")
        conv_done = sem("conv_done")
        qk_ready = sem("qk_ready")
        nm_spread = sem("nm_spread")
        arg_done = sem("arg_done")
        exp_done = sem("exp_done")
        st_done = sem("st_done")
        st_used = sem("st_used")
        wt_masked = sem("wt_masked")
        num_done = sem("num_done")
        num_copied = sem("num_copied")
        ml_var = sem("ml_var")
        ml_sd = sem("ml_sd")
        hn_ready = sem("hn_ready")
        hn_turned = sem("hn_turned")
        yml_ready = sem("yml_ready")
        yml_hi = sem("yml_hi")
        yml_lo = sem("yml_lo")
        ql_done = sem("ql_done")
        ql_ready = sem("ql_ready")
        s_done = sem("s_done")
        s_masked = sem("s_masked")
        nmax_ready = sem("nmax_ready")
        p_ready = sem("p_ready")
        pt_turned = sem("pt_turned")
        pt_even = sem("pt_even")
        pt_odd = sem("pt_odd")
        pv_step = sem("pv_step")
        ol_ready = sem("ol_ready")
        y_done = sem("y_done")
        y_ready = sem("y_ready")
        yt_turned = sem("yt_turned")
        ya_hi = sem("ya_hi")
        ya_lo = sem("ya_lo")
        gb_in = sem("gb_in")
        z_turned = sem("z_turned")
        bst3_done = sem("bst3_done")
        z_copied = sem("z_copied")
        var3_done = sem("var3_done")
        sd3_done = sem("sd3_done")
        centred = sem("centred")
        scaled = sem("scaled")
        out_dve = sem("out_dve")
        out_pool = sem("out_pool")
        stored = sem("stored")

        POOL_HALVES = (1, 3, 5)

        def half_row(v, q):
            return v[:, q // 2, (q % 2) * 512:(q % 2 + 1) * 512]

        block = ctx.enter_context(nc.Block())

        def landed(u, s, late):
            return 16 * u + (32 - 16 * s + (16 if late and s else 0))

        def filled(eng, use):
            if use % 2 == 0:
                eng.wait_ge(half_done, use // 2 + 1)
            else:
                eng.wait_ge(w_used, MIX0 + use // 2 + 1)

        def keys(r, n, b):
            return ps[0:r, b, 0:n] if n <= 512 else ps[0:r, b:b + 2, 0:n // 2]

        def like_keys(v, n):
            return v if n <= 512 else halves(v)

        def kview(w):
            return w[0].rearrange("(k p) n -> p k n", p=P)

        def slot3(t, s, n):
            return t[:, s, 0:(UW // n if n != P else UW // P) * n].rearrange("p (k n) -> p k n", n=n)

        @block.sync
        def _(sp):
            w_in = kview(a["w_in"])
            w_out = kview(a["w_out"])

            def load_inputs(c):
                w = slice(c * (D // 2), (c + 1) * (D // 2))
                sp.dma_start(xin[0:N_META, 0, w], a["meta_tokens"][:, w]).then_inc(rows_in[c], 16)
                sp.dma_start(xin[:, 1:NT, w], a["x"][0].rearrange("(j p) d -> p j d", p=P)[:, :, w]).then_inc(rows_in[c], 16)

            def slot_free(u, first):
                if not first:
                    sp.wait_ge(w_lo, u - 1)

            def load_gate_up(p, s, f, u, first=False):
                slot_free(u, first)
                g, v = kview(a[f"ffn{p // 2 + 1}_w_gate"]), kview(a[f"ffn{p // 2 + 1}_w_up"])
                dst = wraw[:, s, :].rearrange("p (m k n) -> p m k n", m=2, n=P)
                if first and s == 0:
                    load_inputs(0)
                    sp.dma_start(dst[:, 0], g[:, :, bass.ts(f, P)]).then_inc(gate0_in, 16)
                    for k0 in (0, 4):
                        sp.dma_start(dst[:, 1, k0:k0 + 4], v[:, k0:k0 + 4, bass.ts(f, P)]).then_inc(raw_in[s], 16)
                    return
                sp.dma_start(dst[:, 0], g[:, :, bass.ts(f, P)]).then_inc(raw_in[s], 16)
                sp.dma_start(dst[:, 1], v[:, :, bass.ts(f, P)]).then_inc(raw_in[s], 16)

            def load_down(p, half, m, u):
                slot_free(u, False)
                w = kview(a[f"ffn{p // 2 + 1}_w_down"])
                dst = wraw[:, half, 0:DOWN_W].rearrange("p (k n) -> p k n", n=P)
                for k0, k1 in ((0, 6), (6, HALF_FT)):
                    sp.dma_start(dst[:, k0:k1, :],
                                 w[:, half * HALF_FT + k0:half * HALF_FT + k1, bass.ts(m, P)]).then_inc(raw_in[half], 16)

            def ffn(p):
                u0 = UNIT0[p]
                for s in range(2):
                    load_gate_up(p, s, s, u0 + s, first=(p == 0))
                    if p == 0 and s == 0:
                        load_inputs(1)
                if p == 0:
                    load_vectors()
                with sp.Fori(1, FT // 2) as i:
                    for s in range(2):
                        load_gate_up(p, s, 2 * i + s, 2 * i + (u0 + s))
                for half in range(2):
                    load_down(p, half, 0, u0 + FT + half)
                if p == 2:
                    sp.wait_ge(w_used, u0 + FT)
                    sp.dma_start(gb[:, 0, :], a["ln3_g"].broadcast_to([P, D])).then_inc(gb_in, 16)
                    sp.dma_start(gb[:, 1, :], a["ln3_b"].broadcast_to([P, D])).then_inc(gb_in, 16)
                with sp.Fori(1, KT) as m:
                    for half in range(2):
                        load_down(p, half, m, 2 * m + (u0 + FT + half))

            def mixer():
                for n in range(MIX_UNITS):
                    u = MIX0 + n
                    s = u % 2
                    slot_free(u, False)
                    dst = slot3(wraw, s, 256)
                    if n == 1:
                        sp.dma_start(dst[:, :, 0:LAT], w_in[:, :, C_CKV:C_CKV + LAT]).then_inc(raw_in[s], 16)
                        sp.dma_start(dst[:, :, LAT:S_IF], w_in[:, :, C_KI:C_KI + S_IF - LAT]).then_inc(raw_in[s], 16)
                        sp.dma_start(dst[:, :, S_IF:256], w_in[:, :, C_IF:C_IF + 8]).then_inc(raw_in[s], 16)
                        continue
                    if n == 3:
                        load_mixer_params()
                    if n < N_PROJ:
                        c0 = {0: C_QI, 2: C_QA, 3: C_QA + 256, 4: C_QK, 5: C_QK + 256, 6: C_V, 7: C_V + 256,
                              8: C_O, 9: C_O + 256}[n]
                        src = w_in[:, :, c0:c0 + 256]
                    else:
                        src = w_out[:, :, (n - N_PROJ) * 256:(n - N_PROJ + 1) * 256]
                    for k0 in (0, 4):
                        sp.dma_start(dst[:, k0:k0 + 4, :], src[:, k0:k0 + 4, :]).then_inc(raw_in[s], 16)

            def load_mixer_params():
                sp.wait_ge(w_used, FFN_UNITS)
                sp.dma_start(wuk[:, :, :], a["w_uk"][0].rearrange("(q two) d c -> (two d) q c", two=2)).then_inc(par_in, 16)
                sp.dma_start(wuv[:, :, :], a["w_uv"][0].rearrange("h c d -> c h d")).then_inc(par_in, 16)
                sp.dma_start(kvg[:, :], a["kv_norm_g"].broadcast_to([P, LAT])).then_inc(par_in, 16)
                sp.dma_start(bg[:, 0:4], a["b_igate"].broadcast_to([P, 4])).then_inc(par_in, 16)
                sp.dma_start(bg[:, 4:8], a["b_fgate"].broadcast_to([P, 4])).then_inc(par_in, 16)

            def load_vectors():
                r = 0
                for name in ("ln1_g", "ln1_b", "ln2_g", "ln2_b"):
                    sp.dma_start(vrows[r:r + KT, :], a[name].rearrange("o (k p) -> (o k) p", p=P)).then_inc(vrows_in, 16)
                    r += KT
                sp.dma_start(vrows[V_MLG:V_CONV, :], a["ml_norm_g"].rearrange("o (k p) -> (o k) p", p=P)).then_inc(vrows_in, 16)
                sp.dma_start(vrows[V_CONV:NV, :], a["conv_w"].rearrange("o j (c p) -> (o j c) p", p=P)).then_inc(vrows_in, 16)

            ffn(0)
            mixer()
            ffn(2)
            for q in range(8):
                if q in POOL_HALVES:
                    sp.wait_ge(out_pool, POOL_HALVES.index(q) + 1)
                else:
                    sp.wait_ge(out_dve, q + 1 - sum(i < q for i in POOL_HALVES))
                sp.dma_start(out[0, (q // 2) * P:(q // 2 + 1) * P, (q % 2) * 512:(q % 2 + 1) * 512], half_row(zrow, q))\
                    .then_inc(stored, 16)
            sp.wait_ge(stored, 8 * 16)

        @block.gpsimd
        def _(pool):
            n_pl = [0]

            def link(ins):
                n_pl[0] += 1
                ins.then_inc(pl, 1)
                pool.wait_ge(pl, n_pl[0])

            def constants():
                link(pool.memset(ident[:, :], 0.0))
                pool.affine_select(out=ident[:, :], in_=ident[:, :], compare_op=ALU.not_equal, fill=1.0,
                                   base=0, pattern=[[-1, P]], channel_multiplier=1).then_inc(const_ready, 1)
                pool.memset(mean_w[:, :], 1.0 / D).then_inc(const_ready, 1)

            def x_lo(k, hi_sem, n, done, p):
                pool.wait_ge(hi_sem, n)
                pool.tensor_tensor(flat(xl[:, k, :], p), flat(x[:, k, :], p), flat(xh[:, k, :], p).bitcast(F32), ALU.subtract)\
                    .then_inc(done, 1)

            def sums(p):
                s = F[p]
                if p != 1:
                    pool.wait_ge(s["hl_done"], FT)
                else:
                    pool.wait_ge(nm_spread, ML_H)
                    pool.wait_ge(tok_turned, 1)
                    pool.wait_ge(yml_lo, ML_H)
                pool.memset(zsum, 0.0).then_inc(s["sums_done"], 1)
                pool.memset(ssum, 0.0).then_inc(s["sums_done"], 1)
                pool.wait_ge(s["sums_done"], 2)
                zs, ss = flat(zsum, p), flat(ssum, p)

                def add(m, sq_slot, n):
                    pool.wait_ge(s["z_done"], n)
                    pool.tensor_tensor(zs, zs, flat(x[:, m, :], p), ALU.add).then_inc(s["zsum_done"], 1)
                    pool.wait_ge(s["sq_done"], n)
                    pool.tensor_tensor(ss, ss, flat(sil[:, sq_slot, :], p), ALU.add).then_inc(s["sums_done"], 1)
                    pool.wait_ge(s["zsum_done"], n)
                    pool.wait_ge(s["sums_done"], n + 2)

                if p != 1:
                    with pool.Fori(0, KT // 2 - 1) as i:
                        for e in range(2):
                            add(2 * i + e, e, 2 * i + (e + 1))
                    add(KT - 2, 0, KT - 1)
                    return
                for m in range(KT - 1):
                    add(m, m % 2, m + 1)

            def norm_lo(p):
                for k in range(KT):
                    x_lo(k, F[p]["aff_done"], k + 1, F[p]["split_done"], p)

            def mix_lo(n):
                u = MIX0 + n
                pool.wait_ge(w_hi, u + 1)
                pool.tensor_tensor(wlo[:, u % 2, :], wraw[:, u % 2, :], whi[:, u % 2, :].bitcast(F32), ALU.subtract)\
                    .then_inc(w_lo, 1)

            def mixer():
                pool.wait_ge(w_used, FFN_UNITS)
                pool.memset(up[:, :, 0:CONV - 1], 0.0).then_inc(pad_ready, 1)
                link(pool.memset(sel, 0.0))
                pool.affine_select(out=sel.rearrange("p (h n) -> p h n", h=4), in_=sel.rearrange("p (h n) -> p h n", h=4),
                                   compare_op=ALU.not_equal, fill=1.0, base=0, pattern=[[-1, 4], [0, P]],
                                   channel_multiplier=1).then_inc(pad_ready, 1)
                pool.memset(v1[:, :, :, ML_DV:ML_DV + 1], 1.0).then_inc(pad_ready, 1)
                mix_lo(1)
                norm_lo(0)
                mix_lo(2)
                mix_lo(3)
                for j in range(1, NT):
                    pool.wait_ge(acc_done, 4 * j)
                    d = sc[:, SC_OFF[j] + START[j]:SC_OFF[j] + END[j]]
                    pool.affine_select(out=d, in_=d, compare_op=ALU.is_ge, fill=MASKED, base=0,
                                       pattern=[[-1, P]], channel_multiplier=1).then_inc(idx_masked, 1)
                for n in range(4, N_PROJ + 1):
                    mix_lo(n)
                def causal_mask(j):
                    pool.wait_ge(bias_ready, j)
                    d = sc[:, SC_OFF[j] + START[j]:SC_OFF[j] + END[j]]
                    pool.affine_select(out=d, in_=d, compare_op=ALU.is_ge, fill=UNPICKED, base=0,
                                       pattern=[[-1, P]], channel_multiplier=1).then_inc(mask_ready, 1)

                for j in range(1, NT - 1):
                    causal_mask(j)
                mix_lo(N_PROJ + 1)
                for h in range(ML_H):
                    for i in range(1, NT):
                        pool.wait_ge(st_used, 4 * h + min(i, 3) + 1)
                        d = wt(h, i, START[i], END[i])
                        pool.affine_select(out=d, in_=d, compare_op=ALU.is_ge, fill=0.0, base=0,
                                           pattern=[[1, ROWS[i]]], channel_multiplier=-1).then_inc(wt_masked, 1)
                causal_mask(NT - 1)
                for h in range(ML_H):
                    pool.wait_ge(yml_hi, h + 1)
                    pool.tensor_tensor(xl[:, 4 + h, N_META:T], yml(h), xh[:, 4 + h, N_META:T].bitcast(F32),
                                       ALU.subtract)\
                        .then_inc(yml_lo, 1)

            constants()
            for k in range(KT):
                x_lo(k, xin_hi, k + 1, x_split, 0)
            sums(0)
            mixer()
            sums(1)
            mix_lo(MIX_UNITS + 1)
            norm_lo(1)
            for i, q in enumerate(POOL_HALVES):
                pool.wait_ge(scaled, i + 1)
                if i == 0:
                    pool.wait_ge(gb_in, 32)
                pool.tensor_tensor(half_row(zrow, q), half_row(zrow, q), gb[:, 1, 512:1024], ALU.add).then_inc(out_pool, 1)

        @block.scalar
        def _(act):
            n_ac = [0]

            def link(ins):
                n_ac[0] += 1
                ins.then_inc(ac, 1)
                act.wait_ge(ac, n_ac[0])

            def hi(u, s, width, late, first=False):
                act.wait_ge(raw_in[s], landed(u, s, late))
                if not first:
                    act.wait_ge(w_used, u - 1)
                act.activation(whi[:, s, 0:width], wraw[:, s, 0:width], ACT.Copy).then_inc(w_hi, 1)

            def input_hi():
                for k in range(KT):
                    if k == 1:
                        act.wait_ge(gate0_in, 16)
                        act.activation(whi[:, 0, 0:HALF_W], wraw[:, 0, 0:HALF_W], ACT.Copy).then_inc(gate0_hi, 1)
                    if k == KT // 2:
                        act.wait_ge(raw_in[0], 32)
                        act.activation(whi[:, 0, HALF_W:UW], wraw[:, 0, HALF_W:UW], ACT.Copy).then_inc(w_hi, 1)
                    if k == KT - 2:
                        hi(1, 1, UW, False, first=True)
                    act.wait_ge(x_copied, k + 1)
                    act.activation(xh[:, k, :], x[:, k, :], ACT.Copy).then_inc(xin_hi, 1)

            def ffn(p):
                s, u0, late = F[p], UNIT0[p], p > 0

                def hidden(f, e, first):
                    act.wait_ge(s["gate_done"], f + 1)
                    if not first:
                        act.wait_ge(s["mul_done"], f - 1)
                    act.activation(cols(sil[:, e, :], p), bank(4 * e, p), ACT.Silu).then_inc(s["silu_done"], 1)
                    act.wait_ge(s["mul_done"], f + 1)
                    act.activation(flat(hh[:, f, :], p), flat(ht[:, e, :], p), ACT.Copy).then_inc(s["hh_done"], 1)

                hidden(0, 0, True)
                hi(u0 + 2, 0, UW, late)
                hidden(1, 1, True)
                with act.Fori(1, FT // 2 - 1) as i:
                    for e in range(2):
                        hi(2 * i + (u0 + 1 + e), 1 - e, UW, late)
                        hidden(2 * i + e, e, False)
                hi(u0 + FT - 1, 1, UW, late)
                hidden(FT - 2, 0, False)
                hi(u0 + FT, 0, DOWN_W, late)
                hidden(FT - 1, 1, False)
                hi(u0 + FT + 1, 1, DOWN_W, late)
                hi(u0 + FT + 2, 0, DOWN_W, late)
                with act.Fori(0, KT // 2 - 1) as i:
                    for e in range(2):
                        m = 2 * i + e
                        if p == 0:
                            square(p, m, e)
                        hi(2 * m + (u0 + FT + 3), 1, DOWN_W, late)
                        hi(2 * m + (u0 + FT + 4), 0, DOWN_W, late)
                        if p == 2:
                            copy_rows(m, e)
                if p == 0:
                    square(p, KT - 2, 0)
                hi(u0 + FT + 15, 1, DOWN_W, late)
                if p == 0:
                    hi(MIX0, 0, UW, late)
                    square(p, KT - 1, 1)
                    hi(MIX0 + 1, 1, UW, True)
                else:
                    copy_rows(KT - 2, 0)
                    copy_rows(KT - 1, 1)

            def copy_rows(m, e):
                act.wait_ge(z_turned, m + 1)
                act.activation(zrow[:, :, bass.ts(m, P)], ps[:, 4 + e, :].rearrange("p (j c) -> p j c", j=4), ACT.Copy)\
                    .then_inc(z_copied, 1)

            def square(p, m, e):
                s = F[p]
                act.wait_ge(s["z_done"], m + 1)
                act.wait_ge(s["sums_done"], m + 1)
                act.activation(flat(sil[:, e, :], p), flat(x[:, m, :], p), ACT.Square).then_inc(s["sq_done"], 1)

            def norm(p):
                s = F[p]
                act.wait_ge(s["stats_done"], 1)
                act.activation(cols(sil[:, 0, :], p), bank(4, p), ACT.Square).then_inc(s["mu2_done"], 1)
                act.wait_ge(s["varc_done"], 1)
                act.activation(flat(sil[:, 1, :], p), flat(sil[:, 0, :], p), ACT.Sqrt).then_inc(s["sd_done"], 1)
                for k in range(KT):
                    act.wait_ge(s["norm_done"], k + 1)
                    if k == 0:
                        act.wait_ge(vec_ready, 1)
                    g, b = vec[:, V_G[p] + k:V_G[p] + k + 1], vec[:, V_B[p] + k:V_B[p] + k + 1]
                    xk = flat(x[:, k, :], p)
                    act.activation(flat(xh[:, k, :], p), xk, ACT.Identity, bias=b, scale=g).then_inc(s["hi_done"], 1)
                    act.activation(xk, xk, ACT.Identity, bias=b, scale=g).then_inc(s["aff_done"], 1)

            def proj_out(n, src, dst, func=ACT.Copy):
                filled(act, n)
                act.activation(dst, src, func).then_inc(proj_evac, 1)

            def mixer():
                for c in range(2):
                    proj_out(c, ps[:, 2 * c, :], qi[:, c, N_META:T])
                hi(MIX0 + 2, 0, UW, False)
                for n, (j0, j1) in ((2, (0, 4)), (3, (4, 5))):
                    filled(act, n)
                    src = ps[:, 0:2, :] if n == 2 else ps[:, 2, 0:256]
                    dst = cs[:, j0:j1, :].rearrange("p j n -> p (j n)")
                    act.activation(halves(dst) if n == 2 else dst, src, ACT.Copy).then_inc(proj_evac, 1)
                hi(MIX0 + 3, 1, UW, True)
                act.wait_ge(c_ms, 1)
                act.activation(crms[:, 1, :], crms[:, 0, :], ACT.Sqrt).then_inc(c_sd, 1)
                for c in range(2):
                    act.wait_ge(ki_turned, c + 1)
                    r = slice(64 * c, 64 * c + 64)
                    act.activation(kit[r, 0:END[3]], ps[r, 4 + 2 * c, 0:END[3]], ACT.Copy)
                    act.activation(kit[r, END[3]:T], ps[r, 5 + 2 * c, 0:P], ACT.Copy).then_inc(ki_ready, 1)
                proj_out(4, ps[:, 0, :], qa[:, 0, N_META:T])
                for k in range(4 * (NT - 1)):
                    j = 1 + k // 4
                    act.wait_ge(idx_done, k + 1)
                    if k >= 2:
                        act.wait_ge(acc_done, k - 1)
                    src = keys(ROWS[j], END[j], 4 + 2 * (k % 2))
                    dst = like_keys(sil[0:ROWS[j], k % 2, 0:END[j]], END[j])
                    act.activation(dst, src, ACT.Relu).then_inc(relu_done, 1)
                act.wait_ge(gate_in, 1)
                link(act.activation(gate[:, :, :], gate[:, :, :], ACT.Tanh, scale=1.0 / SOFTCAP))
                link(act.activation(gate2[:, :, :], gate[:, :, 4:8], ACT.Exp, scale=-SOFTCAP))
                act.activation(gate2[:, :, :], gate2[:, :, :], ACT.Ln, bias=1.0).then_inc(gate_act, 1)
                proj_out(5, ps[:, 2, :], qa[:, 1, N_META:T])
                act.wait_ge(ct_turned, 1)
                act.activation(ct[:, 0:END[3]], ps[:, 4, 0:END[3]], ACT.Copy)
                act.activation(ct[:, END[3]:T], ps[:, 5, 0:P], ACT.Copy).then_inc(ct_ready, 1)
                hi(MIX0 + 4, 0, UW, False)
                for c in range(2):
                    proj_out(6 + c, ps[:, 2 * c, :], qa[:, 2 + c, N_META:T])
                hi(MIX0 + 5, 1, UW, True)
                act.wait_ge(pad_ready, 1)
                for n in (4, 5):
                    for c in range(2):
                        proj_out(2 * n + c, pair(2 * c), halves(up[:, 2 * (n - 4) + c, CONV - 1:CONV - 1 + T]))
                    hi(MIX0 + n + 2, n % 2, UW, True)
                act.wait_ge(tok_turned, 1)
                tt = ps[:, 6, 0:NT * 8].rearrange("p (j e) -> p j e", e=8)
                act.activation(tok[:, :, 0:4], tt[:, :, 0:4], ACT.Copy)
                act.activation(tok[:, :, 4:8], tt[:, :, 4:8], ACT.Exp).then_inc(tok_ready, 1)
                for n in (6, 7):
                    h0 = 2 * (n - 6)
                    proj_out(2 * n, ps[:, 0:2, :].rearrange("p b (j h v) -> p (b j) h v", j=2, h=2),
                             v1[:, 0:4, h0:h0 + 2, 0:ML_DV])
                    proj_out(2 * n + 1, ps[:, 2, 0:256].rearrange("p (h v) -> p h v", h=2),
                             v1[:, 4, h0:h0 + 2, 0:ML_DV])
                    hi(MIX0 + n + 2, n % 2, UW, True)
                for c in range(4):
                    act.wait_ge(conv_done, c + 1)
                    act.activation(qk[:, c, :], qk[:, c, :], ACT.Silu).then_inc(qk_ready, 1)
                def exps(h):
                    for i in range(NT):
                        act.wait_ge(arg_done, 5 * h + i + 1)
                        w = wt(h, i, QS[i], T)
                        act.activation(w, w, ACT.Exp).then_inc(exp_done, 1)

                for n in (8, 9):
                    for c in range(2):
                        proj_out(2 * n + c, ps[:, 2 * c, :], sg[:, 2 * (n - 8) + c, N_META:T], ACT.Sigmoid)
                    hi(MIX0 + n + 2, n % 2, UW, True)
                    if n == 8:
                        exps(0)
                        exps(1)
                exps(2)
                def copy_num(h):
                    for c, b in ((0, 4), (1, 7)):
                        act.wait_ge(num_done, 2 * h + c + 1)
                        act.activation(nums[:, h, 2 * c:2 * c + 2, :],
                                       ps[:, b, 0:2 * (ML_DV + 1)].rearrange("p (j v) -> p j v", j=2),
                                       ACT.Copy).then_inc(num_copied, 1)

                copy_num(0)
                exps(3)
                for h in range(1, ML_H):
                    copy_num(h)
                for h in range(ATT_H):
                    if h == 2:
                        act.wait_ge(ml_var, 1)
                        act.activation(mls[:, 0, :], mls[:, 0, :], ACT.Sqrt).then_inc(ml_sd, 1)
                    act.wait_ge(ql_done, h + 1)
                    act.activation(ql[:, h, N_META:T], ps[:, 4 + h % 4, :], ACT.Copy).then_inc(ql_ready, 1)
                attention()
                for m in range(KT):
                    square(1, m, m % 2)
                    if m in LATE_UNITS:
                        hi(MIX0 + LATE_UNITS[m], LATE_UNITS[m] % 2, UW, True)
                hi(UNIT0[2] + 1, 1, UW, True)

            def mlstm_hi(h):
                act.wait_ge(yml_ready, h + 1)
                act.activation(xh[:, 4 + h, N_META:T], yml(h), ACT.Copy).then_inc(yml_hi, 1)

            def attention():
                def exps(G, qs):
                    j, g = 1 + G // 2, G % 2
                    n = END[j]
                    for q in qs:
                        k = 4 * G + q
                        h = 4 * g + q
                        act.wait_ge(nmax_ready, k + 1)
                        if q == 0 and G >= 2:
                            act.wait_ge(pt_turned, TP0[G - 1])
                        if q == 0 and G == 1:
                            act.wait_ge(hn_turned, ML_H)
                        act.activation(pbuf[G % 2][:, q, 0:n], sil[:, k % 2, 0:n], ACT.Exp,
                                       bias=nmax[:, j, h:h + 1], scale=ATT_SCALE,
                                       accum_out=rsum[:, j, h:h + 1]).then_inc(p_ready, 1)

                def copy_odd(G, tiles):
                    for i in tiles:
                        t = TP0[G] + i
                        if t % 2 == 1:
                            act.wait_ge(pt_turned, t + 1)
                            if t >= 2:
                                act.wait_ge(pv_step, t - 1)
                            act.activation(pt_flat[0:ROWS[i], 512:1024], ps[0:ROWS[i], 1, :], ACT.Copy)\
                                .then_inc(pt_odd, 1)

                late = None
                for G in range(GROUPS + 1):
                    for half in range(2):
                        if G < GROUPS:
                            exps(G, (2 * half, 2 * half + 1))
                        if half == 0:
                            if G >= 1:
                                copy_odd(G - 1, (0, 1))
                        if (G, half) in ((0, 1), (1, 0)):
                            for h in (2 * G, 2 * G + 1):
                                mlstm_hi(h)
                    if G >= 1:
                        j, g = 1 + (G - 1) // 2, (G - 1) % 2
                        copy_odd(G - 1, range(2, j + 1))
                        act.wait_ge(pv_step, TP0[G])
                        if G - 1 >= 2:
                            act.wait_ge(y_done, j - 1)
                        act.activation(olt[g], ps[:, 3, :], ACT.Copy).then_inc(ol_ready, 1)
                        if late is not None:
                            att_hi(late)
                            late = None
                        if g == 1:
                            late = j
                att_hi(NT - 1)

            def att_hi(j):
                act.wait_ge(yt_turned, j)
                act.activation(xh[:, 0:4, START[j]:END[j]], ps[:, 2, :].rearrange("p (c r) -> p c r", c=4),
                               ACT.Copy).then_inc(ya_hi, 1)

            input_hi()
            ffn(0)
            norm(0)
            mixer()
            norm(1)
            ffn(2)
            act.wait_ge(var3_done, 1)
            act.activation(sd3, mv3[:, :, 1], ACT.Sqrt).then_inc(sd3_done, 1)
            for i, q in enumerate(POOL_HALVES):
                act.wait_ge(centred, q + 1)
                act.activation(half_row(zrow, q), half_row(zrow, q), ACT.Copy, scale=rstd3[:, q // 2:q // 2 + 1])\
                    .then_inc(scaled, 1)

        @block.tensor
        def _(pe):
            def split_product(s, col, k, b, first, last, data, p=0, passes=(0, 1, 2)):
                w_h, w_l = whi[:, s, col:col + P], wlo[:, s, col:col + P]
                a_h, a_l = data
                for n, (w, v) in enumerate(((w_h, a_h), (w_l, a_h), (w_h, a_l))):
                    if n in passes:
                        for e, width, mov in moving(v[:, k, :], p):
                            mm = pe.matmul(ps[:, b + e, 0:width], w, mov, start=(first and n == 0), stop=(last and n == 2))
                return mm

            X = (xh, xl)

            def turn(k):
                b = 4 + 2 * (k % 2)
                if k >= 2:
                    pe.wait_ge(x_copied, k - 1)
                if k % 4 == 0:
                    pe.wait_ge(rows_in[k // 4], 16 * 2)
                for j in range(NT):
                    dst = ps[:, b, START[j]:END[j]] if j < 4 else ps[:, b + 1, 0:P]
                    tp = pe.transpose(dst, xin[0:ROWS[j], j, k * P:(k + 1) * P], ident[0:ROWS[j], 0:ROWS[j]])
                tp.then_inc(x_turned, 1)

            def ffn(p):
                s, u0 = F[p], UNIT0[p]
                x_hi, x_ready = (xin_hi, x_split) if p == 0 else (F[1]["hi_done"], F[1]["split_done"])

                def first_unit(ks, ms):
                    for k in ks:
                        for passes, done in (((0, 1), x_hi), ((2,), x_ready)):
                            pe.wait_ge(done, k + 1)
                            for m in ms:
                                mm = split_product(0, m * KT * P + k * P, k, 2 * m, k == 0, k == KT - 1, X, p, passes)
                                if k == KT - 1 and passes == (2,):
                                    mm.then_inc(w_used if m else s["gate_done"], 1)

                if p == 0:
                    pe.wait_ge(const_ready, 2)
                    keep_warm(WARM_START)
                    for k in range(4):
                        turn(k)
                    pe.wait_ge(gate0_lo, 1)
                    first_unit(range(4), (0,))
                    pe.wait_ge(w_lo, 1)
                    first_unit((0, 1), (1,))
                    turn(4)
                    first_unit((2,), (1,))
                    turn(5)
                    first_unit((3,), (1,))
                    turn(6)
                    first_unit((4,), (0, 1))
                    turn(7)
                    first_unit((5, 6, 7), (0, 1))
                    pe.wait_ge(x_copied, KT)
                else:
                    pe.wait_ge(w_lo, u0 + 1)
                    first_unit(range(KT), (0, 1))

                def gate_up(f, u, e):
                    pe.wait_ge(w_lo, u + 1)
                    if not isinstance(f, int):
                        pe.wait_ge(s["mul_done"], f - 1)
                    for m in range(2):
                        for k in range(KT):
                            mm = split_product(e, m * KT * P + k * P, k, 4 * e + 2 * m, k == 0, k == KT - 1, X, p)
                        mm.then_inc(w_used if m else s["gate_done"], 1)

                gate_up(1, u0 + 1, 1)
                with pe.Fori(1, FT // 2) as i:
                    for e in range(2):
                        gate_up(2 * i + e, 2 * i + (u0 + e), e)

                def down(m, b, u):
                    for half in range(2):
                        pe.wait_ge(w_lo, u + (half + 1))
                        for k in range(HALF_FT):
                            kk = half * HALF_FT + k
                            if isinstance(m, int) and m == 0 and kk == FT - 1:
                                pe.wait_ge(s["hl_done"], FT)
                            mm = split_product(half, k * P, kk, b, kk == 0, kk == FT - 1, (hh, hl), p)
                        mm.then_inc(w_used, 1)
                        if p == 2 and half == 0 and not (isinstance(m, int) and m == 0):
                            turn_z(m - 1, 5 - b // 2, m)

                def turn_z(m, b, n):
                    pe.wait_ge(s["z_done"], n)
                    if not (isinstance(m, int) and m == 0):
                        pe.wait_ge(z_copied, m)
                    for j in range(4):
                        mm = pe.transpose(ps[:, b, j * P:(j + 1) * P], ht[:, b - 4, START[j + 1]:END[j + 1]], ident[:, :])
                    mm.then_inc(z_turned, 1)

                pe.wait_ge(s["mul_done"], FT - 1)
                pe.wait_ge(s["hl_done"], FT - 1)
                for m in range(2):
                    down(m, 2 * m, u0 + FT + 2 * m)
                if p == 0:
                    pe.wait_ge(vrows_in, 16 * 6)
                    pe.transpose(ps[:, 7, 0:NV], vrows[:, :], ident[0:NV, 0:NV]).then_inc(vec_turned, 1)
                with pe.Fori(1, KT // 2) as i:
                    for e in range(2):
                        pe.wait_ge(s["z_done"], 2 * i + (e - 1))
                        down(2 * i + e, 2 * e, 4 * i + (u0 + FT + 2 * e))
                if p == 2:
                    turn_z(KT - 1, 5, KT)

            def keep_warm(n):
                for _ in range(n):
                    pe.matmul(ps[:, 0, 0:P], mean_w[:, :], mean_w[:, :], start=True, stop=True)

            def stats(p):
                s = F[p]
                pe.wait_ge(s["sums_done"], KT + 1)
                if p == 0:
                    pe.wait_ge(vec_ready, 1)
                for b, v in ((4, zsum), (6, ssum)):
                    for e, width, mov in moving(v, p):
                        pe.matmul(ps[:, b + e, 0:width], mean_w[:, :], mov, start=True, stop=False)
                for b, v, done in ((4, x[:, KT - 1, :], "z_done"), (6, sil[:, (KT - 1) % 2, :], "sq_done")):
                    pe.wait_ge(s[done], KT)
                    for e, width, mov in moving(v, p):
                        mm = pe.matmul(ps[:, b + e, 0:width], mean_w[:, :], mov, start=False, stop=True)
                    mm.then_inc(s["stats_done"], 1)

            def by_feature(n, use, mc, p=0):
                u = MIX0 + n
                for k in range(KT):
                    mm = split_product(u % 2, k * 256 + mc * P, k, 2 * (use % 2), k == 0, k == KT - 1, X, p)
                mm.then_inc(w_used if use % 2 else half_done, 1)

            def by_token(dst, j, w_h, w_l):
                for k in range(KT):
                    t0 = START[j]
                    v_h, v_l = xh[:, k, t0:t0 + P], xl[:, k, t0:t0 + P]
                    for n, (v, w) in enumerate(((v_h, w_h(k)), (v_l, w_h(k)), (v_h, w_l(k)))):
                        mm = pe.matmul(dst, v, w, start=(k == 0 and n == 0), stop=(k == KT - 1 and n == 2))
                return mm

            def bank_pair_free(use):
                if use >= 2:
                    pe.wait_ge(proj_evac, use - 1)

            def unit(n, p=0):
                pe.wait_ge(w_lo, MIX0 + n + 1)
                for c in range(2):
                    bank_pair_free(2 * n + c)
                    by_feature(n, 2 * n + c, c, p)

            def unit_v(n):
                u = MIX0 + n
                s = u % 2
                pe.wait_ge(w_lo, u + 1)
                for j in range(NT):
                    if j in (0, 4):
                        bank_pair_free(2 * n + j // 4)
                    mm = by_token(ps[:, j // 2, (j % 2) * 256:(j % 2) * 256 + 256], j,
                                  lambda k: whi[:, s, k * 256:(k + 1) * 256], lambda k: wlo[:, s, k * 256:(k + 1) * 256])
                    if j >= 3:
                        mm.then_inc(half_done if j == 3 else w_used, 1)

            def mixer():
                s = MIX0 % 2
                pe.wait_ge(w_lo, MIX0 + 1)
                for k in range(KT):
                    for passes, done in (((0, 1), "hi_done"), ((2,), "split_done")):
                        pe.wait_ge(F[0][done], k + 1)
                        for c in range(2):
                            mm = split_product(s, k * 256 + c * P, k, 2 * c, k == 0, k == KT - 1, X, 1, passes)
                            if k == KT - 1 and passes == (2,):
                                mm.then_inc(w_used if c else half_done, 1)
                unit_v(1)
                pe.wait_ge(w_lo, MIX0 + 3)
                bank_pair_free(4)
                q_a0 = lambda k: split_product((MIX0 + 2) % 2, k * 256, k, 0, k == 0, k == KT - 1, X, 1)
                for k in range(4):
                    q_a0(k)
                pe.wait_ge(proj_evac, 4)
                for c in range(2):
                    for j in range(NT):
                        b, o = (4 + 2 * c, START[j]) if j < 4 else (5 + 2 * c, 0)
                        c0 = S_KI - 64 * c
                        mm = pe.transpose(ps[:, b, o:o + ROWS[j]], cs[0:ROWS[j], j, c0:c0 + P], ident[0:ROWS[j], 0:ROWS[j]])
                    mm.then_inc(ki_turned, 1)
                for k in range(4, KT):
                    mm = q_a0(k)
                mm.then_inc(half_done, 1)
                pe.wait_ge(ki_ready, 2)
                bank_pair_free(5)
                for k in range(4 * (NT - 1)):
                    j, h = 1 + k // 4, k % 4
                    r0, n = 64 * (h % 2), END[j]
                    if k >= 2:
                        pe.wait_ge(relu_done, k - 1)
                    cols = 1 if n <= 512 else 2
                    for e in range(cols):
                        w = n // cols
                        mm = pe.matmul(ps[0:ROWS[j], 4 + 2 * (k % 2) + e, 0:w], qi[r0:r0 + 64, h // 2, START[j]:END[j]],
                                       qi[r0:r0 + 64, 2, e * w:(e + 1) * w], start=True, stop=True)
                    mm.then_inc(idx_done, 1)
                    if k % 2 == 1:
                        kk = k // 2
                        mm = split_product((MIX0 + 2) % 2, kk * 256 + P, kk, 2, kk == 0, kk == KT - 1, X, 1)
                mm.then_inc(w_used, 1)
                pe.wait_ge(w_lo, MIX0 + 4)
                bank_pair_free(6)
                by_feature(3, 6, 0, 1)
                pe.wait_ge(relu_done, 4 * (NT - 1))
                pe.wait_ge(c_ready, 1)
                for j in range(NT):
                    dst = ps[:, 4, START[j]:END[j]] if j < 4 else ps[:, 5, 0:P]
                    mm = pe.transpose(dst, cmat[0:ROWS[j], j, :], ident[0:ROWS[j], 0:ROWS[j]])
                mm.then_inc(ct_turned, 1)
                pe.wait_ge(gate_act, 1)

                def turn_rows(src, b):
                    for j in range(NT):
                        dst = ps[0:4, b, START[j]:END[j]] if j < 4 else ps[0:4, b + 1, 0:P]
                        mm = pe.transpose(dst, src[0:ROWS[j], j, 0:4], ident[0:ROWS[j], 0:ROWS[j]])
                    mm.then_inc(row_turned, 1)

                turn_rows(gate, 6)
                pe.wait_ge(ct_ready, 1)
                turn_rows(gate2, 4)
                bank_pair_free(7)
                by_feature(3, 7, 1, 1)
                unit(4)
                unit(5)
                pe.wait_ge(row_ready, 1)
                for j in range(NT):
                    for c, src in ((0, ig_row), (4, b_row)):
                        mm = pe.transpose(ps[:, 6, 8 * j + c:8 * j + c + 4], src[:, START[j]:START[j] + P], ident[0:4, 0:4])
                mm.then_inc(tok_turned, 1)
                unit_v(6)
                unit_v(7)
                pe.wait_ge(pad_ready, 3)
                pe.wait_ge(tok_ready, 1)
                spread(0)
                spread(1)
                unit(8, 1)
                pe.wait_ge(w_lo, MIX0 + 10)
                bank_pair_free(18)
                by_feature(9, 18, 0, 1)
                spread(2)
                bank_pair_free(19)
                by_feature(9, 19, 1, 1)
                mlstm()
                attention()
                for n in range(N_PROJ, MIX_UNITS):
                    for c in range(2):
                        if (n, c) > (N_PROJ + 1, 0):
                            out_product(n, c, MLSTM_K, True)
                        if (n, c) == (N_PROJ, 0):
                            pe.wait_ge(ya_lo, NT - 1)
                        out_product(n, c, ATT_K, False)

            MLSTM_K, ATT_K = (4, 5, 6, 7), (0, 1, 2, 3)

            def out_product(n, c, ks, first):
                m = 2 * (n - N_PROJ) + c
                s = (MIX0 + n) % 2
                if first:
                    pe.wait_ge(w_lo, MIX0 + n + 1)
                    if m >= 4:
                        pe.wait_ge(F[1]["z_done"], m - 3)
                for k in ks:
                    mm = split_product(s, k * 256 + c * P, k, 4 + m % 4, first and k == ks[0], not first and k == ks[-1], X, 1)
                if not first:
                    mm.then_inc(w_used if c else half_done, 1)

            def spread(h):
                if h >= 2:
                    pe.wait_ge(arg_done, 5 * (h - 1))
                pe.matmul(ps[:, 5 + h % 2, :], sel[0:4, h * P:(h + 1) * P], lf_row[:, N_META:T], start=True, stop=True)\
                    .then_inc(nm_spread, 1)

            def mlstm():
                def scores(h):
                    r0 = 64 * (h % 2)
                    for b, parts in enumerate(ST_BANKS):
                        if h >= 1:
                            pe.wait_ge(st_used, 4 * (h - 1) + b + 1)
                        for i, o in parts:
                            mm = pe.matmul(ps[0:ROWS[i], b, o:o + T - QS[i]], qk[r0:r0 + 64, 2 + h // 2, START[i]:END[i]],
                                           qk[r0:r0 + 64, h // 2, QS[i]:T], start=True, stop=True)
                        mm.then_inc(st_done, 1)

                def numerators(h):
                    pe.wait_ge(wt_masked, 4 * (h + 1))
                    for c, b in ((0, 4), (1, 7)):
                        if h >= 1:
                            pe.wait_ge(num_copied, 2 * h - 1 + c)
                        for q in range(2):
                            j = 1 + 2 * c + q
                            for i in range(j + 1):
                                mm = pe.matmul(ps[:, b, q * (ML_DV + 1):(q + 1) * (ML_DV + 1)],
                                               wt(h, i, START[j], END[j]), v1[0:ROWS[i], i, h, :],
                                               start=(i == 0), stop=(i == j))
                        mm.then_inc(num_done, 1)

                spread(3)
                pe.wait_ge(proj_evac, 2 * N_PROJ)
                pe.wait_ge(qk_ready, 4)
                for h in range(ML_H):
                    scores(h)
                    if h >= 1:
                        numerators(h - 1)
                numerators(ML_H - 1)
                pe.wait_ge(arg_done, 5 * ML_H)
                pe.wait_ge(par_in, 16 * 5)
                for h in range(ATT_H):
                    r0 = 64 * (h % 2)
                    if h in (0, 3):
                        pe.wait_ge(num_copied, 2 * ML_H - (h == 0))
                    if h >= 4:
                        pe.wait_ge(ql_ready, h - 3)
                    pe.matmul(ps[:, 4 + h % 4, :], wuk[r0:r0 + 64, h // 2, :], qa[r0:r0 + 64, h // 2, N_META:T],
                              start=True, stop=True).then_inc(ql_done, 1)

            def turn_mlstm():
                pe.wait_ge(st_used, 4 * ML_H)
                for h in range(ML_H):
                    pe.wait_ge(hn_ready, h + 1)
                    for j in range(4):
                        mm = pe.transpose(ps[:, h, j * P:(j + 1) * P], nums[:, h, j, 0:ML_DV], ident[:, :])
                    mm.then_inc(hn_turned, 1)

            def attention():
                def scores(k):
                    j, h = 1 + k // ATT_H, k % ATT_H
                    n = END[j]
                    if k < 3:
                        pe.wait_ge(ql_ready, (5, 7, ATT_H)[k])
                    if k >= 2:
                        pe.wait_ge(s_masked, k - 1)
                    parts = 1 if n <= 512 else 2
                    w = n // parts
                    for e in range(parts):
                        mm = pe.matmul(ps[:, 4 + 2 * (k % 2) + e, 0:w], ql[:, h, START[j]:END[j]],
                                       ct[:, e * w:(e + 1) * w], start=True, stop=True)
                    mm.then_inc(s_done, 1)

                def turn(G, i):
                    t = TP0[G] + i
                    if i == 0:
                        pe.wait_ge(p_ready, 4 * G + 4)
                    if t >= 2:
                        pe.wait_ge(pt_even if t % 2 == 0 else pt_odd, t // 2)
                    for q in range(4):
                        mm = pe.transpose(ps[0:ROWS[i], t % 2, q * P:(q + 1) * P], pbuf[G % 2][:, q, START[i]:END[i]],
                                          ident[:, :])
                    mm.then_inc(pt_turned, 1)

                def weigh(G, i):
                    t = TP0[G] + i
                    pe.wait_ge(pt_even if t % 2 == 0 else pt_odd, t // 2 + 1)
                    if i == 0 and G >= 1:
                        pe.wait_ge(ol_ready, G)
                    pe.matmul(ps[:, 3, :], cmat[0:ROWS[i], i, :], pt_flat[0:ROWS[i], (t % 2) * 512:(t % 2 + 1) * 512],
                              start=(i == 0), stop=(i == 1 + G // 2)).then_inc(pv_step, 1)

                def project(j):
                    pe.wait_ge(ol_ready, 2 * j)
                    if j >= 2:
                        pe.wait_ge(ya_lo, j - 1)
                    for h in range(ATT_H):
                        mm = pe.matmul(ps[:, 2, h * ATT_D:(h + 1) * ATT_D], olt[h // 4][:, (h % 4) * P:(h % 4 + 1) * P],
                                       wuv[:, h, :], start=True, stop=True)
                    mm.then_inc(y_done, 1)

                def turn_y(j):
                    pe.wait_ge(y_ready, j)
                    for c in range(4):
                        mm = pe.transpose(ps[:, 2, c * P:(c + 1) * P], yatt[:, c * P:(c + 1) * P], ident[:, :])
                    mm.then_inc(yt_turned, 1)

                late = None
                for G in range(GROUPS + 1):
                    last_tile = 1 + (G - 1) // 2
                    for half in range(2):
                        if G < GROUPS:
                            for q in (2 * half, 2 * half + 1):
                                scores(4 * G + q)
                        if half == 0:
                            if G == 0:
                                turn_mlstm()
                            if G == 1:
                                pe.wait_ge(yml_ready, 2)
                            if late is not None:
                                project(late)
                            if G >= 1:
                                turn(G - 1, 0)
                                turn(G - 1, 1)
                    if G >= 1:
                        if G == 1:
                            pe.wait_ge(yml_ready, ML_H)
                        for i in range(last_tile + 1):
                            if 2 <= i + 1 <= last_tile:
                                turn(G - 1, i + 1)
                            weigh(G - 1, i)
                        if late is not None:
                            turn_y(late)
                        late = last_tile if (G - 1) % 2 else None
                pe.wait_ge(yml_lo, ML_H)
                pe.wait_ge(s_masked, ATT_H * (NT - 1))
                out_product(N_PROJ, 0, MLSTM_K, True)
                project(late)
                out_product(N_PROJ, 1, MLSTM_K, True)
                turn_y(late)
                out_product(N_PROJ + 1, 0, MLSTM_K, True)

            ffn(0)
            stats(0)
            keep_warm(WARM_NORM)
            mixer()
            stats(1)
            keep_warm(WARM_NORM)
            ffn(2)

        @block.vector
        def _(dve):
            n_dv = [0]

            def link(ins):
                n_dv[0] += 1
                ins.then_inc(dv, 1)
                dve.wait_ge(dv, n_dv[0])

            def lo(u, s, width):
                dve.wait_ge(w_hi, u + 1)
                dve.tensor_tensor(wlo[:, s, 0:width], wraw[:, s, 0:width], whi[:, s, 0:width].bitcast(F32), ALU.subtract)\
                    .then_inc(w_lo, 1)

            def inputs():
                for k in range(KT):
                    b = 4 + 2 * (k % 2)
                    if k in (3, 4):
                        w = slice(0, HALF_W) if k == 3 else slice(HALF_W, UW)
                        dve.wait_ge(gate0_hi if k == 3 else w_hi, 1)
                        dve.tensor_tensor(wlo[:, 0, w], wraw[:, 0, w], whi[:, 0, w].bitcast(F32), ALU.subtract)\
                            .then_inc(gate0_lo if k == 3 else w_lo, 1)
                    dve.wait_ge(x_turned, k + 1)
                    dve.tensor_copy(x[:, k, 0:END[3]], ps[:, b, 0:END[3]])
                    dve.tensor_copy(x[:, k, END[3]:T], ps[:, b + 1, 0:P]).then_inc(x_copied, 1)
            def residual(p, m, b, c):
                if p == 1:
                    filled(dve, 2 * N_PROJ + m)
                else:
                    dve.wait_ge(w_used, 2 * m + (UNIT0[p] + FT + 2))
                z = cols(x[:, m, :], p)
                if p == 2 and not (isinstance(m, int) and m < 2):
                    dve.wait_ge(z_turned, m - 1)
                dve.scalar_tensor_tensor(ht[:, b // 2, N_META:T] if p == 2 else z, bank(b, p), c, z, ALU.mult, ALU.add)\
                    .then_inc(F[p]["z_done"], 1)

            def ffn(p):
                s, u0 = F[p], UNIT0[p]

                def hidden(f, e):
                    dve.wait_ge(w_used, f + (u0 + 1))
                    dve.wait_ge(s["silu_done"], f + 1)
                    dve.tensor_tensor(cols(ht[:, e, :], p), bank(4 * e + 2, p), cols(sil[:, e, :], p), ALU.mult)\
                        .then_inc(s["mul_done"], 1)
                    dve.wait_ge(s["hh_done"], f + 1)
                    dve.tensor_tensor(flat(hl[:, f, :], p), flat(ht[:, e, :], p), flat(hh[:, f, :], p).bitcast(F32), ALU.subtract)\
                        .then_inc(s["hl_done"], 1)

                if p == 0:
                    lo(u0 + 1, 1, UW)
                hidden(0, 0)
                lo(u0 + 2, 0, UW)
                hidden(1, 1)
                with dve.Fori(1, FT // 2 - 1) as i:
                    for e in range(2):
                        lo(2 * i + (u0 + 1 + e), 1 - e, UW)
                        hidden(2 * i + e, e)
                lo(u0 + FT - 1, 1, UW)
                hidden(FT - 2, 0)
                lo(u0 + FT, 0, DOWN_W)
                hidden(FT - 1, 1)
                lo(u0 + FT + 1, 1, DOWN_W)
                lo(u0 + FT + 2, 0, DOWN_W)
                for m in range(2):
                    residual(p, m, 2 * m, 0.5 / ALPHA)
                    if p == 2 and m == 1:
                        row_stats(0)
                    lo(2 * m + (u0 + FT + 3), 1, DOWN_W)
                    lo(2 * m + (u0 + FT + 4), 0, DOWN_W)
                if p == 0:
                    dve.wait_ge(vec_turned, 1)
                    dve.tensor_copy(vec[:, :], ps[:, 7, 0:NV]).then_inc(vec_ready, 1)
                with dve.Fori(1, KT // 2 - 1) as i:
                    for e in range(2):
                        m = 2 * i + e
                        residual(p, m, 2 * e, 0.5 / ALPHA)
                        if p == 2:
                            row_stats(m - 1)
                        lo(2 * m + (u0 + FT + 3), 1, DOWN_W)
                        lo(2 * m + (u0 + FT + 4), 0, DOWN_W)
                residual(p, KT - 2, 0, 0.5 / ALPHA)
                if p == 2:
                    row_stats(KT - 3)
                lo(u0 + FT + 15, 1, DOWN_W)
                if p == 0:
                    lo(MIX0, 0, UW)
                else:
                    row_stats(KT - 2)
                residual(p, KT - 1, 2, 0.5 / ALPHA)
                if p == 2:
                    row_stats(KT - 1)

            def row_stats(m):
                dve.wait_ge(z_copied, m + 1)
                for j in range(4):
                    dve.bn_stats(bst3[:, j, bass.ts(m, 6)], zrow[:, j, bass.ts(m, P)]).then_inc(bst3_done, 1)

            def norm_rows():
                dve.wait_ge(bst3_done, 4 * KT)
                for j in range(4):
                    ins = dve.bn_aggr(mv3[:, j, :], bst3[:, j, :])
                link(ins)
                dve.tensor_scalar(mv3[:, :, 1], mv3[:, :, 1], EPS / ALPHA ** 2, None, ALU.add).then_inc(var3_done, 1)
                dve.wait_ge(gb_in, 32)

                def centre(q):
                    v = half_row(zrow, q)
                    dve.scalar_tensor_tensor(v, v, mv3[:, q // 2, 0:1], gb[:, 0, (q % 2) * 512:(q % 2 + 1) * 512],
                                             ALU.subtract, ALU.mult).then_inc(centred, 1)

                def finish(q):
                    dve.wait_ge(centred, q + 1)
                    v = half_row(zrow, q)
                    dve.scalar_tensor_tensor(v, v, rstd3[:, q // 2:q // 2 + 1], gb[:, 1, (q % 2) * 512:(q % 2 + 1) * 512],
                                             ALU.mult, ALU.add).then_inc(out_dve, 1)

                centre(0)
                dve.wait_ge(sd3_done, 1)
                link(dve.reciprocal(rstd3, sd3))
                for q in range(1, 8):
                    centre(q)
                    if q - 1 not in POOL_HALVES:
                        finish(q - 1)
                finish(7)

            def norm(p):
                s = F[p]
                eps = EPS / ALPHA ** 2

                def centre(k):
                    z = cols(x[:, k, :], p)
                    dve.tensor_tensor(z, z, bank(4, p), ALU.subtract).then_inc(s["sub_done"], 1)

                var = flat(sil[:, 0, :], p)
                dve.wait_ge(s["stats_done"], 2)
                dve.wait_ge(s["mu2_done"], 1)
                dve.tensor_tensor(cols(sil[:, 0, :], p), bank(6, p), cols(sil[:, 0, :], p), ALU.subtract).then_inc(s["var_done"], 1)
                dve.wait_ge(s["var_done"], 1)
                dve.tensor_scalar(var, var, eps, eps, ALU.add, ALU.max).then_inc(s["varc_done"], 1)
                centre(0)
                centre(1)
                dve.wait_ge(s["sd_done"], 1)
                dve.reciprocal(var, flat(sil[:, 1, :], p)).then_inc(s["rstd_done"], 1)
                dve.wait_ge(s["rstd_done"], 1)
                for k in range(KT):
                    if 2 <= k + 1 < KT:
                        centre(k + 1)
                    dve.wait_ge(s["sub_done"], k + 1)
                    dve.tensor_tensor(flat(x[:, k, :], p), flat(x[:, k, :], p), var, ALU.mult).then_inc(s["norm_done"], 1)

            def index_scores():
                dve.wait_ge(proj_evac, 4)
                link(dve.tensor_scalar(wi[:, :, :], cs[:, :, S_WI:S_WI + 4], IDX_SCALE, None, ALU.mult))
                dve.wait_ge(par_in, 16 * 5)
                dve.tensor_tensor(gate[:, :, :], cs[:, :, S_IF:S_IF + 8], bg[:, :].unsqueeze(1).broadcast_to([P, NT, 8]), ALU.add)\
                    .then_inc(gate_in, 1)
                sq = qk_flat[:, 0:NT * LAT].rearrange("p (j c) -> p j c", j=NT)
                link(dve.tensor_tensor(sq, cmat, cmat, ALU.mult))
                link(dve.tensor_reduce(crms[:, 0, :], sq, AX.X, ALU.add))
                dve.tensor_scalar(crms[:, 0, :], crms[:, 0, :], 1.0 / LAT, EPS, ALU.mult, ALU.add).then_inc(c_ms, 1)
                dve.wait_ge(c_sd, 1)
                dve.wait_ge(ki_turned, 2)
                link(dve.reciprocal(crms[:, 0, :], crms[:, 1, :]))
                link(dve.tensor_tensor(cmat, cmat, crms[:, 0, :].unsqueeze(2).broadcast_to([P, NT, LAT]), ALU.mult))
                dve.tensor_tensor(cmat, cmat, kvg[:, :].unsqueeze(1).broadcast_to([P, NT, LAT]), ALU.mult).then_inc(c_ready, 1)
                for k in range(4 * (NT - 1)):
                    j, h = 1 + k // 4, k % 4
                    dst = sc[:, SC_OFF[j]:SC_OFF[j] + END[j]]
                    dve.wait_ge(relu_done, k + 1)
                    src = sil[:, k % 2, 0:END[j]]
                    if h == 0:
                        dve.tensor_scalar(dst, src, wi[:, j, 0:1], None, ALU.mult).then_inc(acc_done, 1)
                    else:
                        dve.wait_ge(acc_done, k)
                        dve.scalar_tensor_tensor(dst, src, wi[:, j, h:h + 1], dst, ALU.mult, ALU.add).then_inc(acc_done, 1)

            def select(j, r0=0, r1=TOPK // 8):
                w = sc[:, SC_OFF[j]:SC_OFF[j] + END[j]]
                dve.wait_ge(idx_masked, j)
                for r in range(r0, r1):
                    link(dve.max(top8[:, r % 2, :], w))
                    link(dve.match_replace(w, top8[:, r % 2, :], w, TAKEN))
                if r1 == TOPK // 8:
                    dve.tensor_scalar(w, w, (MASKED + TAKEN) / 2, UNPICKED, ALU.is_gt, ALU.mult).then_inc(bias_ready, 1)

            def gate_rows():
                link(dve.memset(m_row, 0.0))

                def fetch(row, b, c):
                    dve.tensor_scalar(row[:, 0:END[3]], ps[0:4, b, 0:END[3]], c, None, ALU.mult)
                    return dve.tensor_scalar(row[:, END[3]:T], ps[0:4, b + 1, 0:P], c, None, ALU.mult)

                dve.wait_ge(row_turned, 1)
                link(fetch(ig_row, 6, SOFTCAP))
                dve.wait_ge(row_turned, 2)
                link(fetch(lf_row, 4, -1.0))
                link(dve.tensor_tensor_scan(b_row, lf_row, m_row, 0.0, ALU.add, ALU.add))
                link(dve.tensor_tensor(ig_row, ig_row, b_row, ALU.subtract))
                link(dve.tensor_tensor_scan(m_row, ig_row, ig_row, -1.0e30, ALU.max, ALU.max))
                link(dve.tensor_scalar(lf_row, m_row, -1.0, None, ALU.mult))
                dve.scalar_tensor_tensor(b_row, b_row, -1.0, m_row, ALU.mult, ALU.subtract).then_inc(row_ready, 1)

            def convolve():
                for c in range(4):
                    dve.wait_ge(proj_evac, 8 + c + 1)
                    for t in range(CONV):
                        tap = vec[:, V_CONV + 4 * t + c:V_CONV + 4 * t + c + 1]
                        src = up[:, c, t:t + T]
                        if t == 0:
                            ins = dve.tensor_scalar(qk[:, c, :], src, tap, None, ALU.mult)
                        else:
                            ins = dve.scalar_tensor_tensor(qk[:, c, :], src, tap, qk[:, c, :], ALU.mult, ALU.add)
                        if t < CONV - 1:
                            link(ins)
                    ins.then_inc(conv_done, 1)

            def arguments(h):
                dve.wait_ge(nm_spread, h + 1)
                if h == 3:
                    dve.wait_ge(num_done, 2)
                for i in range(NT):
                    R = ROWS[i]
                    dve.tensor_scalar(wt(h, i, QS[i], T), ps[0:R, 5 + h % 2, QS[i] - N_META:SEQ], tok[0:R, i, h:h + 1],
                                      0.0, ALU.add, ALU.min).then_inc(arg_done, 1)

            def mlstm():
                def weights(h):
                    for b, parts in enumerate(ST_BANKS):
                        dve.wait_ge(st_done, 4 * h + b + 1)
                        dve.wait_ge(exp_done, 5 * h + (1, 2, 3, 5)[b])
                        for i, o in parts:
                            w = wt(h, i, QS[i], T)
                            ins = dve.scalar_tensor_tensor(w, ps[0:ROWS[i], b, o:o + T - QS[i]], K_SCALE, w, ALU.mult, ALU.mult)
                        ins.then_inc(st_used, 1)

                def head_stats(h):
                    for j in range(4):
                        if j in (0, 2):
                            dve.wait_ge(num_copied, 2 * h + 1 + j // 2)
                        dve.bn_stats(bst[:, h * 4 + j, :], nums[:, h, j, 0:ML_DV]).then_inc(dv, 1)
                        n_dv[0] += 1
                    dve.wait_ge(dv, n_dv[0])
                    for q in range(4 * h, 4 * h + 4):
                        dve.bn_aggr(mv[:, q, :], bst[:, q, :]).then_inc(dv, 1)
                        n_dv[0] += 1

                weights(0)
                weights(1)
                arguments(2)
                select(4, 12, TOPK // 8)
                weights(2)
                arguments(3)
                head_stats(0)
                head_stats(1)
                weights(3)
                head_stats(2)
                head_stats(3)
                dve.wait_ge(dv, n_dv[0])
                hj = lambda v: v.rearrange("p (h j) -> p h j", h=ML_H)
                em = tok[:, :, :].rearrange("p j e -> p e j")[:, 4:8, 1:NT]
                den = nums[:, :, :, ML_DV]
                link(dve.scalar_tensor_tensor(hj(mls[:, 0, :]), den, -1.0, den, ALU.mult, ALU.max))
                link(dve.tensor_tensor(hj(mls[:, 0, :]), hj(mls[:, 0, :]), em, ALU.max))
                link(dve.reciprocal(mls[:, 1, :], mls[:, 0, :]))
                link(dve.tensor_tensor(mls[:, 0, :], mls[:, 1, :], mls[:, 1, :], ALU.mult))
                link(dve.tensor_tensor(mls[:, 0, :], mls[:, 0, :], mv[:, :, 1], ALU.mult))
                dve.tensor_scalar(mls[:, 0, :], mls[:, 0, :], EPS, None, ALU.add).then_inc(ml_var, 1)
                dve.wait_ge(ml_sd, 1)
                link(dve.reciprocal(mls[:, 2, :], mls[:, 0, :]))
                link(dve.tensor_tensor(mls[:, 2, :], mls[:, 2, :], mls[:, 1, :], ALU.mult))
                for h in range(ML_H):
                    for j in range(4):
                        q = h * 4 + j
                        v = nums[:, h, j, 0:ML_DV]
                        ins = dve.tensor_scalar(v, v, mv[:, q, 0:1], mls[:, 2, q:q + 1], ALU.subtract, ALU.mult)
                    ins.then_inc(hn_ready, 1)

            def gated_mlstm(heads):
                for h in heads:
                    dve.wait_ge(hn_turned, h + 1)
                    g = vec[:, V_MLG + h:V_MLG + h + 1]
                    dve.scalar_tensor_tensor(yml(h), ps[:, h, :], g, sg[:, h, N_META:T], ALU.mult, ALU.mult)\
                        .then_inc(yml_ready, 1)

            def attention():
                def masked(k):
                    j, h = 1 + k // ATT_H, k % ATT_H
                    n = END[j]
                    dve.wait_ge(s_done, k + 1)
                    if k >= 2:
                        dve.wait_ge(p_ready, k - 1)
                    if h == 0:
                        dve.wait_ge(mask_ready, j)
                    dst, msk = (like_keys(v, n) for v in (sil[:, k % 2, 0:n], sc[:, SC_OFF[j]:SC_OFF[j] + n]))
                    dve.tensor_tensor_reduce(dst, keys(P, n, 4 + 2 * (k % 2)), msk, 1.0, -3.0e38, ALU.add, ALU.max,
                                             smax[:, j, h:h + 1]).then_inc(s_masked, 1)
                    dve.wait_ge(s_masked, k + 1)
                    dve.tensor_scalar(nmax[:, j, h:h + 1], smax[:, j, h:h + 1], -ATT_SCALE, None, ALU.mult)\
                        .then_inc(nmax_ready, 1)

                def normalise(j):
                    dve.wait_ge(p_ready, ATT_H * j)
                    link(dve.reciprocal(rinv[:, j, :], rsum[:, j, :]))
                    dve.wait_ge(y_done, j)
                    if j >= 2:
                        dve.wait_ge(yt_turned, j - 1)
                    dve.tensor_tensor(yatt.rearrange("p (h d) -> p h d", h=ATT_H),
                                      ps[:, 2, :].rearrange("p (h d) -> p h d", h=ATT_H),
                                      rinv[:, j, :].unsqueeze(2).broadcast_to([P, ATT_H, ATT_D]), ALU.mult).then_inc(y_ready, 1)

                def att_lo(j):
                    dve.wait_ge(ya_hi, j)
                    dve.tensor_tensor(xl[:, 0:4, START[j]:END[j]], ps[:, 2, :].rearrange("p (c r) -> p c r", c=4),
                                      xh[:, 0:4, START[j]:END[j]].bitcast(F32), ALU.subtract).then_inc(ya_lo, 1)

                late = None
                def copy_even(G, tiles):
                    for i in tiles:
                        t = TP0[G] + i
                        if t % 2 == 0:
                            dve.wait_ge(pt_turned, t + 1)
                            if t >= 2:
                                dve.wait_ge(pv_step, t - 1)
                            dve.tensor_copy(pt_flat[0:ROWS[i], 0:512], ps[0:ROWS[i], 0, :]).then_inc(pt_even, 1)

                for G in range(GROUPS + 1):
                    last_tile = 1 + (G - 1) // 2
                    for half in range(2):
                        if G < GROUPS:
                            for q in (2 * half, 2 * half + 1):
                                masked(4 * G + q)
                        if G == 0:
                            gated_mlstm((2 * half, 2 * half + 1))
                        if half == 0:
                            if late is not None:
                                normalise(late)
                            if G >= 1:
                                copy_even(G - 1, (0, 1))
                    if G >= 1:
                        copy_even(G - 1, range(2, last_tile + 1))
                        if late is not None:
                            att_lo(late)
                        late = last_tile if (G - 1) % 2 else None
                normalise(late)
                att_lo(late)

            inputs()
            ffn(0)
            norm(0)
            index_scores()
            select(1)
            select(2)
            gate_rows()
            select(3)
            convolve()
            select(4, 0, 8)
            dve.wait_ge(tok_ready, 1)
            arguments(0)
            arguments(1)
            select(4, 8, 12)
            mlstm()
            attention()
            for m in range(KT):
                residual(1, m, 4 + m % 4, 1.0 / ALPHA)
                if m in LATE_UNITS:
                    lo(MIX0 + LATE_UNITS[m], LATE_UNITS[m] % 2, UW)
            norm(1)
            ffn(2)
            norm_rows()


_INS = ["x", "meta_tokens", "ln1_g", "ln1_b", "ffn1_w_gate", "ffn1_w_up", "ffn1_w_down", "w_in", "w_uk", "w_uv",
        "kv_norm_g", "conv_w", "b_igate", "b_fgate", "ml_norm_g", "w_out", "ln2_g", "ln2_b",
        "ffn2_w_gate", "ffn2_w_up", "ffn2_w_down", "ln3_g", "ln3_b"]


def kernel(**inputs):
    import concourse.bacc as _bacc
    from concourse.bass_utils import run_bass_kernel_spmd as _run

    nc = _bacc.Bacc("TRN2", target_bir_lowering=False, num_devices=1)
    arrays, aps = {}, {}
    for name in _INS:
        v = np.ascontiguousarray(inputs[name])
        arrays[f"in_{name}"] = v
        aps[name] = nc.dram_tensor(f"in_{name}", v.shape, mybir.dt.from_np(v.dtype), kind="ExternalInput").ap()
    out = nc.dram_tensor("out_0", (1, SEQ, D), F32, kind="ExternalOutput").ap()
    build(nc, aps, out)
    r = _run(nc, [arrays], core_ids=[0])
    return r.results[0]["out_0"]
```
